# Optimizing a Trainium2 kernel written in Bass

```python
import math
import jax, jax.numpy as jnp
from jax import lax
import numpy as np

D_MODEL = 1024
BATCH = 1
SEQ = 512
DEPTH = 2

D_MLSTM = D_MODEL
N_MLSTM_HEADS = 4
MLSTM_HEAD_DIM = D_MLSTM // N_MLSTM_HEADS
D_CONV = D_MODEL
N_CONV_GROUPS = 8
D_MIX = D_MLSTM + D_CONV
D_IN_PROJ = 2 * D_MLSTM + 2 * D_CONV
MLSTM_CONV_K = 4
CONFORMER_CONV_K = 31
CHUNK = 128
D_FF = 4 * D_MODEL
N_ADA = 6
EPS = 1e-6


def rms_norm(x, g):
    xf = x.astype(jnp.float32)
    y = xf * lax.rsqrt(jnp.mean(xf * xf, axis=-1, keepdims=True) + EPS)
    return (y * g.astype(jnp.float32)).astype(x.dtype)

def group_layer_norm(x, n_groups, g, b=None):
    shp = x.shape
    xf = x.astype(jnp.float32).reshape(*shp[:-1], n_groups, shp[-1] // n_groups)
    mu = jnp.mean(xf, axis=-1, keepdims=True)
    xc = xf - mu
    var = jnp.mean(xc * xc, axis=-1, keepdims=True)
    y = (xc * lax.rsqrt(var + EPS)).reshape(shp) * g.astype(jnp.float32)
    if b is not None:
        y = y + b.astype(jnp.float32)
    return y.astype(x.dtype)

def causal_depthwise_conv(x, w, b):
    K, C = w.shape
    y = lax.conv_general_dilated(
        x, w[:, None, :].astype(x.dtype), window_strides=(1,), padding=[(K - 1, 0)],
        dimension_numbers=("NWC", "WIO", "NWC"), feature_group_count=C)
    return y + b.astype(x.dtype)

def mlstm_chunkwise(q, k, v, ig, lf):
    B, T, H, Dh = q.shape
    nc = T // CHUNK

    def to_chunks(a):
        a = a.astype(jnp.float32).reshape(B, nc, CHUNK, H, *a.shape[3:])
        return jnp.moveaxis(a, (1, 3), (0, 2))

    xs = (to_chunks(q), to_chunks(k), to_chunks(v), to_chunks(ig), to_chunks(lf))
    causal = jnp.tril(jnp.ones((CHUNK, CHUNK), dtype=bool))

    def body(carry, inp):
        C, n, m = carry
        qc, kc, vc, igc, lfc = inp
        b = jnp.cumsum(lfc, axis=-1)
        logw = b[..., :, None] - b[..., None, :] + igc[..., None, :]
        logw = jnp.where(causal, logw, -jnp.inf)
        g = b + m[..., None]
        m_t = jnp.maximum(g, jnp.max(logw, axis=-1))
        w = jnp.exp(logw - m_t[..., None])
        inter = jnp.exp(g - m_t)
        s = jnp.einsum("bhtd,bhsd->bhts", qc, kc) * w
        num = jnp.einsum("bhts,bhse->bhte", s, vc) + inter[..., None] * jnp.einsum("bhtd,bhde->bhte", qc, C)
        den = jnp.sum(s, axis=-1) + inter * jnp.einsum("bhtd,bhd->bht", qc, n)
        h = num / jnp.maximum(jnp.abs(den), jnp.exp(-m_t))[..., None]
        b_last = b[..., -1]
        a = b_last[..., None] - b + igc
        m_new = jnp.maximum(b_last + m, jnp.max(a, axis=-1))
        wk = jnp.exp(a - m_new[..., None])
        decay = jnp.exp(b_last + m - m_new)
        C_new = decay[..., None, None] * C + jnp.einsum("bhs,bhsd,bhse->bhde", wk, kc, vc)
        n_new = decay[..., None] * n + jnp.einsum("bhs,bhsd->bhd", wk, kc)
        return (C_new, n_new, m_new), h

    init = (jnp.zeros((B, H, Dh, Dh), jnp.float32), jnp.zeros((B, H, Dh), jnp.float32),
            jnp.zeros((B, H), jnp.float32))
    _, hs = lax.scan(body, init, xs)
    return jnp.moveaxis(hs, (0, 2), (1, 3)).reshape(B, T, H, Dh)

def mixer(h, w_in, w_conv_m, b_conv_m, w_q, w_k, w_v, w_gates, b_gates, g_mh,
          w_dw, b_dw, g_cn, b_cn, w_out):
    B, T, _ = h.shape
    H, Dh = N_MLSTM_HEADS, MLSTM_HEAD_DIM
    u = h @ w_in.astype(h.dtype)
    x_m, z, glu_a, glu_b = jnp.split(u, [D_MLSTM, 2 * D_MLSTM, 2 * D_MLSTM + D_CONV], axis=-1)

    x_c = jax.nn.silu(causal_depthwise_conv(x_m, w_conv_m, b_conv_m))
    xc_h = x_c.reshape(B, T, H, Dh)
    xm_h = x_m.reshape(B, T, H, Dh)
    q = jnp.einsum("bthd,hde->bthe", xc_h, w_q.astype(h.dtype))
    k = jnp.einsum("bthd,hde->bthe", xc_h, w_k.astype(h.dtype))
    v = jnp.einsum("bthd,hde->bthe", xm_h, w_v.astype(h.dtype))
    qkv = jnp.concatenate([q, k, v], axis=-1).reshape(B, T, H, 3 * Dh)
    qkv = jnp.moveaxis(qkv, 2, 3).reshape(B, T, 3 * D_MLSTM)
    gates = (qkv @ w_gates.astype(h.dtype) + b_gates.astype(h.dtype)).astype(jnp.float32)
    ig, fg = gates[..., :H], gates[..., H:]
    lf = jax.nn.log_sigmoid(fg)
    h_m = mlstm_chunkwise(q, k * (Dh ** -0.5), v, ig, lf)
    h_m = group_layer_norm(h_m.reshape(B, T, D_MLSTM), H, g_mh).astype(h.dtype)
    h_m = jax.nn.sigmoid(z) * h_m

    a = glu_a * jax.nn.sigmoid(glu_b)
    a = causal_depthwise_conv(a, w_dw, b_dw)
    a = jax.nn.silu(group_layer_norm(a, N_CONV_GROUPS, g_cn, b_cn))

    return jnp.concatenate([h_m, a], axis=-1) @ w_out.astype(h.dtype)

def first_inputs(seed: int = 0) -> dict:
    key = jax.random.key(seed)
    ks = jax.random.split(key, 26)
    f32 = jnp.float32

    def nrm(k, shape, fan_in, scale=1.0):
        return jax.random.normal(k, shape, f32) * (scale * fan_in ** -0.5)

    def gain(k, shape):
        return 1.0 + 0.05 * jax.random.normal(k, shape, f32)

    def small(k, shape):
        return 0.02 * jax.random.normal(k, shape, f32)

    H = N_MLSTM_HEADS
    ig_bias = 0.1 * jax.random.normal(ks[24], (DEPTH, H), f32)
    fg_bias = jnp.linspace(3.0, 6.0, H, dtype=f32)[None, :] + 0.1 * jax.random.normal(ks[25], (DEPTH, H), f32)
    return {
        "x": jax.random.normal(ks[0], (BATCH, SEQ, D_MODEL), f32),
        "c": jax.random.normal(ks[1], (BATCH, D_MODEL), f32),
        "w_ada": nrm(ks[2], (DEPTH, D_MODEL, N_ADA * D_MODEL), D_MODEL, 0.5),
        "b_ada": small(ks[3], (DEPTH, N_ADA * D_MODEL)),
        "g_pre_mix": gain(ks[4], (DEPTH, D_MODEL)),
        "g_post_mix": gain(ks[5], (DEPTH, D_MODEL)),
        "g_pre_mlp": gain(ks[6], (DEPTH, D_MODEL)),
        "g_post_mlp": gain(ks[7], (DEPTH, D_MODEL)),
        "w_in": nrm(ks[8], (DEPTH, D_MODEL, D_IN_PROJ), D_MODEL),
        "w_conv_m": nrm(ks[9], (DEPTH, MLSTM_CONV_K, D_MLSTM), MLSTM_CONV_K),
        "b_conv_m": small(ks[10], (DEPTH, D_MLSTM)),
        "w_q": nrm(ks[11], (DEPTH, H, MLSTM_HEAD_DIM, MLSTM_HEAD_DIM), MLSTM_HEAD_DIM),
        "w_k": nrm(ks[12], (DEPTH, H, MLSTM_HEAD_DIM, MLSTM_HEAD_DIM), MLSTM_HEAD_DIM),
        "w_v": nrm(ks[13], (DEPTH, H, MLSTM_HEAD_DIM, MLSTM_HEAD_DIM), MLSTM_HEAD_DIM),
        "w_gates": nrm(ks[14], (DEPTH, 3 * D_MLSTM, 2 * H), 3 * D_MLSTM),
        "b_gates": jnp.concatenate([ig_bias, fg_bias], axis=-1),
        "g_mh": gain(ks[15], (DEPTH, D_MLSTM)),
        "w_dw": nrm(ks[16], (DEPTH, CONFORMER_CONV_K, D_CONV), CONFORMER_CONV_K),
        "b_dw": small(ks[17], (DEPTH, D_CONV)),
        "g_cn": gain(ks[18], (DEPTH, D_CONV)),
        "b_cn": small(ks[19], (DEPTH, D_CONV)),
        "w_out": nrm(ks[20], (DEPTH, D_MIX, D_MODEL), D_MIX),
        "w_ff1": nrm(ks[21], (DEPTH, D_MODEL, D_FF), D_MODEL),
        "w_ff2": nrm(ks[22], (DEPTH, D_FF, D_MODEL), D_FF),
    }

def first_block(x, c, w_ada, b_ada, g_pre_mix, g_post_mix, g_pre_mlp, g_post_mlp, w_in,
              w_conv_m, b_conv_m, w_q, w_k, w_v, w_gates, b_gates, g_mh, w_dw, b_dw,
              g_cn, b_cn, w_out, w_ff1, w_ff2):
    c_act = jax.nn.silu(c.astype(jnp.float32))
    for l in range(DEPTH):
        mod = (c_act @ w_ada[l].astype(jnp.float32) + b_ada[l].astype(jnp.float32)).astype(x.dtype)
        sh_mix, sc_mix, gt_mix, sh_mlp, sc_mlp, gt_mlp = [m[:, None, :] for m in jnp.split(mod, N_ADA, axis=-1)]

        h = rms_norm(x, g_pre_mix[l]) * (1 + sc_mix) + sh_mix
        y = mixer(h, w_in[l], w_conv_m[l], b_conv_m[l], w_q[l], w_k[l], w_v[l], w_gates[l], b_gates[l],
                  g_mh[l], w_dw[l], b_dw[l], g_cn[l], b_cn[l], w_out[l])
        x = x + gt_mix * rms_norm(y, g_post_mix[l])

        h = rms_norm(x, g_pre_mlp[l]) * (1 + sc_mlp) + sh_mlp
        f = jnp.square(jax.nn.relu(h @ w_ff1[l].astype(h.dtype))) @ w_ff2[l].astype(h.dtype)
        x = x + gt_mlp * rms_norm(f, g_post_mlp[l])
    return x


DEPTH_2 = 1

GRID_W = 64
CTX_LEN = 256
CONV_W = 1024
CONV_K = 3
N_HEADS = 16
HEAD_DIM = 64
ATTN_W = N_HEADS * HEAD_DIM
WIN_ROWS_MAX = 8
WIN_COLS = 16
ROPE_BASE = 10000.0
N_BRANCH = 2
IN_SIZES = [CONV_W] * 4 + [ATTN_W] * 4 + [D_MODEL] * N_BRANCH
IN_COLS = sum(IN_SIZES)
K_OFF = 4 * CONV_W + ATTN_W
V_END = 4 * CONV_W + 3 * ATTN_W


def _rmsnorm(u, g):
    u32 = u.astype(jnp.float32)
    return (u32 * lax.rsqrt(jnp.mean(u32 * u32, axis=-1, keepdims=True) + EPS)).astype(u.dtype) * g

def _modulation(cond, w_mod, b_mod):
    m = jax.nn.silu(cond) @ w_mod + b_mod
    return jnp.split(m, 3, axis=-1)

def _split_in(p):
    idx = np.cumsum(IN_SIZES)[:-1].tolist()
    return jnp.split(p, idx, axis=-1)

def _dwconv3(u, w, b):
    L = u.shape[1]
    up = jnp.pad(u, ((0, 0), (1, 1), (0, 0)))
    return up[:, :L] * w[0] + up[:, 1:L + 1] * w[1] + up[:, 2:] * w[2] + b

def _rope_2d_tables(L, dtype):
    t = jnp.arange(L, dtype=jnp.int32)
    row = (t // GRID_W).astype(jnp.float32)
    col = (t % GRID_W).astype(jnp.float32)
    half = HEAD_DIM // 2
    inv = ROPE_BASE ** (-jnp.arange(0, half, 2, dtype=jnp.float32) / half)
    ang_r = row[:, None] * inv
    ang_c = col[:, None] * inv
    ang = jnp.concatenate([ang_r, ang_r, ang_c, ang_c], axis=-1)
    return jnp.cos(ang).astype(dtype), jnp.sin(ang).astype(dtype)

def _rot_half_axial(u):
    u1, u2, u3, u4 = jnp.split(u, 4, axis=-1)
    return jnp.concatenate([-u2, u1, -u4, u3], axis=-1)

def _apply_rope(u, cos, sin):
    return u * cos[None, :, None, :] + _rot_half_axial(u) * sin[None, :, None, :]

def _heads(u):
    return u.reshape(u.shape[0], u.shape[1], N_HEADS, HEAD_DIM)

def _neighbourhood_attention(q, k, v, k_ctx, v_ctx, rpb):
    bsz, L, H, Dh = q.shape
    rows = L // GRID_W
    wr = min(WIN_ROWS_MAX, rows)
    n_nb = wr * WIN_COLS
    scale = HEAD_DIM ** -0.5
    qg = q.reshape(bsz, rows, GRID_W, H, Dh)
    kg = k.reshape(bsz, rows, GRID_W, H, Dh)
    vg = v.reshape(bsz, rows, GRID_W, H, Dh)
    col = jnp.arange(GRID_W, dtype=jnp.int32)
    col_start = jnp.clip(col - WIN_COLS // 2, 0, GRID_W - WIN_COLS)
    col_idx = col_start[:, None] + jnp.arange(WIN_COLS, dtype=jnp.int32)
    dc_idx = col_idx - col[:, None] + (WIN_COLS - 1)

    def row_block(r):
        rs = jnp.clip(r - wr // 2, 0, rows - wr)
        q_r = lax.dynamic_index_in_dim(qg, r, axis=1, keepdims=False)
        k_slab = lax.dynamic_slice_in_dim(kg, rs, wr, axis=1)
        v_slab = lax.dynamic_slice_in_dim(vg, rs, wr, axis=1)
        k_win = k_slab[:, :, col_idx]
        v_win = v_slab[:, :, col_idx]
        dr_idx = rs + jnp.arange(wr, dtype=jnp.int32) - r + (WIN_ROWS_MAX - 1)
        bias = rpb[:, dr_idx[None, :, None], dc_idx[:, None, :]]
        s_nb = (jnp.einsum('bqhd,bpqjhd->bqhpj', q_r, k_win).astype(jnp.float32) * scale
                + jnp.transpose(bias, (1, 0, 2, 3))[None].astype(jnp.float32))
        s_nb = s_nb.reshape(bsz, GRID_W, H, n_nb)
        s_ctx = jnp.einsum('bqhd,bchd->bqhc', q_r, k_ctx).astype(jnp.float32) * scale
        p = jax.nn.softmax(jnp.concatenate([s_nb, s_ctx], axis=-1), axis=-1).astype(v.dtype)
        p_nb = p[..., :n_nb].reshape(bsz, GRID_W, H, wr, WIN_COLS)
        p_ctx = p[..., n_nb:]
        return (jnp.einsum('bqhpj,bpqjhd->bqhd', p_nb, v_win)
                + jnp.einsum('bqhc,bchd->bqhd', p_ctx, v_ctx))

    out = lax.map(row_block, jnp.arange(rows, dtype=jnp.int32))
    return jnp.transpose(out, (1, 0, 2, 3, 4)).reshape(bsz, L, H * Dh)

def _ctx_attention(q, k, v):
    scale = HEAD_DIM ** -0.5
    s = jnp.einsum('bqhd,bkhd->bhqk', q, k).astype(jnp.float32) * scale
    p = jax.nn.softmax(s, axis=-1).astype(v.dtype)
    o = jnp.einsum('bhqk,bkhd->bqhd', p, v)
    return o.reshape(o.shape[0], o.shape[1], ATTN_W)

def _mixer_out(parts, attn_o, conv_w, conv_b, w_out_conv, w_out_attn, w_o):
    b_gate, c_gate, x_in, z_a, _, _, _, z_b, g_a, g_b = parts
    y_a = (jax.nn.silu(z_a) * b_gate * _dwconv3(c_gate * x_in, conv_w, conv_b)) @ w_out_conv
    y_b = (jax.nn.silu(z_b) * attn_o) @ w_out_attn
    merged = jax.nn.sigmoid(g_a) * y_a + jax.nn.sigmoid(g_b) * y_b
    return merged @ w_o

def second_inputs(seed: int = 0) -> dict:
    key = jax.random.key(seed)
    ks = jax.random.split(key, 16)
    f32 = jnp.float32
    nrm = lambda k, shape, s: jax.random.normal(k, shape, f32) * s
    return {
        "x": nrm(ks[0], (BATCH, SEQ, D_MODEL), 1.0),
        "c": nrm(ks[1], (BATCH, D_MODEL), 1.0),
        "ctx": nrm(ks[2], (BATCH, CTX_LEN, D_MODEL), 1.0),
        "c_ctx": nrm(ks[3], (D_MODEL,), 1.0),
        "w_mod": nrm(ks[4], (DEPTH_2, D_MODEL, 3 * D_MODEL), D_MODEL ** -0.5),
        "b_mod": nrm(ks[5], (DEPTH_2, 3 * D_MODEL), 0.02),
        "pre_g": 1.0 + nrm(ks[6], (DEPTH_2, D_MODEL), 0.05),
        "post_g": 1.0 + nrm(ks[7], (DEPTH_2, D_MODEL), 0.05),
        "w_in": nrm(ks[8], (DEPTH_2, D_MODEL, IN_COLS), D_MODEL ** -0.5),
        "conv_w": nrm(ks[9], (DEPTH_2, CONV_K, CONV_W), CONV_K ** -0.5),
        "conv_b": nrm(ks[10], (DEPTH_2, CONV_W), 0.02),
        "rpb": nrm(ks[11], (DEPTH_2, N_HEADS, 2 * WIN_ROWS_MAX - 1, 2 * WIN_COLS - 1), 0.1),
        "w_out_conv": nrm(ks[12], (DEPTH_2, CONV_W, D_MODEL), CONV_W ** -0.5),
        "w_out_attn": nrm(ks[13], (DEPTH_2, ATTN_W, D_MODEL), ATTN_W ** -0.5),
        "w_o": nrm(ks[14], (DEPTH_2, D_MODEL, D_MODEL), D_MODEL ** -0.5),
    }

def second_block(x, c, ctx, c_ctx, w_mod, b_mod, pre_g, post_g, w_in, conv_w, conv_b, rpb,
              w_out_conv, w_out_attn, w_o):
    L = x.shape[1]
    cos, sin = _rope_2d_tables(L, x.dtype)
    for i in range(DEPTH_2):
        last = i == DEPTH_2 - 1
        sh, sc, gt = _modulation(c, w_mod[i], b_mod[i])
        sh_c, sc_c, gt_c = _modulation(c_ctx, w_mod[i], b_mod[i])
        h = _rmsnorm(x, pre_g[i]) * (1.0 + sc[:, None, :]) + sh[:, None, :]
        hc = _rmsnorm(ctx, pre_g[i]) * (1.0 + sc_c) + sh_c
        parts = _split_in(h @ w_in[i])
        q = _apply_rope(_heads(parts[4]), cos, sin)
        k = _apply_rope(_heads(parts[5]), cos, sin)
        v = _heads(parts[6])
        if last:
            kv_c = hc @ w_in[i][:, K_OFF:V_END]
            k_c, v_c = jnp.split(kv_c, 2, axis=-1)
            k_c, v_c = _heads(k_c), _heads(v_c)
        else:
            parts_c = _split_in(hc @ w_in[i])
            k_c, v_c = _heads(parts_c[5]), _heads(parts_c[6])
        attn = _neighbourhood_attention(q, k, v, k_c, v_c, rpb[i])
        y = _mixer_out(parts, attn, conv_w[i], conv_b[i], w_out_conv[i], w_out_attn[i], w_o[i])
        if not last:
            attn_c = _ctx_attention(_heads(parts_c[4]), k_c, v_c)
            y_c = _mixer_out(parts_c, attn_c, conv_w[i], conv_b[i], w_out_conv[i], w_out_attn[i], w_o[i])
            ctx = ctx + gt_c * _rmsnorm(y_c, post_g[i])
        x = x + gt[:, None, :] * _rmsnorm(y, post_g[i])
    return x


def setup_inputs(seed=0):
    out = dict(first_inputs(seed))
    for name, value in second_inputs(seed + 1).items():
        if name != "x":
            out[name + "_2"] = value
    return out


def reference(
    x, c, w_ada, b_ada, g_pre_mix, g_post_mix, g_pre_mlp, g_post_mlp, w_in, w_conv_m, b_conv_m,
    w_q, w_k, w_v, w_gates, b_gates, g_mh, w_dw, b_dw, g_cn, b_cn, w_out, w_ff1, w_ff2, c_2,
    ctx_2, c_ctx_2, w_mod_2, b_mod_2, pre_g_2, post_g_2, w_in_2, conv_w_2, conv_b_2, rpb_2,
    w_out_conv_2, w_out_attn_2, w_o_2,
):
    x = first_block(
        x, c, w_ada, b_ada, g_pre_mix, g_post_mix, g_pre_mlp, g_post_mlp, w_in, w_conv_m,
        b_conv_m, w_q, w_k, w_v, w_gates, b_gates, g_mh, w_dw, b_dw, g_cn, b_cn, w_out, w_ff1,
        w_ff2,
    )
    return second_block(
        x, c_2, ctx_2, c_ctx_2, w_mod_2, b_mod_2, pre_g_2, post_g_2, w_in_2, conv_w_2, conv_b_2,
        rpb_2, w_out_conv_2, w_out_attn_2, w_o_2,
    )


_drawn_inputs = setup_inputs


def setup_inputs(seed=0):
    import zlib

    import numpy as np

    out = dict(_drawn_inputs(seed))
    spreads = {}
    factors = {'b_conv_m': 4.333,
     'g_mh': 3.238,
     'b_dw': 3.922,
     'b_cn': 7.292,
     'conv_b_2': 8.0,
     'rpb_2': 8.0}
    for name, (base, spread) in spreads.items():
        noise = np.random.default_rng([zlib.crc32(name.encode()), seed]).standard_normal(out[name].shape)
        drawn = base * np.exp(spread * noise) if base else spread * noise
        out[name] = __import__('jax').numpy.asarray(drawn.astype(out[name].dtype))
    for name, factor in factors.items():
        out[name] = (out[name] * factor).astype(out[name].dtype)
    return out
```

```python
from collections import deque
from contextlib import ExitStack

import numpy as np

import concourse.bass as bass
from concourse import mybir

F32 = mybir.dt.float32
F32R = mybir.dt.float32r
ALU = mybir.AluOpType
ACT = mybir.ActivationFunctionType
AX = mybir.AxisListType

P = 128
D = 1024
T = 512
DT = D // P
DEPTH = 2
HEADS, HEAD_D = 4, 256
CONV_M, CONV_G = 4, 31
FF = 4 * D
QUARTER = FF // 4 // P
EPS = 1e-6
NEG = -1e30

GRID = 64
ROWS = T // GRID
CTX = 256
A_HEADS, A_DIM = 16, 64
WIN = 16
CH_COLS = P // ROWS
N_CH = T // P
K_COLS = 32
K_START = [0, 8, 24, 32]
TOEP = 48
RPB_W = 64
SLOT = 2048


class Queue:

    def __init__(self, engine, sem):
        self.engine, self.sem, self.count, self.seen = engine, sem, 0, {}

    def wait(self, *marks):
        for mark in marks:
            if mark is None:
                continue
            sem, value = mark
            if self.seen.get(sem.name, 0) < value:
                self.seen[sem.name] = value
                self.engine.wait_ge(sem, value)

    def do(self, step):
        self.count += 1
        step(self.engine).then_inc(self.sem, 1)
        return (self.sem, self.count)

    def quiet(self, step):
        step(self.engine)


class Landing:

    def __init__(self, sem):
        self.sem, self.count = sem, 0

    def load(self, queue, dst, src):
        self.count += 16
        queue.engine.dma_start(dst, src).then_inc(self.sem, 16)
        return (self.sem, self.count)


def build(nc, A, out, probe=None):
    ctx = ExitStack()
    with ctx:
        sem = lambda name: ctx.enter_context(nc.semaphore(name))
        base = (nc.sbuf_base + 63) // 64 * 64
        n_arena = (nc.sbuf_usable_end - base) // 32 * 32
        ctx.enter_context(nc.sbuf_tensor("arena", [P, n_arena // 4 - 16], F32))

        def at(name, slot, shape, dtype=F32, part=0):
            return nc.alloc_sbuf_tensor_at(name, shape, dtype, offset=base + int(slot * SLOT) + 4 * part)

        pe, act, dve, pool = Queue(nc.tensor, sem("pe_done")), Queue(nc.scalar, sem("act_done")), \
            Queue(nc.vector, sem("dve_done")), Queue(nc.gpsimd, sem("pool_done"))
        sp = Queue(nc.sync, None)

        psum = [ctx.enter_context(nc.psum_tensor(f"bank{i}", [P, 512], F32)) for i in range(8)]
        bank_turn = [0]
        bank_free = [[] for _ in range(8)]

        def take_bank():
            while bank_free[bank_turn[0] % 8] is None:
                bank_turn[0] += 1
            i = bank_turn[0] % 8
            bank_turn[0] += 1
            pe.wait(*bank_free[i])
            bank_free[i] = None
            return i, psum[i]

        par = [at(f"params{l}", 32 + l, [P, 512]) for l in range(DEPTH)]
        par2 = at("params_second", 34, [P, 128])
        cols = at("columns", 34, [P, 384], part=128)
        ident = at("ident", 103, [P, P])
        ones = at("ones", 103, [P, P], part=128)
        misc = at("misc", 103, [P, 64], part=256)
        eps_col, one_col = misc[:, 0:1], misc[:, 1:2]
        gate_bias = [misc[0:8, 2 + l:3 + l] for l in range(DEPTH)]
        rowmax, rowsum = misc[:, 8:16], misc[:, 16:48]

        c = [0]

        def column(n):
            c[0] += n
            return cols[:, c[0] - n:c[0]]

        mod = [column(48) for _ in range(DEPTH)]
        mod2, mod2c = column(24), column(16)
        s_mix, s_mlp, g_mixo, g_mlpo = ([column(8) for _ in range(DEPTH)] for _ in range(4))
        s_2, s_2c, g_2o = column(8), column(8), column(8)
        cact = column(24)

        m_ones = [pool.do(lambda e: e.memset(ones[:, :], 1.0)),
                  pool.do(lambda e: e.memset(ident[:, :], 0.0)),
                  pool.do(lambda e: e.memset(eps_col, EPS)),
                  pool.do(lambda e: e.memset(one_col, 1.0))]
        pool.wait(m_ones[1])
        m_ident = pool.do(lambda e: e.affine_select(out=ident[:, :], in_=ident[:, :], compare_op=ALU.not_equal,
                                                    fill=1.0, base=0, pattern=[[-1, P]], channel_multiplier=1))

        stage = at("param_rows", 90, [P, 9, P])
        m_stage = pool.do(lambda e: e.memset(stage[:, :, :], 0.0))
        land_par = Landing(sem("params_landed"))
        sp.wait(m_stage)

        def rows(tile, r, src):
            n = src.shape[0]
            while n:
                k = min(n, P - r)
                a = stage[r:r + k, tile, :]
                land_par.load(sp, a, src[src.shape[0] - n:src.shape[0] - n + k, :])
                n -= k
                r += k
                if r == P:
                    tile, r = tile + 1, 0

        vec = lambda ap: ap.rearrange("(n p) -> n p", p=P)
        tap = lambda ap: ap.rearrange("k (n p) -> (k n) p", p=P)
        rows(8, 0, vec(A["b_mod_2"][0]))
        rows(8, 24, vec(A["pre_g_2"][0]))
        rows(8, 32, vec(A["post_g_2"][0]))
        rows(8, 40, tap(A["conv_w_2"][0]))
        rows(8, 64, vec(A["conv_b_2"][0]))
        rows(8, 72, vec(A["c"][0]))
        rows(8, 80, vec(A["c_2"][0]))
        rows(8, 88, vec(A["c_ctx_2"]))
        B_ADA, G_PRE_MIX, G_POST_MIX, G_PRE_MLP, G_POST_MLP, B_CONV_M, G_MH, B_DW, G_CN, B_CN = \
            0, 48, 56, 64, 72, 80, 88, 96, 104, 112
        W_CONV_M, W_DW = 128, 160
        for l in range(DEPTH):
            rows(4 * l, B_ADA, vec(A["b_ada"][l]))
            for r, n in ((G_PRE_MIX, "g_pre_mix"), (G_POST_MIX, "g_post_mix"), (G_PRE_MLP, "g_pre_mlp"),
                         (G_POST_MLP, "g_post_mlp"), (B_CONV_M, "b_conv_m"), (G_MH, "g_mh"), (B_DW, "b_dw"),
                         (G_CN, "g_cn"), (B_CN, "b_cn")):
                rows(4 * l, r, vec(A[n][l]))
            rows(4 * l + 1, 0, tap(A["w_conv_m"][l]))
            rows(4 * l + 1, 32, tap(A["w_dw"][l]))
        for l in range(DEPTH):
            land_par.load(sp, gate_bias[l], A["b_gates"][l].rearrange("(g o) -> g o", o=1))
        m_par = (land_par.sem, land_par.count)

        x_all = at("x_all", 24, [P, DT, T])
        x = [x_all[:, i, :] for i in range(DT)]
        x_tok = at("x_tok", 80, [P, N_CH, D])
        land_x = Landing(sem("x_landed"))
        m_xt = land_x.load(sp, x_tok[:, :, :], A["x"][0].rearrange("(j p) n -> p j n", p=P))

        def to_columns(tiles, dst_of, marks):
            i, ps = take_bank()
            for n, t in enumerate(tiles):
                pe.wait(*marks)
                m = pe.do(lambda e, n=n, t=t: e.transpose(ps[:, n * P:(n + 1) * P], stage[:, t, :], ident[:, :]))
            dve.wait(m)
            m = dve.do(lambda e: e.tensor_copy(dst_of, ps[:, 0:len(tiles) * P]))
            bank_free[i] = [m]
            return m

        m_par2 = to_columns([8], par2[:, :], [m_par, m_ident])
        m_parl = [to_columns(range(4 * l, 4 * l + 4), par[l][:, :], [m_par, m_ident]) for l in range(DEPTH)]
        act.wait(m_par2)
        m_cact = act.do(lambda e: e.activation(cact, par2[:, 72:96], ACT.Silu))

        def transpose_in(src_of, dst_of, n_feat, n_chunk, marks, extra=()):
            done = []
            for f in range(n_feat):
                i, ps = take_bank()
                for j in range(n_chunk):
                    pe.wait(*marks)
                    m = pe.do(lambda e, f=f, j=j: e.transpose(ps[:, j * P:(j + 1) * P], src_of(f, j), ident[:, :]))
                q = (dve, act)[f % 2]
                q.wait(m, *extra)
                if f % 2:
                    m = act.do(lambda e, f=f, ps=ps: e.activation(dst_of(f), ps[:, 0:n_chunk * P], ACT.Copy))
                else:
                    m = dve.do(lambda e, f=f, ps=ps: e.tensor_copy(dst_of(f), ps[:, 0:n_chunk * P]))
                bank_free[i] = [m]
                done.append(m)
            return done

        m_x = transpose_in(lambda f, j: x_tok[:, j, f * P:(f + 1) * P], lambda f: x[f][:, :], DT, N_CH,
                           [m_xt, m_ident])

        RAW, HL = 2, 2
        raw = [at(f"w_raw{i}", 4 * i, [P, 2048]) for i in range(RAW)]
        w_hi = [at(f"w_hi{i}", 8 + 4 * i, [P, 2048], F32R) for i in range(HL)]
        w_lo = [at(f"w_lo{i}", 16 + 4 * i, [P, 2048], F32R) for i in range(HL)]
        land_w = [Landing(sem(f"w_landed{i}")) for i in range(RAW)]
        plan = []

        def plan_gemm(key, w, row0, kt, col0, groups, interleave=()):
            interleave = deque(interleave)
            for g in range(groups):
                for kh in range(kt // 4):
                    src = w[row0 + kh * 512:row0 + kh * 512 + 512, col0 + g * 512:col0 + g * 512 + 512]
                    plan.append(((key, g, kh), [(0, 2048, src.rearrange("(k p) n -> p k n", p=P))], True))
                    if interleave:
                        plan.append(interleave.popleft())
            plan.extend(interleave)

        def gemv_blocks(key, w, g0, g1):
            return [((key, g, kh), [(0, 2048, w[kh * 512:kh * 512 + 512, g * 512:g * 512 + 512]
                                     .rearrange("(k p) n -> p k n", p=P))], False)
                    for g in range(g0, g1) for kh in range(2)]

        plan += gemv_blocks("ada0", A["w_ada"][0], 0, 4)
        GLU_B, GLU_A, X_M, Z = 3072, 2048, 0, 1024
        for l in range(DEPTH):
            rest = deque(gemv_blocks("ada0", A["w_ada"][0], 4, 12) if l == 0 else [])
            take = lambda n: [rest.popleft() for _ in range(min(n, len(rest)))]
            for half in range(2):
                plan_gemm(f"glu_b{l}{half}", A["w_in"][l], 0, DT, GLU_B + 512 * half, 1, take(2))
                plan_gemm(f"glu_a{l}{half}", A["w_in"][l], 0, DT, GLU_A + 512 * half, 1, take(2))
            for half in range(2):
                plan_gemm(f"x_m{l}{half}", A["w_in"][l], 0, DT, X_M + 512 * half, 1, take(2))
                plan_gemm(f"z{l}{half}", A["w_in"][l], 0, DT, Z + 512 * half, 1, take(2))
                for h in (2 * half, 2 * half + 1):
                    plan.append(((f"qkv{l}", h, 0), [(512 * n, 512, A[w][l, h].rearrange("(k p) n -> p k n", p=P))
                                                     for n, w in enumerate(("w_q", "w_k", "w_v"))], True))
            plan_gemm(f"w_out{l}", A["w_out"][l], 0, 2 * DT, 0, 2)
            nxt = gemv_blocks("ada1", A["w_ada"][1], 0, 12) if l == 0 else gemv_blocks("mod2", A["w_mod_2"][0], 0, 6)
            nxt = deque(nxt)
            take = lambda n: [nxt.popleft() for _ in range(min(n, len(nxt)))]
            for step in ("up0", "up1", "down0", "up2", "down1", "up3", "down2", "down3"):
                q = int(step[-1])
                if step[:2] == "up":
                    plan_gemm(f"{step}_{l}", A["w_ff1"][l], 0, DT, q * 1024, 2, take(4))
                else:
                    plan_gemm(f"{step}_{l}", A["w_ff2"][l], q * 1024, DT, 0, 2, take(4))
        w2 = A["w_in_2"][0]
        for key, col in (("q2", 4096), ("k2", 5120), ("v2", 6144), ("z_b", 7168)):
            plan_gemm(key, w2, 0, DT, col, 2)
        plan_gemm("w_out_attn", A["w_out_attn_2"][0], 0, DT, 0, 2)
        plan_gemm("g_b", w2, 0, DT, 9216, 2)
        for half in range(2):
            for key, col in (("z_a", 3072), ("b_gate", 0), ("c_gate", 1024), ("x_in", 2048)):
                plan_gemm(f"{key}{half}", w2, 0, DT, col + 512 * half, 1)
        plan_gemm("g_a", w2, 0, DT, 8192, 2)
        plan_gemm("w_out_conv", A["w_out_conv_2"][0], 0, DT, 0, 2)
        plan_gemm("w_o", A["w_o_2"][0], 0, DT, 0, 2)

        raw_free = [None] * RAW
        hl_free = [None] * HL
        ready = {}
        nxt_load, nxt_prep, split_count, used = [0], [0], [0], [0]

        def issue_loads(limit):
            while nxt_load[0] < min(limit, len(plan)):
                n = nxt_load[0]
                s = n % RAW
                sp.wait(raw_free[s])
                for off, size, src in plan[n][1]:
                    k, w = src.shape[1], src.shape[2]
                    dst = raw[s][:, off:off + size].rearrange("p (k n) -> p k n", k=k)
                    land_w[s].load(sp, dst, src)
                landed[n] = (land_w[s].sem, land_w[s].count)
                nxt_load[0] += 1

        landed = {}
        gemv_done = {}

        def prepare(limit):
            while nxt_prep[0] < min(limit, len(plan)):
                n = nxt_prep[0]
                issue_loads(n + 1)
                key, parts, split = plan[n]
                s = n % RAW
                size = sum(p[1] for p in parts)
                if split:
                    t = split_count[0] % HL
                    split_count[0] += 1
                    act.wait(landed[n], hl_free[t])
                    m = act.do(lambda e, s=s, t=t, size=size: e.activation(w_hi[t][:, 0:size], raw[s][:, 0:size],
                                                                           ACT.Copy))
                    pool.wait(landed[n], m)
                    m = pool.do(lambda e: e.tensor_tensor(
                        w_lo[t][:, 0:size], raw[s][:, 0:size], w_hi[t][:, 0:size].bitcast(F32), ALU.subtract))
                    raw_free[s] = m
                    ready[key] = (t, m)
                else:
                    raw_free[s] = consume_gemv(key, raw[s], landed[n])
                nxt_prep[0] += 1
                pump(2, 2)

        gemv_acc = [at("gemv_acc", 101, [P, 512]), at("gemv_acc_ctx", 102, [P, 512])]
        gemv_last = {0: None, 1: None}
        gemv_free = {0: None, 1: None}
        TARGETS = {"ada0": [(0, 0, mod[0], 48)], "ada1": [(0, 0, mod[1], 48)],
                   "mod2": [(0, 1, mod2, 24), (1, 2, mod2c, 16)]}
        m_mod = {}

        def consume_gemv(key, w, m_landed):
            name, g, kh = key
            if kh == 0:
                flush_gemv()
            for a, which, dst, n_dst in TARGETS[name]:
                if 4 * g >= n_dst:
                    continue
                acc = gemv_acc[a]
                for k in range(4):
                    if kh == 0 and k == 0:
                        dve.wait(m_landed, m_cact, gemv_free[a])
                        gemv_last[a] = dve.do(lambda e, acc=acc, which=which: e.tensor_scalar(
                            acc[:, :], w[:, 0:512], cact[:, 8 * which:8 * which + 1], None, ALU.mult))
                    else:
                        dve.wait(m_landed, gemv_last[a])
                        gemv_last[a] = dve.do(lambda e, acc=acc, which=which, k=k: e.scalar_tensor_tensor(
                            acc[:, :], w[:, 512 * k:512 * k + 512],
                            cact[:, 8 * which + 4 * kh + k:8 * which + 4 * kh + k + 1], acc[:, :], ALU.mult, ALU.add))
            end = (dve.sem, dve.count)
            if kh == 1:
                for a, which, dst, n_dst in TARGETS[name]:
                    if 4 * g >= n_dst:
                        continue
                    gemv_tail.append((name, a, g, dst, gemv_last[a]))
            return end

        gemv_tail = []

        def flush_gemv():
            while gemv_tail:
                name, a, g, dst, m = gemv_tail.pop(0)
                i, ps = take_bank()
                pe.wait(m, m_ones[0])
                for n in range(4):
                    step = lambda e, n=n, a=a: e.matmul(ps[:, n:n + 1], gemv_acc[a][:, n * P:(n + 1) * P],
                                                        ones[:, 0:1], start=True, stop=True)
                    if n < 3:
                        pe.quiet(step)
                gemv_free[a] = m = pe.do(step)
                bias = par2[:, 4 * g:4 * g + 4] if name == "mod2" else par[int(name[-1])][:, 4 * g:4 * g + 4]
                dve.wait(m, m_par2, *m_parl)
                m = dve.do(lambda e, ps=ps, dst=dst, g=g, bias=bias: e.tensor_tensor(
                    dst[:, 4 * g:4 * g + 4], ps[:, 0:4], bias, ALU.add))
                bank_free[i] = [m]
                m_mod[name, a] = m

        fill = {"dve": deque(), "pool": deque()}

        def pump(n_dve, n_pool):
            for _ in range(min(n_dve, len(fill["dve"]))):
                fill["dve"].popleft()()
            for _ in range(min(n_pool, len(fill["pool"]))):
                fill["pool"].popleft()()

        def products(ps_ap, whi, wlo, xhi, xlo, first, last, mark):
            seq = [(wlo, xhi), (whi, xlo), (whi, xhi)]
            for n, (a, b) in enumerate(seq):
                step = lambda e, a=a, b=b, n=n: e.matmul(ps_ap, a, b, start=first and n == 0,
                                                         stop=last and n == 2)
                if mark and n == 2:
                    return pe.do(step)
                pe.quiet(step)

        def gemm(key, group, kt, rhs, evac, second=None, evac2=None, fills=(2, 1)):
            banks = [take_bank() for _ in range(4)]
            if second:
                banks2 = [take_bank() for _ in range(2)]
            for kh in range(kt // 4):
                while (key, group, kh) not in ready:
                    prepare(nxt_prep[0] + 1)
                t, m_w = ready.pop((key, group, kh))
                if nxt_prep[0] < len(plan):
                    prepare(nxt_prep[0] + 1)
                    while nxt_prep[0] < len(plan) and not plan[nxt_prep[0] - 1][2]:
                        prepare(nxt_prep[0] + 1)
                issue_loads(nxt_prep[0] + 1)
                pe.wait(m_w)
                for m in range(4):
                    for k in range(4):
                        hi, lo, mark = rhs[4 * kh + k]
                        pe.wait(*(mark if isinstance(mark, list) else [mark]))
                        c0 = 512 * k + P * m
                        first, last = kh == 0 and k == 0, kh == kt // 4 - 1 and k == 3
                        done = products(banks[m][1][:, 0:hi.shape[1]], w_hi[t][:, c0:c0 + P], w_lo[t][:, c0:c0 + P],
                                        hi, lo, first, last, k == 3)
                        if last:
                            banks[m] += (done,)
                    if second:
                        ps2 = banks2[m // 2][1][:, (m % 2) * CTX:(m % 2 + 1) * CTX]
                        for k in range(4):
                            hi, lo, mark = second[4 * kh + k]
                            pe.wait(*(mark if isinstance(mark, list) else [mark]))
                            c0 = 512 * k + P * m
                            first = kh == 0 and k == 0
                            last = kh == kt // 4 - 1 and k == 3
                            seq = [(w_lo, hi), (w_hi, lo), (w_hi, hi)]
                            for n, (a, b) in enumerate(seq):
                                step = lambda e, a=a, b=b, c0=c0, ps2=ps2, st=(first and n == 0 and m % 2 == 0), \
                                    en=(last and n == 2): e.matmul(ps2, a[t][:, c0:c0 + P], b, start=st, stop=en,
                                                                   skip_group_check=True)
                                if k == 3 and n == 2:
                                    done = pe.do(step)
                                else:
                                    pe.quiet(step)
                        if last:
                            banks2[m // 2] += (done,)
                    pump(*fills)
                hl_free[t] = done
            flush_gemv()
            for m in range(4):
                i, ps, done = banks[m]
                bank_free[i] = evac(4 * group + m, ps, done)
            if second:
                for m in range(2):
                    i, ps, _, done = banks2[m]
                    bank_free[i] = evac2(2 * group + m, ps, done)

        def mean_square(tiles, marks, sq_ring, sq_free, n_tok, scale, rstd, rstd_free, ones_w=None, pre=None):
            i, ps = take_bank()
            for n, tl in enumerate(tiles):
                r = n % len(sq_ring)
                act.wait(*([marks[n]] if not isinstance(marks[n], list) else marks[n]), sq_free[r])
                m = act.do(lambda e, tl=tl, r=r: e.activation(sq_ring[r], tl, ACT.Square))
                pe.wait(m, m_ones[0])
                sq_free[r] = pe.do(lambda e, r=r, n=n: e.matmul(ps[:, 0:n_tok], ones[:, :], sq_ring[r],
                                                                start=n == 0, stop=n == len(tiles) - 1))
            act.wait(sq_free[r], rstd_free, *m_ones)
            m = act.do(lambda e: e.activation(rstd, ps[:, 0:n_tok], ACT.Ln, bias=eps_col, scale=scale))
            bank_free[i] = [m]
            act.wait(m)
            return act.do(lambda e: e.activation(rstd, rstd, ACT.Exp, scale=-0.5))

        def modulate(tiles, marks, rstd, m_rstd, s, sh, m_s, tmp, tmp_free, hi, lo, war):
            got = []
            for n, tl in enumerate(tiles):
                r = n % len(tmp)
                dve.wait(marks[n], m_rstd, m_s, tmp_free[r])
                m1 = dve.do(lambda e, tl=tl, r=r, n=n: e.scalar_tensor_tensor(tmp[r], tl, s[:, n:n + 1], rstd,
                                                                              ALU.mult, ALU.mult))
                act.wait(m1, *war)
                m2 = act.do(lambda e, r=r, n=n: e.activation(hi[n], tmp[r], ACT.Identity, bias=sh[:, n:n + 1]))
                got.append((m2, r, n))
                if n >= 1:
                    got[n - 1] = lo_part(got[n - 1], tmp, sh, hi, lo, tmp_free, war)
            got[-1] = lo_part(got[-1], tmp, sh, hi, lo, tmp_free, war)
            return got

        def lo_part(g, tmp, sh, hi, lo, tmp_free, war):
            m2, r, n = g
            dve.wait(m2, *war)
            m3 = dve.do(lambda e: e.scalar_tensor_tensor(lo[n], tmp[r], sh[:, n:n + 1], hi[n].bitcast(F32),
                                                         ALU.add, ALU.subtract))
            tmp_free[r] = m3
            return (hi[n], lo[n], m3)

        def scale_columns(dst, g, sc, mark):
            dve.wait(mark)
            m = dve.do(lambda e: e.tensor_scalar(dst, sc, 1.0, None, ALU.add))
            dve.wait(m)
            return dve.do(lambda e: e.tensor_tensor(dst, dst, g, ALU.mult))

        def gate_columns(dst, g, gt, mark):
            dve.wait(mark)
            return dve.do(lambda e: e.tensor_tensor(dst, gt, g, ALU.mult))

        def split(src, hi, lo, marks, war=()):
            act.wait(*marks, *war)
            m = act.do(lambda e: e.activation(hi, src, ACT.Copy))
            dve.wait(m, *marks, *war)
            m2 = dve.do(lambda e: e.tensor_tensor(lo, src, hi.bitcast(F32), ALU.subtract))
            return m2

        x_spill = nc.dram_tensor("x_spill", (D, T), F32, kind="Internal").ap().rearrange("(n p) t -> p n t", p=P)
        land_spill, land_back = Landing(sem("x_spilled")), Landing(sem("x_back"))

        def now():
            return [(q.sem, q.count) for q in (pe, act, dve, pool) if q.count]

        y = [at(f"y{i}", 84 + i, [P, T]) for i in range(DT)]
        tmpf = [at(f"tmp{i}", 92 + i, [P, T]) for i in range(9)]

        def residual(tiles, marks, g, m_g, rstd, m_rstd, tmps, x_marks):
            res, prod = [], []
            for n in range(DT):
                dve.wait(marks[n], m_rstd, m_g)
                prod.append(dve.do(lambda e, n=n: e.scalar_tensor_tensor(tiles[n], tiles[n], g[:, n:n + 1], rstd,
                                                                         ALU.mult, ALU.mult)))
                if n >= 1:
                    k = n - 1
                    dve.wait(prod[k], x_marks[k])
                    res.append(dve.do(lambda e, k=k: e.tensor_tensor(x[k][:, :], x[k][:, :], tiles[k], ALU.add)))
            dve.wait(prod[-1], x_marks[-1])
            res.append(dve.do(lambda e: e.tensor_tensor(x[DT - 1][:, :], x[DT - 1][:, :], tiles[DT - 1], ALU.add)))
            return res

        h_hi = [at(f"h_hi{i}", 35 + i, [P, T], F32R) for i in range(DT)]
        h_lo = [at(f"h_lo{i}", 43 + i, [P, T], F32R) for i in range(DT)]
        sq_ring = [tmpf[0][:, :], tmpf[1][:, :]]
        sq_free = [None, None]
        rstd = tmpf[2][:, :]
        mod_tmp = [t[:, :] for t in tmpf[3:7]]
        x_ap = [t[:, :] for t in x]
        y_ap = [t[:, :] for t in y]
        full = lambda tiles: [t[:, :] for t in tiles]

        a_pad = [at(f"a_pad{i}", 51, [P, CONV_G - 1 + T], part=(CONV_G + 1 + T) * i) for i in range(DT)]
        conv_acc = [at(f"conv_acc{i}", 24 + i, [P, T]) for i in range(DT)]
        sig_b = [at(f"sig_b{i}", 88 + i, [P, T]) for i in range(4)]
        xm = [(at(f"xm_hi{i}", 60 + i, [P, T], F32R), at(f"xm_lo{i}", 64 + i, [P, T], F32R)) for i in range(4)]
        xc = [(at(f"xc_hi{i}", 68 + i, [P, T], F32R), at(f"xc_lo{i}", 72 + i, [P, T], F32R)) for i in range(4)]
        x_pad = [at(f"x_pad{i}", 96, [P, CONV_M - 1 + T], part=(CONV_M + 4 + T) * i) for i in range(2)]
        acc4 = [at(f"acc4_{i}", 92 + i, [P, T]) for i in range(2)]
        xcf = [at(f"xcf{i}", 94 + i, [P, T]) for i in range(2)]
        sig_z = [at(f"sig_z{i}", 88 + i, [P, T]) for i in range(DT)]
        q_slot = lambda h, m: (76 if h < 2 else 35) + 2 * (h % 2) + m
        qkv = {(s, h, m): at(f"{'qkv'[s]}{h}{m}", q_slot(h, m) + 4 * s, [P, T])
               for s in range(3) for h in range(HEADS) for m in range(2)}
        hm_hi = [at(f"hm_hi{n}", q_slot(n // 2, n % 2) + 4, [P, T], F32R) for n in range(DT)]
        hm_lo = [at(f"hm_lo{n}", q_slot(n // 2, n % 2), [P, T], F32R) for n in range(DT)]
        wg = at("w_gates_sb", 59, [P, 6, 32], part=256)
        a_hi = [at(f"a_hi{i}", 60 + i, [P, T], F32R) for i in range(DT)]
        a_lo = [at(f"a_lo{i}", 68 + i, [P, T], F32R) for i in range(DT)]
        a_sq = [at(f"a_sq{i}", 60 + i, [P, T]) for i in range(DT)]
        a_rstd = [at(f"a_rstd{i}", 68 + i, [P, T]) for i in range(DT)]
        g8 = at("gates", 49, [8, T])
        row_t, row_lf, row_ones = (at(n, s, [4, T]) for n, s in (("row_t", 96), ("row_lf", 97), ("row_ones", 98)))
        row_negm, row_em = at("row_negm", 99, [4, T]), at("row_em", 100, [4, T])
        row_b, row_c = at("row_b", 101, [4, T]), at("row_c", 102, [4, T])
        c_col = misc[:, 48:64]
        v_t = at("v_t", 47, [P, N_CH, HEAD_D])
        pt = [at(f"p_t{j}", 96, [P, T - P * j], part=sum(T - P * i for i in range(j))) for j in range(N_CH)]
        negm_bc, diag = at("negm_bc", 101, [P, T]), at("diag", 102, [P, T])
        den, hm_sq = at("den", 49, [P, T]), [at("hm_sq0", 49, [P, T]), at("hm_sq1", 50, [P, T])]
        hm_rstd = at("hm_rstd", 101, [P, T])
        land_wg = Landing(sem("w_gates_landed"))

        f1 = [[(at(f"f1_hi{b}{i}", 51 + 16 * b + i, [P, T], F32R), at(f"f1_lo{b}{i}", 59 + 16 * b + i, [P, T], F32R))
               for i in range(QUARTER)] for b in range(2)]

        def finish_conv(l, i, m_acc):
            acc = conv_acc[i][:, :]
            p = par[l]
            b, ps = take_bank()
            pe.wait(m_acc, m_ones[0])
            m = pe.do(lambda e: e.matmul(ps[:, :], ones[:, :], acc, start=True, stop=True))
            dve.wait(m)
            m = dve.do(lambda e: e.scalar_tensor_tensor(acc, ps[:, :], -1.0 / P, acc, ALU.mult, ALU.add))
            bank_free[b] = [m]
            act.wait(m)
            m = act.do(lambda e: e.activation(a_sq[i][:, :], acc, ACT.Square))
            b, ps2 = take_bank()
            pe.wait(m)
            m = pe.do(lambda e: e.matmul(ps2[:, :], ones[:, :], a_sq[i][:, :], start=True, stop=True))
            act.wait(m)
            m = act.do(lambda e: e.activation(a_rstd[i][:, :], ps2[:, :], ACT.Ln, bias=eps_col, scale=1.0 / P))
            bank_free[b] = [m]
            act.wait(m)
            m = act.do(lambda e: e.activation(a_rstd[i][:, :], a_rstd[i][:, :], ACT.Exp, scale=-0.5))
            dve.wait(m)
            m = dve.do(lambda e: e.scalar_tensor_tensor(acc, acc, p[:, G_CN + i:G_CN + i + 1], a_rstd[i][:, :],
                                                        ALU.mult, ALU.mult))
            act.wait(m)
            m = act.do(lambda e: e.activation(acc, acc, ACT.Silu, bias=p[:, B_CN + i:B_CN + i + 1]))
            return split(acc, a_hi[i][:, :], a_lo[i][:, :], [m])

        def layer(l, m_x):
            p = par[l]
            flush_gemv()
            m_s = scale_columns(s_mix[l], p[:, G_PRE_MIX:G_PRE_MIX + 8], mod[l][:, 8:16], m_mod[f"ada{l}", 0])
            act.wait(*m_x)
            m_spill = land_spill.load(act, x_spill, x_all[:, :, :])
            m_wg = land_wg.load(act, wg[:, :, :],
                                A["w_gates"][l].rearrange("(n p h) g -> p n (h g)", p=P, h=HEADS))
            m_r = mean_square(x_ap, m_x, sq_ring, sq_free, T, 1.0 / D, rstd, None)
            tmp_free = [None] * 4
            h = modulate(x_ap, m_x, rstd, m_r, s_mix[l], mod[l][:, 0:8], m_s, mod_tmp, tmp_free,
                         full(h_hi), full(h_lo), m_x)

            dve.wait(*m_x)
            for i in range(DT):
                m_pad = dve.do(lambda e, i=i: e.memset(a_pad[i][:, 0:CONV_G - 1], 0.0))
            m_a, m_acc = {}, {}
            sig = {}

            def conv_taps(queue, tiles):
                def tap_of(i, k):
                    w = p[:, W_DW + 8 * k + i:W_DW + 8 * k + i + 1]
                    src, acc = a_pad[i][:, k:k + T], conv_acc[i][:, :]
                    if k == 0:
                        queue.wait(m_a[i], m_pad, m_spill, h[-1][2], *m_parl)
                        m_acc[i] = queue.do(lambda e: e.tensor_scalar(acc, src, w, p[:, B_DW + i:B_DW + i + 1],
                                                                      ALU.mult, ALU.add))
                    else:
                        queue.wait(m_acc[i])
                        m_acc[i] = queue.do(lambda e: e.scalar_tensor_tensor(acc, src, w, acc, ALU.mult, ALU.add))
                return [lambda i=i, k=k: tap_of(i, k) for k in range(CONV_G) for i in tiles]

            def glu_b_evac(n, ps, done):
                act.wait(done, m_a.get(n - 4))
                sig[n] = act.do(lambda e: e.activation(sig_b[n % 4][:, :], ps[:, :], ACT.Sigmoid))
                return [sig[n]]

            def glu_a_evac(n, ps, done):
                dve.wait(done, sig[n], m_pad)
                m_a[n] = dve.do(lambda e: e.tensor_tensor(a_pad[n][:, CONV_G - 1:], ps[:, :], sig_b[n % 4][:, :],
                                                          ALU.mult))
                return [m_a[n]]

            for half in range(2):
                gemm(f"glu_b{l}{half}", 0, DT, h, lambda n, ps, done: glu_b_evac(4 * half + n, ps, done))
                gemm(f"glu_a{l}{half}", 0, DT, h, lambda n, ps, done: glu_a_evac(4 * half + n, ps, done))
                for i in (4 * half, 4 * half + 2):
                    fill["dve"].extend(conv_taps(dve, (i, i + 1)))

            m_xm, m_xc, m_qkv = [None] * 4, [None] * 4, {}
            pad_free, acc_free, xcf_free = [None, None], [None, None], [None, None]
            dve.wait(h[-1][2])
            for i in range(2):
                m_pad3 = dve.do(lambda e, i=i: e.memset(x_pad[i][:, 0:CONV_M - 1], 0.0))

            def x_m_evac(n, ps, done, war):
                j, r = n % 4, n % 2
                hi, lo = xm[j][0][:, :], xm[j][1][:, :]
                act.wait(done, pad_free[r], *war)
                m_hi = act.do(lambda e: e.activation(hi, ps[:, :], ACT.Copy))
                m_f = act.do(lambda e: e.activation(x_pad[r][:, CONV_M - 1:], ps[:, :], ACT.Copy))
                dve.wait(m_hi, m_f, *war)
                m_lo = dve.do(lambda e: e.tensor_tensor(lo, x_pad[r][:, CONV_M - 1:], hi.bitcast(F32), ALU.subtract))
                m_xm[j] = m_lo
                acc = acc4[r][:, :]
                dve.wait(m_f, m_pad3, acc_free[r])
                for k in range(CONV_M):
                    w = p[:, W_CONV_M + 8 * k + n:W_CONV_M + 8 * k + n + 1]
                    src = x_pad[r][:, k:k + T]
                    if k == 0:
                        m = dve.do(lambda e, w=w, src=src: e.tensor_scalar(acc, src, w, None, ALU.mult))
                    else:
                        dve.wait(m)
                        m = dve.do(lambda e, w=w, src=src: e.scalar_tensor_tensor(acc, src, w, acc, ALU.mult, ALU.add))
                pad_free[r] = m
                act.wait(m, xcf_free[r])
                m = acc_free[r] = act.do(lambda e: e.activation(xcf[r][:, :], acc, ACT.Silu,
                                                                bias=p[:, B_CONV_M + n:B_CONV_M + n + 1]))
                m_xc[j] = xcf_free[r] = split(xcf[r][:, :], xc[j][0][:, :], xc[j][1][:, :], [m], war)
                return [m_f]

            m_z = {}

            def z_evac(n, ps, done):
                act.wait(done, m_a[7], *xcf_free)
                m_z[n] = act.do(lambda e: e.activation(sig_z[n][:, :], ps[:, :], ACT.Sigmoid))
                return [m_z[n]]

            war = []
            for half in range(2):
                gemm(f"x_m{l}{half}", 0, DT, h, lambda n, ps, done: x_m_evac(4 * half + n, ps, done, war))
                gemm(f"z{l}{half}", 0, DT, h, lambda n, ps, done: z_evac(4 * half + n, ps, done))
                for head in (2 * half, 2 * half + 1):
                    while (f"qkv{l}", head, 0) not in ready:
                        prepare(nxt_prep[0] + 1)
                    t, m_w = ready.pop((f"qkv{l}", head, 0))
                    prepare(nxt_prep[0] + 1)
                    issue_loads(nxt_prep[0] + 1)
                    pe.wait(m_w)
                    for s in range(3):
                        src, marks = (xm, m_xm) if s == 2 else (xc, m_xc)
                        for m in range(2):
                            b, ps = take_bank()
                            for k in range(2):
                                j = 2 * (head % 2) + k
                                pe.wait(marks[j])
                                c0 = 512 * s + 256 * k + P * m
                                done = products(ps[:, :], w_hi[t][:, c0:c0 + P], w_lo[t][:, c0:c0 + P],
                                                src[j][0][:, :], src[j][1][:, :], k == 0, k == 1, k == 1)
                            dst = qkv[s, head, m][:, :]
                            if m:
                                act.wait(done)
                                mk = act.do(lambda e, dst=dst, ps=ps: e.activation(dst, ps[:, :], ACT.Copy))
                            else:
                                dve.wait(done)
                                mk = dve.do(lambda e, dst=dst, ps=ps: e.tensor_copy(dst, ps[:, :]))
                            bank_free[b] = [mk]
                            m_qkv[s, head, m] = mk
                    hl_free[t] = done
                    pump(4, 3)
                war = [done]

            b, ps = take_bank()
            first = True
            for s in range(3):
                for m in range(2):
                    for head in range(HEADS):
                        pe.wait(m_qkv[s, head, m], m_wg)
                        step = lambda e, s=s, m=m, head=head, st=first: e.matmul(
                            ps[0:8, :], wg[:, 2 * s + m, 8 * head:8 * head + 8], qkv[s, head, m][:, :],
                            start=st, stop=(s, m, head) == (2, 1, HEADS - 1))
                        first = False
                        if (s, m, head) == (2, 1, HEADS - 1):
                            done = pe.do(step)
                        else:
                            pe.quiet(step)
            act.wait(done, m_par)
            m_g8 = act.do(lambda e: e.activation(g8[:, :], ps[0:8, :], ACT.Identity, bias=gate_bias[l]))
            bank_free[b] = [m_g8]
            b, ps_f = take_bank()
            pe.wait(m_g8)
            m_f = pe.do(lambda e: e.matmul(ps_f[0:4, :], ident[0:8, 4:8], g8[:, :], start=True, stop=True))
            act.wait(m_f, *[(q.sem, q.count) for q in (dve,)])
            m = act.do(lambda e: e.activation(row_t[:, :], ps_f[0:4, :], ACT.Abs))
            act.wait(m)
            m = act.do(lambda e: e.activation(row_t[:, :], row_t[:, :], ACT.Exp, scale=-1.0))
            act.wait(m)
            m = act.do(lambda e: e.activation(row_t[:, :], row_t[:, :], ACT.Ln, bias=one_col[0:4, :]))
            dve.wait(m_f, m)
            m_o = dve.do(lambda e: e.memset(row_ones[:, :], 1.0))
            m2 = dve.do(lambda e: e.tensor_scalar(row_lf[:, :], ps_f[0:4, :], 0.0, None, ALU.min))
            bank_free[b] = [m2, m]
            dve.wait(m2)
            m = dve.do(lambda e: e.tensor_tensor(row_lf[:, :], row_lf[:, :], row_t[:, :], ALU.subtract))
            dve.wait(m, m_o)
            m = dve.do(lambda e: e.tensor_tensor_scan(row_b[:, :], row_ones[:, :], row_lf[:, :], 0.0, ALU.mult, ALU.add))
            dve.wait(m)
            m_c = dve.do(lambda e: e.tensor_tensor(row_c[:, :], g8[0:4, :], row_b[:, :], ALU.subtract))
            dve.wait(m_c)
            m = dve.do(lambda e: e.tensor_tensor_scan(row_t[:, :], row_ones[:, :], row_c[:, :], 0.0, ALU.mult, ALU.max))
            dve.wait(m)
            m_nm = dve.do(lambda e: e.tensor_scalar(row_negm[:, :], row_t[:, :], -1.0, None, ALU.mult))
            m = dve.do(lambda e: e.tensor_tensor(row_em[:, :], row_b[:, :], row_t[:, :], ALU.add))
            act.wait(m)
            m_em = act.do(lambda e: e.activation(row_em[:, :], row_em[:, :], ACT.Exp, scale=-1.0))
            b, ps = take_bank()
            pe.wait(m_c)
            for j in range(N_CH):
                m = pe.do(lambda e, j=j: e.transpose(ps[:, 4 * j:4 * j + 4], row_c[:, j * P:(j + 1) * P],
                                                     ident[0:4, 0:4]))
            dve.wait(m)
            m_cc = dve.do(lambda e: e.tensor_copy(c_col, ps[:, 0:4 * N_CH]))
            bank_free[b] = [m_cc]

            m_hm, head_end = {}, [m_nm, m_em, m_cc]
            for head in range(HEADS):
                sel = ident[0:4, head:head + 1].to_broadcast([4, P])
                for jj in range(2):
                    b, ps = take_bank()
                    for j in (2 * jj, 2 * jj + 1):
                        for m in range(2):
                            pe.wait(m_qkv[2, head, m], m_ident)
                            mt = pe.do(lambda e, j=j, m=m, jj=jj, ps=ps: e.transpose(
                                ps[:, (2 * (j - 2 * jj) + m) * P:(2 * (j - 2 * jj) + m + 1) * P],
                                qkv[2, head, m][:, j * P:(j + 1) * P], ident[:, :]))
                    dve.wait(mt, *head_end)
                    m_vt = dve.do(lambda e, jj=jj, ps=ps: e.tensor_copy(
                        v_t[:, 2 * jj:2 * jj + 2, :], ps[:, :].rearrange("p (j n) -> p j n", j=2)))
                    bank_free[b] = [m_vt]
                b, ps = take_bank()
                pe.wait(m_nm)
                m = pe.do(lambda e: e.matmul(ps[:, :], sel, row_negm[:, :], start=True, stop=True))
                act.wait(m, *head_end)
                m_bc = act.do(lambda e, ps=ps: e.activation(negm_bc[:, :], ps[:, :], ACT.Copy))
                bank_free[b] = [m_bc]
                pool.wait(m_bc, *head_end)
                m_dg = pool.do(lambda e: e.affine_select(
                    out=diag[:, :].rearrange("p (j t) -> p j t", j=N_CH),
                    in_=negm_bc[:, :].rearrange("p (j t) -> p j t", j=N_CH), compare_op=ALU.is_ge, fill=NEG, base=0,
                    pattern=[[0, N_CH], [1, P]], channel_multiplier=-1))
                m_p = []
                for j in range(N_CH):
                    cj = c_col[:, 4 * j + head:4 * j + head + 1]
                    act.wait(m_dg)
                    m_e = act.do(lambda e, j=j, cj=cj: e.activation(pt[j][:, 0:P], diag[:, j * P:(j + 1) * P],
                                                                    ACT.Exp, bias=cj))
                    if j < N_CH - 1:
                        m_e = act.do(lambda e, j=j, cj=cj: e.activation(pt[j][:, P:], negm_bc[:, (j + 1) * P:],
                                                                        ACT.Exp, bias=cj))
                    b, ps = take_bank()
                    n_t = T - j * P
                    for m in range(2):
                        pe.wait(m_qkv[0, head, m], m_qkv[1, head, m])
                        ms = pe.do(lambda e, j=j, m=m, ps=ps, n_t=n_t: e.matmul(
                            ps[:, 0:n_t], qkv[1, head, m][:, j * P:(j + 1) * P], qkv[0, head, m][:, j * P:],
                            start=m == 0, stop=m == 1))
                    dve.wait(ms, m_e)
                    m = dve.do(lambda e, j=j, ps=ps, n_t=n_t: e.scalar_tensor_tensor(
                        pt[j][:, :], ps[:, 0:n_t], float(HEAD_D) ** -0.5, pt[j][:, :], ALU.mult, ALU.mult))
                    bank_free[b] = [m]
                    m_p.append(m)
                b_den, ps_den = take_bank()
                for j in range(N_CH):
                    pe.wait(m_p[j])
                    m_den = pe.do(lambda e, j=j: e.matmul(ps_den[:, j * P:], ones[:, :], pt[j][:, :],
                                                          start=j == 0, stop=j == N_CH - 1))
                b_em, ps_em = take_bank()
                pe.wait(m_em)
                m_emb = pe.do(lambda e: e.matmul(ps_em[:, :], sel, row_em[:, :], start=True, stop=True))
                act.wait(m_den, m_g8, *head_end)
                m = act.do(lambda e: e.activation(den[:, :], ps_den[:, :], ACT.Abs))
                bank_free[b_den] = [m]
                dve.wait(m, m_emb)
                m = dve.do(lambda e: e.tensor_tensor(den[:, :], den[:, :], ps_em[:, :], ALU.max))
                bank_free[b_em] = [m]
                dve.wait(m)
                m_rec = dve.do(lambda e: e.reciprocal(den[:, :], den[:, :]))
                hm = [qkv[0, head, m][:, :] for m in range(2)]
                m_h = []
                pe.wait(m_vt)
                for m in range(2):
                    b, ps = take_bank()
                    for j in range(N_CH):
                        mv = pe.do(lambda e, j=j, m=m, ps=ps: e.matmul(
                            ps[:, j * P:], v_t[:, j, m * P:(m + 1) * P], pt[j][:, :],
                            start=j == 0, stop=j == N_CH - 1))
                    dve.wait(mv, m_rec)
                    mk = dve.do(lambda e, m=m, ps=ps: e.tensor_tensor(hm[m], ps[:, :], den[:, :], ALU.mult))
                    bank_free[b] = [mk]
                    m_h.append(mk)
                b, ps = take_bank()
                for m in range(2):
                    pe.wait(m_h[m])
                    mm = pe.do(lambda e, m=m, ps=ps: e.matmul(ps[:, :], ones[:, :], hm[m], start=m == 0, stop=m == 1))
                b2, ps2 = take_bank()
                for m in range(2):
                    dve.wait(mm, m_h[m])
                    m_h[m] = dve.do(lambda e, m=m, ps=ps: e.scalar_tensor_tensor(hm[m], ps[:, :], -1.0 / HEAD_D, hm[m],
                                                                                 ALU.mult, ALU.add))
                    act.wait(m_h[m], m_g8)
                    mk = act.do(lambda e, m=m: e.activation(hm_sq[m][:, :], hm[m], ACT.Square))
                    pe.wait(mk)
                    m_v = pe.do(lambda e, m=m, ps2=ps2: e.matmul(ps2[:, :], ones[:, :], hm_sq[m][:, :],
                                                                 start=m == 0, stop=m == 1))
                bank_free[b] = [m_h[1]]
                act.wait(m_v)
                mk = act.do(lambda e, ps2=ps2: e.activation(hm_rstd[:, :], ps2[:, :], ACT.Ln, bias=eps_col,
                                                            scale=1.0 / HEAD_D))
                bank_free[b2] = [mk]
                act.wait(mk)
                m_rs = act.do(lambda e: e.activation(hm_rstd[:, :], hm_rstd[:, :], ACT.Exp, scale=-0.5))
                head_end = [m_rs]
                for m in range(2):
                    n = 2 * head + m
                    dve.wait(m_rs, m_h[m])
                    mk = dve.do(lambda e, m=m, n=n: e.scalar_tensor_tensor(
                        hm[m], hm[m], p[:, G_MH + n:G_MH + n + 1], hm_rstd[:, :], ALU.mult, ALU.mult))
                    dve.wait(mk, m_z[n])
                    mk = dve.do(lambda e, m=m, n=n: e.tensor_tensor(hm[m], hm[m], sig_z[n][:, :], ALU.mult))
                    m_hm[n] = split(hm[m], hm_hi[n][:, :], hm_lo[n][:, :], [mk])
                head_end = [mk, m_rs, m_v, mv]
                pump(30, 16)
            pump(1000, 1000)
            m_aa = [finish_conv(l, i, m_acc[i]) for i in range(DT)]
            act.wait(m_aa[-1], m_spill)
            m_back = land_back.load(act, x_all[:, :, :], x_spill)

            mix = [(hm_hi[n][:, :], hm_lo[n][:, :], m_hm[n]) for n in range(DT)] + \
                  [(a_hi[n][:, :], a_lo[n][:, :], m_aa[n]) for n in range(DT)]
            m_y = [None] * DT

            def y_evac(n, ps, done):
                act.wait(done, *m_hm.values())
                m_y[n] = act.do(lambda e: e.activation(y[n][:, :], ps[:, :], ACT.Copy))
                return [m_y[n]]

            for g in range(2):
                gemm(f"w_out{l}", g, 2 * DT, mix, y_evac)
            flush_gemv()
            m_g = gate_columns(g_mixo[l], p[:, G_POST_MIX:G_POST_MIX + 8], mod[l][:, 16:24], m_mod[f"ada{l}", 0])
            m_s = scale_columns(s_mlp[l], p[:, G_PRE_MLP:G_PRE_MLP + 8], mod[l][:, 32:40], m_mod[f"ada{l}", 0])
            m_r = mean_square(y_ap, m_y, sq_ring, sq_free, T, 1.0 / D, rstd, None)
            m_x = residual(y_ap, m_y, g_mixo[l], m_g, rstd, m_r, None, [m_back] * DT)
            m_r = mean_square(x_ap, m_x, sq_ring, sq_free, T, 1.0 / D, rstd, m_x[-1])
            h = modulate(x_ap, m_x, rstd, m_r, s_mlp[l], mod[l][:, 24:32], m_s, mod_tmp, tmp_free,
                         full(h_hi), full(h_lo), m_x)

            hidden = [[None] * QUARTER for _ in range(2)]
            t_free = [None] * 3
            m_yq = [None] * DT

            def up_evac(b, n, ps, done):
                r = n % 3
                t1, t2 = tmpf[3 + 2 * r][:, :], tmpf[4 + 2 * r][:, :]
                hi, lo = (t[:, :] for t in f1[b][n])
                act.wait(done, t_free[r])
                m1 = act.do(lambda e: e.activation(t1, ps[:, :], ACT.Relu))
                dve.wait(m1, t_free[r])
                m2 = dve.do(lambda e: e.tensor_tensor(t2, t1, t1, ALU.mult))
                t_free[r] = split(t2, hi, lo, [m2])
                hidden[b][n] = (hi, lo, t_free[r])
                return [m1]

            def down_evac(q, n, ps, done):
                if q == 0:
                    act.wait(done, *m_x)
                    m_yq[n] = act.do(lambda e: e.activation(y[n][:, :], ps[:, :], ACT.Copy))
                else:
                    dve.wait(done, m_yq[n])
                    m_yq[n] = dve.do(lambda e: e.tensor_tensor(y[n][:, :], y[n][:, :], ps[:, :], ALU.add))
                return [m_yq[n]]

            for step in ("up0", "up1", "down0", "up2", "down1", "up3", "down2", "down3"):
                q = int(step[-1])
                for g in range(2):
                    if step[:2] == "up":
                        gemm(f"{step}_{l}", g, DT, h, lambda n, ps, done: up_evac(q % 2, n, ps, done))
                    else:
                        gemm(f"{step}_{l}", g, DT, hidden[q % 2], lambda n, ps, done: down_evac(q, n, ps, done))
            m_g = gate_columns(g_mlpo[l], p[:, G_POST_MLP:G_POST_MLP + 8], mod[l][:, 40:48], m_mod[f"ada{l}", 0])
            m_r = mean_square(y_ap, m_yq, sq_ring, sq_free, T, 1.0 / D, rstd, h[-1][2])
            return residual(y_ap, m_yq, g_mlpo[l], m_g, rstd, m_r, None, m_x)

        def second(m_x):
            flush_gemv()
            hc_hi = [at(f"hc_hi{i}", 51, [P, CTX], F32R, part=CTX * i) for i in range(DT)]
            hc_lo = [at(f"hc_lo{i}", 55, [P, CTX], F32R, part=CTX * i) for i in range(DT)]
            q2 = [at(f"q2_{i}", 59 + i, [P, T]) for i in range(DT)]
            k2 = [at(f"k2_{i}", 67 + i, [P, T]) for i in range(DT)]
            vw = at("v_windows", 75, [P, 2 * N_CH, D])
            kc = at("k_ctx", 91, [P, DT, CTX])
            vc = at("v_ctx", 95, [P, 2, D])
            c_tok = at("ctx_tok", 59, [P, CTX // P, D])
            c_f = [at(f"ctx_f{i}", 63, [P, CTX], part=CTX * i) for i in range(DT)]
            csq = [at(f"ctx_sq{i}", 67, [P, CTX], part=CTX * i)[:, :] for i in range(2)]
            c_rstd = at("ctx_rstd", 68, [P, CTX])
            c_tmp = [at(f"ctx_tmp{i}", 69, [P, CTX], part=CTX * i)[:, :] for i in range(4)]
            rope = at("rope", 75, [P, 2, T])
            raw_t = [at(f"rope_in{i}", 77 + i, [P, T]) for i in range(3)]
            rot_t = [at(f"rope_rot{i}", 80 + i, [P, T]) for i in range(3)]
            v_f = at("v_f", 99, [P, N_CH, ROWS, K_COLS])
            vc_f = [at(f"v_ctx_f{i}", 101 + i, [P, 2 * CTX]) for i in range(2)]
            rot = at("rotation", 103, [P, P], part=320)
            mask = at("mask", 51, [P, 3, ROWS * K_COLS])
            bias = [at(f"bias{i}", 52, [P, 3, ROWS * K_COLS], part=256 + 768 * i) for i in range(2)]
            toep = [at(f"toeplitz{i}", 55, [P, ROWS, TOEP], part=256 + ROWS * TOEP * i) for i in range(2)]
            pr = [at(f"prob{i}", s, [P, T]) for i, s in enumerate((57, 58, 99))]
            prt = [at(f"prob_t{i}", 100 + i, [P, T]) for i in range(3)]

            land_c = Landing(sem("second_landed"))
            act.wait(*m_x)
            m_ctx = land_c.load(act, c_tok[:, :, :], A["ctx_2"][0].rearrange("(j p) n -> p j n", p=P))
            land_rope = Landing(sem("rope_landed"))
            m_rope = land_rope.load(act, rope[:, :, :], A["rope"].rearrange("f p t -> p f t"))

            m = pool.do(lambda e: e.memset(rot[:, :], 0.0))
            pool.wait(m)
            view = rot[:, :].rearrange("p (b h c) -> p b h c", h=2, c=16)
            m = pool.do(lambda e: e.affine_select(out=view[:, :, 1, :], in_=view[:, :, 1, :],
                                                  compare_op=ALU.not_equal, fill=1.0, base=0,
                                                  pattern=[[32, 4], [1, 16]], channel_multiplier=-1))
            pool.wait(m)
            m_rot = pool.do(lambda e: e.affine_select(out=view[:, :, 0, :], in_=view[:, :, 0, :],
                                                      compare_op=ALU.not_equal, fill=-1.0, base=16,
                                                      pattern=[[32, 4], [1, 16]], channel_multiplier=-1))

            m_s = scale_columns(s_2, par2[:, 24:32], mod2[:, 8:16], m_mod["mod2", 0])
            m_sc = scale_columns(s_2c, par2[:, 24:32], mod2c[:, 8:16], m_mod["mod2", 1])
            m_r = mean_square(x, m_x, sq_ring, sq_free, T, 1.0 / D, rstd, m_x[-1])
            h = modulate(x, m_x, rstd, m_r, s_2, mod2[:, 0:8], m_s, mod_tmp, [None] * 4,
                         full(h_hi), full(h_lo), m_x)
            m_c = transpose_in(lambda f, j: c_tok[:, j, f * P:(f + 1) * P], lambda f: c_f[f][:, :], DT, CTX // P,
                               [m_ctx, m_ident])
            m_r = mean_square([t[:, :] for t in c_f], m_c, csq, [None, None], CTX, 1.0 / D, c_rstd[:, :], None)
            hc = modulate([t[:, :] for t in c_f], m_c, c_rstd[:, :], m_r, s_2c, mod2c[:, 0:8], m_sc, c_tmp,
                          [None] * 4, full(hc_hi), full(hc_lo), m_x)

            rope_free = [None] * 3
            m_q, m_k = {}, {}

            def rope_evac(dst, got, scale, n, ps, done):
                r = n % 3
                t, ro = raw_t[r][:, :], rot_t[r][:, :]
                act.wait(done, rope_free[r], *m_x)
                m1 = act.do(lambda e: e.activation(t, ps[:, :], ACT.Copy, scale=scale))
                b, ps2 = take_bank()
                pe.wait(m1, m_rot)
                m2 = pe.do(lambda e: e.matmul(ps2[:, :], rot[:, :], t, start=True, stop=True))
                dve.wait(m2, m_rope, rope_free[r])
                m3 = dve.do(lambda e: e.tensor_tensor(ro, ps2[:, :], rope[:, 1, :], ALU.mult))
                bank_free[b] = [m3]
                pool.wait(m2, m_rope, hc[-1][2])
                m4 = pool.do(lambda e: e.tensor_tensor(t, t, rope[:, 0, :], ALU.mult))
                dve.wait(m4, m3)
                if dst is q2:
                    kept = dst[n][:, :].rearrange("p (i r a) -> p r i a", i=N_CH, r=ROWS)
                    t, ro = (v.rearrange("p (r i a) -> p r i a", i=N_CH, r=ROWS) for v in (t, ro))
                else:
                    kept = dst[n][:, :]
                got[n] = rope_free[r] = dve.do(lambda e: e.tensor_tensor(kept, t, ro, ALU.add))
                return [m1]

            m_kc = {}

            def kc_evac(n, ps, done):
                act.wait(done, hc[-1][2], *m_x)
                m_kc[n] = act.do(lambda e: e.activation(kc[:, 2 * n:2 * n + 2, :],
                                                        ps[:, :].rearrange("p (a t) -> p a t", a=2), ACT.Copy))
                return [m_kc[n]]

            for g in range(2):
                gemm("q2", g, DT, h, lambda n, ps, done: rope_evac(q2, m_q, float(A_DIM) ** -0.5, n, ps, done))
            for g in range(2):
                gemm("k2", g, DT, h, lambda n, ps, done: rope_evac(k2, m_k, 1.0, n, ps, done), hc, kc_evac)

            vf_free, vcf_free = None, [None, None]
            m_v, m_vc = {}, {}

            def v_evac(n, ps, done):
                nonlocal vf_free
                act.wait(done, vf_free, *m_q.values())
                grid = ps[:, :].rearrange("p (r c) -> p r c", r=ROWS)
                for i in range(N_CH):
                    m1 = act.do(lambda e: e.activation(v_f[:, i, :, :], grid[:, :, K_START[i]:K_START[i] + K_COLS],
                                                       ACT.Copy))
                for half in range(2):
                    b, ps2 = take_bank()
                    pe.wait(m1)
                    for w in range(4):
                        i, rows_half = (4 * half + w) // 2, (4 * half + w) % 2
                        src = v_f[:, i, 4 * rows_half:4 * rows_half + 4, :].rearrange("p r c -> p (r c)")
                        m2 = pe.do(lambda e: e.transpose(ps2[:, w * P:(w + 1) * P], src, ident[:, :]))
                    dve.wait(m2, m_k[DT - 1])
                    m_v[n] = dve.do(lambda e: e.tensor_copy(vw[:, 4 * half:4 * half + 4, n * P:(n + 1) * P],
                                                            ps2[:, :].rearrange("p (w n) -> p w n", w=4)))
                    bank_free[b] = [m_v[n]]
                vf_free = m2
                return [m1]

            def vc_evac(n, ps, done):
                r = n % 2
                act.wait(done, vcf_free[r])
                m1 = act.do(lambda e: e.activation(vc_f[r][:, :], ps[:, :], ACT.Copy))
                b, ps2 = take_bank()
                pe.wait(m1)
                for j in range(2):
                    for u in range(2):
                        m2 = pe.do(lambda e: e.transpose(ps2[:, (2 * j + u) * P:(2 * j + u + 1) * P],
                                                         vc_f[r][:, u * CTX + j * P:u * CTX + (j + 1) * P], ident[:, :]))
                vcf_free[r] = m2
                dve.wait(m2, *m_x)
                m_vc[n] = dve.do(lambda e: e.tensor_copy(vc[:, :, 2 * n * P:2 * n * P + 2 * P],
                                                         ps2[:, :].rearrange("p (j n) -> p j n", j=2)))
                bank_free[b] = [m_vc[n]]
                return [m1]

            for g in range(2):
                gemm("v2", g, DT, h, v_evac, hc, vc_evac)

            after_v = [(pe.sem, pe.count), m_v[DT - 1], m_vc[3]]
            sp.wait(*after_v)
            land_mask = Landing(sem("mask_landed"))
            m_mask = land_mask.load(sp, mask[:, :, :], A["mask"].rearrange("v p k -> p v k"))
            land_t = [Landing(sem(f"toeplitz_landed{i}")) for i in range(2)]
            toep_free, bias_free = [None, None], [[], []]
            m_toep, m_bias = {}, {}

            def load_toeplitz(hd):
                r = hd % 2
                sp.wait(toep_free[r])
                t = A["rpb_padded"]
                for qr in range(ROWS):
                    src = bass.AP(t.tensor, (hd * (2 * ROWS - 1) + qr) * RPB_W, [[1, CH_COLS], [RPB_W, ROWS], [1, TOEP]])
                    m_toep[hd] = land_t[r].load(sp, toep[r][CH_COLS * qr:CH_COLS * (qr + 1), :, :], src)

            def make_bias(hd):
                r = hd % 2
                for v, off in enumerate((16, 8, 0)):
                    last = TOEP - 1 - off
                    src = toep[r][:, ::-1, last - K_COLS + 1:last + 1][:, :, ::-1]
                    pool.wait(m_toep[hd], m_mask, *bias_free[r], *after_v)
                    m_bias[hd] = pool.do(lambda e: e.tensor_tensor(
                        bias[r][:, v, :].rearrange("p (k b) -> p k b", k=ROWS), src,
                        mask[:, v, :].rearrange("p (k b) -> p k b", k=ROWS), ALU.add))
                toep_free[r] = m_bias[hd]
                bias_free[r] = []

            NB = ROWS * K_COLS
            work = [(hd, i) for hd in range(A_HEADS) for i in range(N_CH)]
            st = {}
            pr_free, prt_free = [None] * 3, [None] * 3
            small_free = [None] * 8
            o_bank, m_o = {}, {}

            def scores(n):
                hd, i = work[n]
                e2, pb, c3, c8 = hd // 2, A_DIM * (hd % 2), n % 3, n % 8
                part = slice(pb, pb + A_DIM)
                b, ps = take_bank()
                qv = q2[e2][part, i * P:(i + 1) * P]
                kv = k2[e2][part, :].rearrange("p (r c) -> p r c", r=ROWS)[:, :, K_START[i]:K_START[i] + K_COLS]
                pe.wait(m_q[e2], m_k[e2], m_kc[e2 // 2])
                pe.quiet(lambda e: e.matmul(ps[:, 0:NB], qv, kv, start=True, stop=True))
                ms = pe.do(lambda e: e.matmul(ps[:, NB:], qv, kc[part, e2, :], start=True, stop=True))
                top, neg = rowmax[:, c8:c8 + 1], rowsum[:, c8:c8 + 1]
                s1, s2 = rowsum[:, 8 + c8:9 + c8], rowsum[:, 16 + c8:17 + c8]
                v = (0, 1, 1, 2)[i]
                dve.wait(ms, small_free[c8])
                m1 = dve.do(lambda e: e.reduce_max(top, ps[:, NB:], AX.X))
                dve.wait(m1, m_bias[hd], pr_free[c3])
                m2 = dve.do(lambda e: e.tensor_tensor_reduce(pr[c3][:, 0:NB], ps[:, 0:NB], bias[hd % 2][:, v, :],
                                                             1.0, top, ALU.add, ALU.max, neg))
                bias_free[hd % 2].append(m2)
                dve.wait(m2)
                m3 = dve.do(lambda e: e.tensor_scalar(neg, neg, -1.0, None, ALU.mult))
                act.wait(m3)
                m4 = act.do(lambda e: e.activation(pr[c3][:, 0:NB], pr[c3][:, 0:NB], ACT.Exp, bias=neg, accum_out=s1))
                m5 = act.do(lambda e: e.activation(pr[c3][:, NB:], ps[:, NB:], ACT.Exp, bias=neg, accum_out=s2))
                bank_free[b] = [m5]
                st[n] = m5

            def normalise(n):
                c3, c8 = n % 3, n % 8
                s1, s2 = rowsum[:, 8 + c8:9 + c8], rowsum[:, 16 + c8:17 + c8]
                dve.wait(st[n])
                m = dve.do(lambda e: e.tensor_tensor(s1, s1, s2, ALU.add))
                dve.wait(m)
                m = dve.do(lambda e: e.reciprocal(s1, s1))
                pool.wait(m)
                st[n] = small_free[c8] = pool.do(lambda e: e.tensor_scalar(pr[c3][:, :], pr[c3][:, :], s1, None, ALU.mult))

            def turn(n):
                c3 = n % 3
                b, ps = take_bank()
                pe.wait(st[n])
                for k in range(4):
                    m = pe.do(lambda e: e.transpose(ps[:, k * P:(k + 1) * P], pr[c3][:, k * P:(k + 1) * P], ident[:, :]))
                pr_free[c3] = m
                act.wait(m, prt_free[c3])
                st[n] = act.do(lambda e: e.activation(prt[c3][:, :], ps[:, :], ACT.Copy))
                bank_free[b] = [st[n]]

            def values(n):
                hd, i = work[n]
                e2, pb, c3 = hd // 2, A_DIM * (hd % 2), n % 3
                part = slice(pb, pb + A_DIM)
                if i == 0:
                    o_bank[hd] = take_bank()
                b, ps = o_bank[hd]
                pe.wait(st[n])
                col = slice(A_DIM * hd, A_DIM * hd + A_DIM)
                for k in range(4):
                    vk = vw[:, 2 * i + k, col] if k < 2 else vc[:, k - 2, col]
                    m = pe.do(lambda e: e.matmul(ps[part, i * P:(i + 1) * P], vk, prt[c3][:, k * P:(k + 1) * P],
                                                 start=k == 0, stop=k == 3))
                prt_free[c3] = m
                if i == N_CH - 1:
                    dve.wait(m)
                    m_o[hd] = dve.do(lambda e: e.tensor_copy(
                        q2[e2][part, :].rearrange("p (r i a) -> p i r a", r=ROWS, i=N_CH),
                        ps[part, :].rearrange("p (i r a) -> p i r a", i=N_CH, r=ROWS)))
                    bank_free[b] = [m_o[hd]]

            load_toeplitz(0)
            load_toeplitz(1)
            make_bias(0)
            for n in range(len(work) + 3):
                if n < len(work):
                    hd, i = work[n]
                    if i == 1 and hd + 1 < A_HEADS:
                        make_bias(hd + 1)
                        if hd + 2 < A_HEADS:
                            load_toeplitz(hd + 2)
                    scores(n)
                if 0 <= n - 1 < len(work):
                    normalise(n - 1)
                if 0 <= n - 2 < len(work):
                    turn(n - 2)
                if 0 <= n - 3 < len(work):
                    values(n - 3)

            m_att = [m_o[A_HEADS - 1], (pe.sem, pe.count)]
            zo = [(at(f"zo_hi{i}", 67 + i, [P, T], F32R), at(f"zo_lo{i}", 75 + i, [P, T], F32R)) for i in range(DT)]
            yb = [at(f"y_b{i}", 83 + i, [P, T]) for i in range(DT)]
            sg = [at(f"sig_g{i}", 51 + i, [P, T]) for i in range(4)]
            z_free, m_zo, m_yb = [None] * 4, {}, {}

            def zb_evac(n, ps, done):
                r = n % 4
                act.wait(done, z_free[r], *m_att)
                m = act.do(lambda e: e.activation(sg[r][:, :], ps[:, :], ACT.Silu))
                dve.wait(m, m_o[2 * n + 1])
                m1 = dve.do(lambda e: e.tensor_tensor(sg[r][:, :], sg[r][:, :], q2[n][:, :], ALU.mult))
                hi, lo = zo[n][0][:, :], zo[n][1][:, :]
                z_free[r] = split(sg[r][:, :], hi, lo, [m1], m_att)
                m_zo[n] = (hi, lo, z_free[r])
                return [m]

            for g in range(2):
                gemm("z_b", g, DT, h, zb_evac)

            def copy_evac(dst, got, n, ps, done):
                act.wait(done, *m_att)
                got[n] = act.do(lambda e: e.activation(dst[n][:, :], ps[:, :], ACT.Copy))
                return [got[n]]

            for g in range(2):
                gemm("w_out_attn", g, DT, m_zo, lambda n, ps, done: copy_evac(yb, m_yb, n, ps, done))

            def gb_evac(n, ps, done):
                r = n % 4
                act.wait(done, z_free[r])
                m = act.do(lambda e: e.activation(sg[r][:, :], ps[:, :], ACT.Sigmoid))
                dve.wait(m, m_yb[n])
                m_yb[n] = z_free[r] = dve.do(lambda e: e.tensor_tensor(yb[n][:, :], yb[n][:, :], sg[r][:, :], ALU.mult))
                return [m]

            for g in range(2):
                gemm("g_b", g, DT, h, gb_evac)

            sz = [at(f"silu_za{i}", 91 + i, [P, T]) for i in range(4)]
            cg = [at(f"c_gate{i}", 95 + i, [P, T]) for i in range(4)]
            up = [at(f"u_pad{i}", 51, [P, T + 2], part=(T + 8) * i) for i in range(4)]
            ac = [at(f"conv3_{i}", 99 + i, [P, T]) for i in range(4)]
            cv = [(at(f"cv_hi{i}", 59 + i, [P, T], F32R), at(f"cv_lo{i}", 67 + i, [P, T], F32R)) for i in range(DT)]
            dve.wait(*z_free, *m_att)
            for i in range(4):
                dve.do(lambda e: e.memset(up[i][:, 0:1], 0.0))
                m_pad = dve.do(lambda e: e.memset(up[i][:, T + 1:T + 2], 0.0))
            sz_m, cg_m, m_cv, ac_free = {}, {}, {}, {}

            def za_evac(n, ps, done):
                act.wait(done, ac_free.get(n - 4), *m_att)
                sz_m[n] = act.do(lambda e: e.activation(sz[n % 4][:, :], ps[:, :], ACT.Silu))
                return [sz_m[n]]

            def bg_evac(n, ps, done):
                dve.wait(done, sz_m[n])
                sz_m[n] = dve.do(lambda e: e.tensor_tensor(sz[n % 4][:, :], sz[n % 4][:, :], ps[:, :], ALU.mult))
                return [sz_m[n]]

            def cg_evac(n, ps, done):
                act.wait(done, ac_free.get(n - 4))
                cg_m[n] = act.do(lambda e: e.activation(cg[n % 4][:, :], ps[:, :], ACT.Copy))
                return [cg_m[n]]

            def xi_evac(n, ps, done):
                r = n % 4
                dve.wait(done, cg_m[n], m_pad, ac_free.get(n - 4))
                m_u = m = dve.do(lambda e: e.tensor_tensor(up[r][:, 1:T + 1], ps[:, :], cg[r][:, :], ALU.mult))
                for k in range(3):
                    w = par2[:, 40 + 8 * k + n:41 + 8 * k + n]
                    dve.wait(m)
                    if k == 0:
                        m = dve.do(lambda e: e.tensor_scalar(ac[r][:, :], up[r][:, 0:T], w, par2[:, 64 + n:65 + n],
                                                             ALU.mult, ALU.add))
                    else:
                        m = dve.do(lambda e: e.scalar_tensor_tensor(ac[r][:, :], up[r][:, k:k + T], w, ac[r][:, :],
                                                                    ALU.mult, ALU.add))
                dve.wait(m, sz_m[n])
                m = dve.do(lambda e: e.tensor_tensor(ac[r][:, :], ac[r][:, :], sz[r][:, :], ALU.mult))
                hi, lo = cv[n][0][:, :], cv[n][1][:, :]
                ac_free[n] = split(ac[r][:, :], hi, lo, [m], [m_yb[DT - 1]])
                m_cv[n] = (hi, lo, ac_free[n])
                return [m_u]

            for half in range(2):
                for key, evac in (("z_a", za_evac), ("b_gate", bg_evac), ("c_gate", cg_evac), ("x_in", xi_evac)):
                    gemm(f"{key}{half}", 0, DT, h, lambda n, ps, done: evac(4 * half + n, ps, done))

            sga = [at(f"sig_ga{i}", 75 + i, [P, T]) for i in range(DT)]
            m_ga, m_mg = {}, {}

            def ga_evac(n, ps, done):
                act.wait(done, m_yb[DT - 1])
                m_ga[n] = act.do(lambda e: e.activation(sga[n][:, :], ps[:, :], ACT.Sigmoid))
                return [m_ga[n]]

            for g in range(2):
                gemm("g_a", g, DT, h, ga_evac)
            h_read = (pe.sem, pe.count)

            def merge_evac(n, ps, done):
                dve.wait(done, m_ga[n])
                m = dve.do(lambda e: e.tensor_tensor(sga[n][:, :], ps[:, :], sga[n][:, :], ALU.mult))
                dve.wait(m, m_yb[n])
                m2 = dve.do(lambda e: e.tensor_tensor(yb[n][:, :], yb[n][:, :], sga[n][:, :], ALU.add))
                hi, lo = h_hi[n][:, :], h_lo[n][:, :]
                m_mg[n] = (hi, lo, split(yb[n][:, :], hi, lo, [m2], [h_read]))
                return [m]

            for g in range(2):
                gemm("w_out_conv", g, DT, m_cv, merge_evac)
            y2 = [at(f"y_second{i}", 51 + i, [P, T]) for i in range(DT)]
            m_y2 = {}
            for g in range(2):
                gemm("w_o", g, DT, m_mg, lambda n, ps, done: copy_evac(y2, m_y2, n, ps, done))
            m_g = gate_columns(g_2o, par2[:, 32:40], mod2[:, 16:24], m_mod["mod2", 0])
            m_r = mean_square(full(y2), m_y2, sq_ring, sq_free, T, 1.0 / D, rstd, None)
            return residual(full(y2), m_y2, g_2o, m_g, rstd, m_r, None, m_x)

        if probe is None or probe >= 1:
            prepare(8)
        if probe is None or probe >= 1:
            m_x = layer(0, m_x)
        if probe is None or probe >= 2:
            m_x = layer(1, m_x)
        if probe is None or probe >= 3:
            m_x = second(m_x)
        m_barrier = m_x

        y_tok = at("y_tok", 35, [P, N_CH, D])
        land_out = Landing(sem("out_landed"))
        for j in range(N_CH):
            for half in range(2):
                i, ps = take_bank()
                for f in range(4):
                    n = 4 * half + f
                    pe.wait(m_x[n])
                    m = pe.do(lambda e, n=n, j=j, f=f, ps=ps: e.transpose(ps[:, f * P:(f + 1) * P],
                                                                          x[n][:, j * P:(j + 1) * P], ident[:, :]))
                q = (dve, act)[half]
                q.wait(m, *m_barrier)
                dst = y_tok[:, j, 512 * half:512 * half + 512]
                if half:
                    m = act.do(lambda e, dst=dst, ps=ps: e.activation(dst, ps[:, :], ACT.Copy))
                else:
                    m = dve.do(lambda e, dst=dst, ps=ps: e.tensor_copy(dst, ps[:, :]))
                bank_free[i] = [m]
                sp.wait(m)
            m_out = land_out.load(sp, out[0, j * P:(j + 1) * P, :], y_tok[:, j, :])
        sp.wait(m_out)
        if land_spill.count:
            sp.wait((land_spill.sem, land_spill.count))


_INS = ["x", "c", "w_ada", "b_ada", "g_pre_mix", "g_post_mix", "g_pre_mlp", "g_post_mlp", "w_in", "w_conv_m",
        "b_conv_m", "w_q", "w_k", "w_v", "w_gates", "b_gates", "g_mh", "w_dw", "b_dw", "g_cn", "b_cn", "w_out",
        "w_ff1", "w_ff2", "c_2", "ctx_2", "c_ctx_2", "w_mod_2", "b_mod_2", "pre_g_2", "post_g_2", "w_in_2",
        "conv_w_2", "conv_b_2", "w_out_conv_2", "w_out_attn_2", "w_o_2"]


def shape_constants():
    tok = np.arange(T)
    half = A_DIM // 2
    inv = np.float32(10000.0) ** (-np.arange(0, half, 2, dtype=np.float32) / np.float32(half))
    ang_r = (tok // GRID).astype(np.float32)[:, None] * inv
    ang_c = (tok % GRID).astype(np.float32)[:, None] * inv
    ang = np.concatenate([ang_r, ang_r, ang_c, ang_c], axis=-1)
    rope = np.stack([np.tile(f(ang).astype(np.float32).T, (P // A_DIM, 1)) for f in (np.cos, np.sin)])
    mask = np.zeros((3, ROWS, CH_COLS, ROWS, K_COLS), np.float32)
    for v, i in enumerate((0, 1, 3)):
        qc = CH_COLS * i + np.arange(CH_COLS)
        kc = K_START[i] + np.arange(K_COLS)
        start = np.clip(qc - WIN // 2, 0, GRID - WIN)[:, None]
        seen = (kc >= start) & (kc < start + WIN)
        mask[v] = np.where(seen, 0.0, NEG)[None, :, None, :]
    return {"rope": rope, "mask": mask.reshape(3, P, ROWS * K_COLS)}


def kernel(**inputs):
    import concourse.bacc as bacc
    from concourse.bass_utils import run_bass_kernel_spmd

    nc = bacc.Bacc("TRN2", target_bir_lowering=False, num_devices=1)
    arrays = {name: np.ascontiguousarray(inputs[name]) for name in _INS}
    rpb = inputs["rpb_2"]
    padded = np.zeros((A_HEADS, 2 * ROWS - 1, RPB_W), rpb.dtype)
    padded[:, :, WIN:WIN + 2 * WIN - 1] = rpb[0][:, ::-1, ::-1]
    arrays["rpb_padded"] = padded
    arrays.update(shape_constants())
    A = {name: nc.dram_tensor(f"in_{name}", a.shape, mybir.dt.from_np(a.dtype), kind="ExternalInput").ap()
         for name, a in arrays.items()}
    out = nc.dram_tensor("x_out", (1, T, D), F32, kind="ExternalOutput").ap()
    build(nc, A, out)
    r = run_bass_kernel_spmd(nc, [{f"in_{name}": a for name, a in arrays.items()}], core_ids=[0])
    return r.results[0]["x_out"]
```

```python
from collections import deque
from contextlib import ExitStack

import numpy as np

import concourse.bass as bass
from concourse import mybir

F32 = mybir.dt.float32
BF16 = mybir.dt.bfloat16
F32R = mybir.dt.float32r
ALU = mybir.AluOpType
ACT = mybir.ActivationFunctionType
AX = mybir.AxisListType

P = 128
D = 1024
T = 512
DT = D // P
DEPTH = 2
HEADS, HEAD_D = 4, 256
CONV_M, CONV_G = 4, 31
FF = 4 * D
QUARTER = FF // 4 // P
EPS = 1e-6
NEG = -1e30

GRID = 64
ROWS = T // GRID
CTX = 256
A_HEADS, A_DIM = 16, 64
WIN = 16
CH_COLS = P // ROWS
N_CH = T // P
K_COLS = 32
K_START = [0, 8, 24, 32]
TOEP = 48
RPB_W = 64
SLOT = 2048


class Queue:

    def __init__(self, engine, sem):
        self.engine, self.sem, self.count, self.seen = engine, sem, 0, {}

    def wait(self, *marks):
        for mark in marks:
            if mark is None:
                continue
            sem, value = mark
            if self.seen.get(sem.name, 0) < value:
                self.seen[sem.name] = value
                self.engine.wait_ge(sem, value)

    def do(self, step):
        self.count += 1
        step(self.engine).then_inc(self.sem, 1)
        return (self.sem, self.count)

    def quiet(self, step):
        step(self.engine)


class Landing:

    def __init__(self, sem):
        self.sem, self.count = sem, 0

    def load(self, queue, dst, src):
        self.count += 16
        queue.engine.dma_start(dst, src).then_inc(self.sem, 16)
        return (self.sem, self.count)


def build(nc, A, out, probe=None):
    ctx = ExitStack()
    with ctx:
        sem = lambda name: ctx.enter_context(nc.semaphore(name))
        base = (nc.sbuf_base + 63) // 64 * 64
        n_arena = (nc.sbuf_usable_end - base) // 32 * 32
        ctx.enter_context(nc.sbuf_tensor("arena", [P, n_arena // 4 - 16], F32))

        def at(name, slot, shape, dtype=F32, part=0):
            return nc.alloc_sbuf_tensor_at(name, shape, dtype, offset=base + int(slot * SLOT) + 4 * part)

        pe, act, dve, pool = Queue(nc.tensor, sem("pe_done")), Queue(nc.scalar, sem("act_done")), \
            Queue(nc.vector, sem("dve_done")), Queue(nc.gpsimd, sem("pool_done"))
        sp = Queue(nc.sync, None)

        psum = [ctx.enter_context(nc.psum_tensor(f"bank{i}", [P, 512], F32)) for i in range(8)]
        bank_turn = [0]
        bank_free = [[] for _ in range(8)]

        def take_bank():
            while bank_free[bank_turn[0] % 8] is None:
                bank_turn[0] += 1
            i = bank_turn[0] % 8
            bank_turn[0] += 1
            pe.wait(*bank_free[i])
            bank_free[i] = None
            return i, psum[i]

        par = [at(f"params{l}", 32 + l, [P, 512]) for l in range(DEPTH)]
        par2 = at("params_second", 34, [P, 128])
        cols = at("columns", 34, [P, 384], part=128)
        ident = at("ident", 103, [P, P])
        ones = at("ones", 103, [P, P], part=128)
        misc = at("misc", 103, [P, 64], part=256)
        ones_bf = at("ones_bf", 103, [P, 2], BF16, part=448)
        eps_col, one_col = misc[:, 0:1], misc[:, 1:2]
        gate_bias = [misc[0:8, 2 + l:3 + l] for l in range(DEPTH)]
        rowmax, rowsum = misc[:, 8:16], misc[:, 16:48]

        c = [0]

        def column(n):
            c[0] += n
            return cols[:, c[0] - n:c[0]]

        mod = [column(48) for _ in range(DEPTH)]
        mod2, mod2c = column(24), column(16)
        s_mix, s_mlp, g_mixo, g_mlpo = ([column(8) for _ in range(DEPTH)] for _ in range(4))
        s_2, s_2c, g_2o = column(8), column(8), column(8)
        cact = column(24)

        m_ones = [pool.do(lambda e: e.memset(ones[:, :], 1.0)),
                  pool.do(lambda e: e.memset(ident[:, :], 0.0)),
                  pool.do(lambda e: e.memset(eps_col, EPS)),
                  pool.do(lambda e: e.memset(one_col, 1.0)),
                  pool.do(lambda e: e.memset(ones_bf[:, :], 1.0))]
        pool.wait(m_ones[1])
        m_ident = pool.do(lambda e: e.affine_select(out=ident[:, :], in_=ident[:, :], compare_op=ALU.not_equal,
                                                    fill=1.0, base=0, pattern=[[-1, P]], channel_multiplier=1))

        stage = at("param_rows", 90, [P, 9, P])
        m_stage = pool.do(lambda e: e.memset(stage[:, :, :], 0.0))
        land_par = Landing(sem("params_landed"))
        sp.wait(m_stage)

        def rows(tile, r, src):
            n = src.shape[0]
            while n:
                k = min(n, P - r)
                a = stage[r:r + k, tile, :]
                land_par.load(sp, a, src[src.shape[0] - n:src.shape[0] - n + k, :])
                n -= k
                r += k
                if r == P:
                    tile, r = tile + 1, 0

        vec = lambda ap: ap.rearrange("(n p) -> n p", p=P)
        tap = lambda ap: ap.rearrange("k (n p) -> (k n) p", p=P)
        rows(8, 0, vec(A["b_mod_2"][0]))
        rows(8, 24, vec(A["pre_g_2"][0]))
        rows(8, 32, vec(A["post_g_2"][0]))
        rows(8, 40, tap(A["conv_w_2"][0]))
        rows(8, 64, vec(A["conv_b_2"][0]))
        rows(8, 72, vec(A["c"][0]))
        rows(8, 80, vec(A["c_2"][0]))
        rows(8, 88, vec(A["c_ctx_2"]))
        B_ADA, G_PRE_MIX, G_POST_MIX, G_PRE_MLP, G_POST_MLP, B_CONV_M, G_MH, B_DW, G_CN, B_CN = \
            0, 48, 56, 64, 72, 80, 88, 96, 104, 112
        W_CONV_M, W_DW = 128, 160
        for l in range(DEPTH):
            rows(4 * l, B_ADA, vec(A["b_ada"][l]))
            for r, n in ((G_PRE_MIX, "g_pre_mix"), (G_POST_MIX, "g_post_mix"), (G_PRE_MLP, "g_pre_mlp"),
                         (G_POST_MLP, "g_post_mlp"), (B_CONV_M, "b_conv_m"), (G_MH, "g_mh"), (B_DW, "b_dw"),
                         (G_CN, "g_cn"), (B_CN, "b_cn")):
                rows(4 * l, r, vec(A[n][l]))
            rows(4 * l + 1, 0, tap(A["w_conv_m"][l]))
            rows(4 * l + 1, 32, tap(A["w_dw"][l]))
        for l in range(DEPTH):
            land_par.load(sp, gate_bias[l], A["b_gates"][l].rearrange("(g o) -> g o", o=1))
        m_par = (land_par.sem, land_par.count)

        x_all = at("x_all", 24, [P, DT, T])
        x = [x_all[:, i, :] for i in range(DT)]
        x_tok = at("x_tok", 80, [P, N_CH, D])
        land_x = Landing(sem("x_landed"))
        m_xt = land_x.load(sp, x_tok[:, :, :], A["x"][0].rearrange("(j p) n -> p j n", p=P))

        def to_columns(tiles, dst_of, marks):
            i, ps = take_bank()
            for n, t in enumerate(tiles):
                pe.wait(*marks)
                m = pe.do(lambda e, n=n, t=t: e.transpose(ps[:, n * P:(n + 1) * P], stage[:, t, :], ident[:, :]))
            dve.wait(m)
            m = dve.do(lambda e: e.tensor_copy(dst_of, ps[:, 0:len(tiles) * P]))
            bank_free[i] = [m]
            return m

        m_par2 = to_columns([8], par2[:, :], [m_par, m_ident])
        m_parl = [to_columns(range(4 * l, 4 * l + 4), par[l][:, :], [m_par, m_ident]) for l in range(DEPTH)]
        act.wait(m_par2)
        m_cact = act.do(lambda e: e.activation(cact, par2[:, 72:96], ACT.Silu))

        def transpose_in(src_of, dst_of, n_feat, n_chunk, marks, extra=()):
            done = []
            for f in range(n_feat):
                i, ps = take_bank()
                for j in range(n_chunk):
                    pe.wait(*marks)
                    m = pe.do(lambda e, f=f, j=j: e.transpose(ps[:, j * P:(j + 1) * P], src_of(f, j), ident[:, :]))
                q = (dve, act)[f % 2]
                q.wait(m, *extra)
                if f % 2:
                    m = act.do(lambda e, f=f, ps=ps: e.activation(dst_of(f), ps[:, 0:n_chunk * P], ACT.Copy))
                else:
                    m = dve.do(lambda e, f=f, ps=ps: e.tensor_copy(dst_of(f), ps[:, 0:n_chunk * P]))
                bank_free[i] = [m]
                done.append(m)
            return done

        m_x = transpose_in(lambda f, j: x_tok[:, j, f * P:(f + 1) * P], lambda f: x[f][:, :], DT, N_CH,
                           [m_xt, m_ident])

        RAW, HL, PIECE = 4, 2, 1024
        raw = [at(f"w_raw{i}", 2 * i, [P, PIECE]) for i in range(RAW)]
        w_hi = [at(f"w_hi{i}", 8 + 4 * i, [P, 2048], F32R) for i in range(HL)]
        w_lo = [at(f"w_lo{i}", 16 + 4 * i, [P, 2048], F32R) for i in range(HL)]
        land_w = [Landing(sem(f"w_landed{i}")) for i in range(RAW)]
        plan = []

        def block(key, src, is_split):
            src = src.rearrange("(k p) n -> p k n", p=P)
            plan_pieces = [[(0, PIECE, src[:, k:k + 2, :])] for k in (0, 2)]
            return (key, plan_pieces, is_split)

        def plan_gemm(key, w, row0, kt, col0, groups, interleave=()):
            interleave = deque(interleave)
            for g in range(groups):
                for kh in range(kt // 4):
                    src = w[row0 + kh * 512:row0 + kh * 512 + 512, col0 + g * 512:col0 + g * 512 + 512]
                    plan.append(block((key, g, kh), src, True))
                    if interleave:
                        plan.append(interleave.popleft())
            plan.extend(interleave)

        def gemv_blocks(key, w, g0, g1):
            return [block((key, g, kh), w[kh * 512:kh * 512 + 512, g * 512:g * 512 + 512], False)
                    for g in range(g0, g1) for kh in range(2)]

        plan += gemv_blocks("ada0", A["w_ada"][0], 0, 4)
        GLU_B, GLU_A, X_M, Z = 3072, 2048, 0, 1024
        for l in range(DEPTH):
            rest = deque(gemv_blocks("ada0", A["w_ada"][0], 4, 12) if l == 0 else [])
            take = lambda n: [rest.popleft() for _ in range(min(n, len(rest)))]
            for half in range(2):
                plan_gemm(f"glu_b{l}{half}", A["w_in"][l], 0, DT, GLU_B + 512 * half, 1, take(2))
                plan_gemm(f"glu_a{l}{half}", A["w_in"][l], 0, DT, GLU_A + 512 * half, 1, take(2))
            for half in range(2):
                plan_gemm(f"x_m{l}{half}", A["w_in"][l], 0, DT, X_M + 512 * half, 1, take(2))
                plan_gemm(f"z{l}{half}", A["w_in"][l], 0, DT, Z + 512 * half, 1, take(2))
                for h in (2 * half, 2 * half + 1):
                    wq, wk, wv = (A[w][l, h].rearrange("(k p) n -> p k n", p=P) for w in ("w_q", "w_k", "w_v"))
                    plan.append(((f"qkv{l}", h, 0), [[(0, 512, wq), (512, 512, wk)], [(0, 512, wv)]], True))
            plan_gemm(f"w_out{l}", A["w_out"][l], 0, 2 * DT, 0, 2)
            nxt = gemv_blocks("ada1", A["w_ada"][1], 0, 12) if l == 0 else gemv_blocks("mod2", A["w_mod_2"][0], 0, 6)
            nxt = deque(nxt)
            take = lambda n: [nxt.popleft() for _ in range(min(n, len(nxt)))]
            for step in ("up0", "up1", "down0", "up2", "down1", "up3", "down2", "down3"):
                q = int(step[-1])
                if step[:2] == "up":
                    plan_gemm(f"{step}_{l}", A["w_ff1"][l], 0, DT, q * 1024, 2, take(4))
                else:
                    plan_gemm(f"{step}_{l}", A["w_ff2"][l], q * 1024, DT, 0, 2, take(4))
        w2 = A["w_in_2"][0]
        for key, col in (("q2", 4096), ("k2", 5120), ("v2", 6144), ("g_b", 9216), ("z_b", 7168)):
            plan_gemm(key, w2, 0, DT, col, 2)
        plan_gemm("w_out_attn", A["w_out_attn_2"][0], 0, DT, 0, 2)
        for half in range(2):
            for key, col in (("z_a", 3072), ("b_gate", 0), ("c_gate", 1024), ("x_in", 2048)):
                plan_gemm(f"{key}{half}", w2, 0, DT, col + 512 * half, 1)
        plan_gemm("g_a", w2, 0, DT, 8192, 2)
        plan_gemm("w_out_conv", A["w_out_conv_2"][0], 0, DT, 0, 2)
        plan_gemm("w_o", A["w_o_2"][0], 0, DT, 0, 2)

        raw_free = [None] * RAW
        hl_free = [None] * HL
        ready = {}
        nxt_prep, split_count = [0], [0]
        all_pieces = [piece for _, pieces, _ in plan for piece in pieces]
        landed = []

        def issue_loads(limit):
            while len(landed) < min(limit, len(all_pieces)):
                s = len(landed) % RAW
                sp.wait(raw_free[s])
                for off, size, src in all_pieces[len(landed)]:
                    dst = raw[s][:, off:off + size].rearrange("p (k n) -> p k n", k=src.shape[1])
                    mark = land_w[s].load(sp, dst, src)
                landed.append(mark)

        taken = [0]

        def prepare(limit):
            while nxt_prep[0] < min(limit, len(plan)):
                key, pieces, is_split = plan[nxt_prep[0]]
                if is_split:
                    t = split_count[0] % HL
                    split_count[0] += 1
                for n, piece in enumerate(pieces):
                    issue_loads(taken[0] + RAW)
                    s, here = taken[0] % RAW, landed[taken[0]]
                    size = sum(p[1] for p in piece)
                    if is_split:
                        part = slice(PIECE * n, PIECE * n + size)
                        act.wait(here, hl_free[t])
                        m = act.do(lambda e: e.activation(w_hi[t][:, part], raw[s][:, 0:size], ACT.Copy))
                        pool.wait(here, m)
                        m = pool.do(lambda e: e.tensor_tensor(w_lo[t][:, part], raw[s][:, 0:size],
                                                              w_hi[t][:, part].bitcast(F32), ALU.subtract))
                        raw_free[s] = m
                        ready[key] = (t, m)
                    else:
                        raw_free[s] = consume_gemv(key, n, raw[s], here)
                    taken[0] += 1
                issue_loads(taken[0] + RAW)
                nxt_prep[0] += 1

        def prefetch():
            while nxt_prep[0] < len(plan) and sum(is_split for _, _, is_split in plan[nxt_prep[0]:nxt_prep[0] + 1]) \
                    and len(ready) < HL:
                prepare(nxt_prep[0] + 1)

        gemv_acc = [at("gemv_acc", 102, [P, 512]), at("gemv_acc_ctx", 83, [P, 512])]
        gemv_part = [at(f"gemv_part{i}", 100, [P, 512], BF16, part=256 * i) for i in range(3)]
        gemv_last = {0: None, 1: None}
        gemv_free = {0: None, 1: None}
        part_free = [None]
        TARGETS = {"ada0": [(0, 0, mod[0], 48)], "ada1": [(0, 0, mod[1], 48)],
                   "mod2": [(0, 1, mod2, 24), (1, 2, mod2c, 16)]}
        m_mod = {}
        gemv_tail, gemv_cut = [], []

        def consume_gemv(key, piece, w, m_landed):
            name, g, kh = key
            if kh == 0 and piece == 0:
                cut_gemv()
            targets = [t for t in TARGETS[name] if 4 * g < t[3]]
            for a, which, dst, _ in targets:
                acc = gemv_acc[a]
                for k in range(2):
                    n = 4 * kh + 2 * piece + k
                    ck, wk = cact[:, 8 * which + n:8 * which + n + 1], w[:, 512 * k:512 * k + 512]
                    if n == 0:
                        dve.wait(m_landed, m_cact, gemv_free[a])
                        gemv_last[a] = dve.do(lambda e: e.tensor_scalar(acc[:, :], wk, ck, None, ALU.mult))
                    else:
                        dve.wait(m_landed, gemv_last[a])
                        gemv_last[a] = dve.do(lambda e: e.scalar_tensor_tensor(acc[:, :], wk, ck, acc[:, :],
                                                                               ALU.mult, ALU.add))
            if kh == 1 and piece == 1:
                gemv_tail.extend((name, a, g, dst, gemv_last[a]) for a, _, dst, _ in targets)
                if len(targets) == 1:
                    cut_gemv()
            return (dve.sem, dve.count)

        def cut_gemv():
            while gemv_tail:
                sum_gemv()
                name, a, g, dst, m = gemv_tail.pop(0)
                acc = gemv_acc[a][:, :]
                dve.wait(m, part_free[0])
                for n in range(3):
                    m = dve.do(lambda e: e.tensor_copy(gemv_part[n][:, :], acc))
                    dve.wait(m)
                    if n < 2:
                        m = dve.do(lambda e: e.tensor_tensor(acc, acc, gemv_part[n][:, :], ALU.subtract))
                        dve.wait(m)
                gemv_free[a] = m
                gemv_cut.append((name, a, g, dst, m))

        def sum_gemv():
            while gemv_cut:
                name, a, g, dst, m_part = gemv_cut.pop(0)
                i, ps = take_bank()
                pe.wait(m_part, *m_ones)
                for n in range(4):
                    for k in range(3):
                        step = lambda e: e.matmul(ps[:, n:n + 1], gemv_part[k][:, n * P:(n + 1) * P],
                                                  ones_bf[:, 0:1], start=k == 0, stop=k == 2)
                        if n < 3 or k < 2:
                            pe.quiet(step)
                part_free[0] = m = pe.do(step)
                bias = par2[:, 4 * g:4 * g + 4] if name == "mod2" else par[int(name[-1])][:, 4 * g:4 * g + 4]
                dve.wait(m, m_par2, *m_parl)
                m = dve.do(lambda e: e.tensor_tensor(dst[:, 4 * g:4 * g + 4], ps[:, 0:4], bias, ALU.add))
                bank_free[i] = [m]
                m_mod[name, a] = m

        def flush_gemv():
            cut_gemv()
            sum_gemv()

        fill, later = deque(), deque()

        def pump(n):
            for _ in range(min(n, len(fill))):
                fill.popleft()()
            if later:
                later.popleft()()

        def products(ps_ap, whi, wlo, xhi, xlo, first, last, mark, shared=False):
            seq = [(wlo, xhi), (whi, xlo), (whi, xhi)]
            for n, (a, b) in enumerate(seq):
                step = lambda e, a=a, b=b, n=n: e.matmul(ps_ap, a, b, start=first and n == 0,
                                                         stop=last and n == 2, skip_group_check=shared)
                if mark and n == 2:
                    return pe.do(step)
                pe.quiet(step)

        def gemm_steps(key, group, kt, rhs, evac, second=None, evac2=None, fills=3):
            banks = [take_bank() for _ in range(4)]
            banks2 = [take_bank() for _ in range(2)] if second else []
            n_kh = kt // 4
            for kh in range(n_kh):
                while (key, group, kh) not in ready:
                    prepare(nxt_prep[0] + 1)
                t, m_w = ready.pop((key, group, kh))
                while nxt_prep[0] < len(plan) and not ready:
                    prepare(nxt_prep[0] + 1)
                pe.wait(m_w)
                for m in range(4):
                    for k in range(4):
                        hi, lo, mark = rhs[4 * kh + k]
                        pe.wait(mark)
                        c0 = 512 * k + P * m
                        last = kh == n_kh - 1 and k == 3
                        done = products(banks[m][1][:, 0:hi.shape[1]], w_hi[t][:, c0:c0 + P], w_lo[t][:, c0:c0 + P],
                                        hi, lo, kh == 0 and k == 0, last, k == 3)
                        if last:
                            banks[m] += (done,)
                        yield
                    if second:
                        ps2 = banks2[m // 2][1][:, (m % 2) * CTX:(m % 2 + 1) * CTX]
                        for k in range(4):
                            hi, lo, mark = second[4 * kh + k]
                            pe.wait(mark)
                            c0 = 512 * k + P * m
                            last = kh == n_kh - 1 and k == 3
                            done = products(ps2, w_hi[t][:, c0:c0 + P], w_lo[t][:, c0:c0 + P], hi, lo,
                                            kh == 0 and k == 0 and m % 2 == 0, last, k == 3, True)
                        if last:
                            banks2[m // 2] += (done,)
                    if m == 3:
                        sum_gemv()
                    if kh == n_kh - 1 and m:
                        i, ps, ready_mark = banks[m - 1]
                        bank_free[i] = evac(4 * group + m - 1, ps, ready_mark)
                    pump(fills)
                hl_free[t] = done
            i, ps, ready_mark = banks[3]
            bank_free[i] = evac(4 * group + 3, ps, ready_mark)
            for m, b in enumerate(banks2):
                bank_free[b[0]] = evac2(2 * group + m, b[1], b[3])

        def gemm(*args, **more):
            for _ in gemm_steps(*args, **more):
                pass

        y = [at(f"y{i}", 84 + i, [P, T]) for i in range(DT)]
        tmpf = [at(f"tmp{i}", 92 + i, [P, T]) for i in range(8)]
        sq_ring = [tmpf[0][:, :], tmpf[1][:, :]]
        sq_free = [None, None]
        rstd = tmpf[2][:, :]
        mod_tmp = [t[:, :] for t in tmpf[3:7]]
        def mean_square(tiles, marks, sq_ring, sq_free, n_tok, scale, rstd, rstd_free, ones_w=None, pre=None):
            prefetch()
            act.quiet(lambda e: e.preload_act_table_set("natural_log_exp_and_others"))
            i, ps = take_bank()
            for n, tl in enumerate(tiles):
                r = n % len(sq_ring)
                act.wait(*([marks[n]] if not isinstance(marks[n], list) else marks[n]), sq_free[r])
                m = act.do(lambda e, tl=tl, r=r: e.activation(sq_ring[r], tl, ACT.Square))
                pe.wait(m, m_ones[0])
                sq_free[r] = pe.do(lambda e, r=r, n=n: e.matmul(ps[:, 0:n_tok], ones[:, :], sq_ring[r],
                                                                start=n == 0, stop=n == len(tiles) - 1))
            act.wait(sq_free[r], rstd_free, *m_ones)
            m = act.do(lambda e: e.activation(rstd, ps[:, 0:n_tok], ACT.Ln, bias=eps_col, scale=scale))
            bank_free[i] = [m]
            act.wait(m)
            return act.do(lambda e: e.activation(rstd, rstd, ACT.Exp, scale=-0.5))

        ssum = tmpf[7][:, :]

        def add_square(n, tile, mark, war):
            r = n % 2
            act.wait(mark, sq_free[r], *war)
            m = act.do(lambda e: e.activation(sq_ring[r], tile, ACT.Square))
            pool.wait(m, *war)
            if n == 0:
                sq_free[r] = pool.do(lambda e: e.tensor_copy(ssum, sq_ring[r]))
            else:
                pool.wait(sq_free[(n - 1) % 2])
                sq_free[r] = pool.do(lambda e: e.tensor_tensor(ssum, ssum, sq_ring[r], ALU.add))
            return sq_free[r]

        def finish_square(m_sum, scale):
            act.quiet(lambda e: e.preload_act_table_set("natural_log_exp_and_others"))
            i, ps = take_bank()
            pe.wait(m_sum)
            m = pe.do(lambda e: e.matmul(ps[:, :], ones[:, :], ssum, start=True, stop=True))
            act.wait(m, *m_ones)
            m = act.do(lambda e: e.activation(rstd, ps[:, :], ACT.Ln, bias=eps_col, scale=scale))
            bank_free[i] = [m]
            act.wait(m)
            m = act.do(lambda e: e.activation(rstd, rstd, ACT.Exp, scale=-0.5))
            prefetch()
            return m

        def modulate(tiles, marks, rstd, m_rstd, s, sh, m_s, tmp, tmp_free, hi, lo, war):
            got = []
            for n, tl in enumerate(tiles):
                r = n % len(tmp)
                dve.wait(marks[n], m_rstd, m_s, tmp_free[r])
                m1 = dve.do(lambda e, tl=tl, r=r, n=n: e.scalar_tensor_tensor(tmp[r], tl, s[:, n:n + 1], rstd,
                                                                              ALU.mult, ALU.mult))
                act.wait(m1, *war)
                m2 = act.do(lambda e, r=r, n=n: e.activation(hi[n], tmp[r], ACT.Identity, bias=sh[:, n:n + 1]))
                got.append((m2, r, n))
                if n >= 1:
                    got[n - 1] = lo_part(got[n - 1], tmp, sh, hi, lo, tmp_free, war)
            got[-1] = lo_part(got[-1], tmp, sh, hi, lo, tmp_free, war)
            return got

        def lo_part(g, tmp, sh, hi, lo, tmp_free, war):
            m2, r, n = g
            dve.wait(m2, *war)
            m3 = dve.do(lambda e: e.scalar_tensor_tensor(lo[n], tmp[r], sh[:, n:n + 1], hi[n].bitcast(F32),
                                                         ALU.add, ALU.subtract))
            tmp_free[r] = m3
            return (hi[n], lo[n], m3)

        def scale_columns(dst, g, sc, mark):
            dve.wait(mark)
            m = dve.do(lambda e: e.tensor_scalar(dst, sc, 1.0, None, ALU.add))
            dve.wait(m)
            return dve.do(lambda e: e.tensor_tensor(dst, dst, g, ALU.mult))

        def gate_columns(dst, g, gt, mark):
            dve.wait(mark)
            return dve.do(lambda e: e.tensor_tensor(dst, gt, g, ALU.mult))

        def split(src, hi, lo, marks, war=()):
            act.wait(*marks, *war)
            m = act.do(lambda e: e.activation(hi, src, ACT.Copy))
            dve.wait(m, *marks, *war)
            m2 = dve.do(lambda e: e.tensor_tensor(lo, src, hi.bitcast(F32), ALU.subtract))
            return m2

        x_spill = nc.dram_tensor("x_spill", (D, T), F32, kind="Internal").ap().rearrange("(n p) t -> p n t", p=P)
        land_spill, land_back = Landing(sem("x_spilled")), Landing(sem("x_back"))

        def now():
            return [(q.sem, q.count) for q in (pe, act, dve, pool) if q.count]


        def residual(tiles, marks, g, m_g, rstd, m_rstd, x_old, x_marks):
            res, prod = [], []
            for n in range(DT):
                dve.wait(marks[n], m_rstd, m_g)
                prod.append(dve.do(lambda e, n=n: e.scalar_tensor_tensor(tiles[n], tiles[n], g[:, n:n + 1], rstd,
                                                                         ALU.mult, ALU.mult)))
                if n >= 1:
                    k = n - 1
                    dve.wait(prod[k], x_marks[k])
                    res.append(dve.do(lambda e, k=k: e.tensor_tensor(x[k], x_old[k], tiles[k], ALU.add)))
            dve.wait(prod[-1], x_marks[-1])
            res.append(dve.do(lambda e: e.tensor_tensor(x[DT - 1], x_old[DT - 1], tiles[DT - 1], ALU.add)))
            return res

        h_hi = [at(f"h_hi{i}", 35 + i, [P, T], F32R) for i in range(DT)]
        h_lo = [at(f"h_lo{i}", 43 + i, [P, T], F32R) for i in range(DT)]
        x_ap = [t[:, :] for t in x]
        y_ap = [t[:, :] for t in y]
        full = lambda tiles: [t[:, :] for t in tiles]

        a_pad = [at(f"a_pad{i}", 51, [P, CONV_G - 1 + T], part=(CONV_G + 1 + T) * i) for i in range(DT)]
        conv_acc = [at(f"conv_acc{i}", 24 + i, [P, T]) for i in range(DT)]
        sig_b = [at(f"sig_b{i}", 88 + i, [P, T]) for i in range(4)]
        xm = [(at(f"xm_hi{i}", 60 + i, [P, T], F32R), at(f"xm_lo{i}", 64 + i, [P, T], F32R)) for i in range(4)]
        xc = [(at(f"xc_hi{i}", 68 + i, [P, T], F32R), at(f"xc_lo{i}", 72 + i, [P, T], F32R)) for i in range(4)]
        x_f = [at(f"x_m_f{i}", 96 + i, [P, T]) for i in range(3)]
        acc4 = [at(f"acc4_{i}", 92 + i, [P, T]) for i in range(4)]
        sig_z = [at(f"sig_z{i}", 88 + i, [P, T]) for i in range(DT)]
        q_slot = lambda h, m: (76 if h < 2 else 35) + 2 * (h % 2) + m
        qkv = {(s, h, m): at(f"{'qkv'[s]}{h}{m}", q_slot(h, m) + 4 * s, [P, T])
               for s in range(3) for h in range(HEADS) for m in range(2)}
        hm_hi = [at(f"hm_hi{n}", q_slot(n // 2, n % 2) + 4, [P, T], F32R) for n in range(DT)]
        hm_lo = [at(f"hm_lo{n}", q_slot(n // 2, n % 2), [P, T], F32R) for n in range(DT)]
        wg = at("w_gates_sb", 59, [P, 6, 32], part=256)
        a_hi = [at(f"a_hi{i}", 51, [P, T], F32R, part=(CONV_G + 1 + T) * i) for i in range(DT)]
        a_lo = [at(f"a_lo{i}", 24 + i, [P, T], F32R) for i in range(DT)]
        a_sq = [at(f"a_sq{i}", 60 + i, [P, T]) for i in range(2)]
        a_rstd = [at(f"a_rstd{i}", 62 + i, [P, T]) for i in range(2)]
        x_old = at("x_old", 60, [P, DT, T])
        g8 = at("gates", 75, [8, T])
        row_t, row_lf, row_ones = (at(n, s, [4, T]) for n, s in (("row_t", 96), ("row_lf", 97), ("row_ones", 98)))
        row_negm, row_em = at("row_negm", 99, [4, T]), at("row_em", 100, [4, T])
        row_b, row_c = at("row_b", 101, [4, T]), at("row_c", 102, [4, T])
        c_col = misc[:, 48:64]
        v_t2 = [at(f"v_t{i}", 47 + 2 * i, [P, N_CH, HEAD_D]) for i in range(2)]
        pt2 = [[at(f"p_t{i}{j}", (96, 66)[i], [P, T - P * j], part=sum(T - P * n for n in range(j)))
                for j in range(N_CH)] for i in range(2)]
        negm_bc, diag = at("negm_bc", 101, [P, T]), at("diag", 102, [P, T])
        den2 = [at(f"den{i}", 70 + i, [P, T]) for i in range(2)]
        hm_sq2 = [[at(f"hm_sq{i}{m}", (72, 64)[i] + m, [P, T]) for m in range(2)] for i in range(2)]
        hm_rstd2 = [at(f"hm_rstd{i}", (74, 69)[i], [P, T]) for i in range(2)]
        land_wg = Landing(sem("w_gates_landed"))

        f1 = [[(at(f"f1_hi{b}{i}", 51 + 16 * b + i, [P, T], F32R), at(f"f1_lo{b}{i}", 59 + 16 * b + i, [P, T], F32R))
               for i in range(QUARTER)] for b in range(2)]

        def finish_conv(p, i, m_acc, ring_free, out):
            acc, r = conv_acc[i][:, :], i % 2
            b, ps = take_bank()
            pe.wait(m_acc[i], m_ones[0])
            m = pe.do(lambda e: e.matmul(ps[:, :], ones[:, :], acc, start=True, stop=True))
            dve.wait(m)
            m = dve.do(lambda e: e.scalar_tensor_tensor(acc, ps[:, :], -1.0 / P, acc, ALU.mult, ALU.add))
            bank_free[b] = [m]
            act.wait(m, ring_free[r])
            m = act.do(lambda e: e.activation(a_sq[r][:, :], acc, ACT.Square))
            yield
            b, ps2 = take_bank()
            pe.wait(m)
            m = pe.do(lambda e: e.matmul(ps2[:, :], ones[:, :], a_sq[r][:, :], start=True, stop=True))
            act.wait(m)
            m = act.do(lambda e: e.activation(a_rstd[r][:, :], ps2[:, :], ACT.Ln, bias=eps_col, scale=1.0 / P))
            bank_free[b] = [m]
            act.wait(m)
            m = act.do(lambda e: e.activation(a_rstd[r][:, :], a_rstd[r][:, :], ACT.Exp, scale=-0.5))
            dve.wait(m)
            m = dve.do(lambda e: e.scalar_tensor_tensor(acc, acc, p[:, G_CN + i:G_CN + i + 1], a_rstd[r][:, :],
                                                        ALU.mult, ALU.mult))
            ring_free[r] = out[i] = m

        def weave(queues):
            running = [[] for _ in queues]
            while any(running) or any(waiting for _, waiting in queues):
                for n, (limit, waiting) in enumerate(queues):
                    while waiting and len(running[n]) < limit and waiting[0][0]():
                        running[n].append(waiting.popleft()[1])
                    for g in list(running[n]):
                        try:
                            next(g)
                        except StopIteration:
                            running[n].remove(g)
                    pump(4)

        def layer(l, m_x):
            p = par[l]
            flush_gemv()
            m_s = scale_columns(s_mix[l], p[:, G_PRE_MIX:G_PRE_MIX + 8], mod[l][:, 8:16], m_mod[f"ada{l}", 0])
            act.wait(*m_x)
            m_spill = land_spill.load(act, x_spill, x_all[:, :, :])
            m_wg = land_wg.load(act, wg[:, :, :],
                                A["w_gates"][l].rearrange("(n p h) g -> p n (h g)", p=P, h=HEADS))
            m_r = mean_square(x_ap, m_x, sq_ring, sq_free, T, 1.0 / D, rstd, None)
            tmp_free = [None] * 4
            h = modulate(x_ap, m_x, rstd, m_r, s_mix[l], mod[l][:, 0:8], m_s, mod_tmp, tmp_free,
                         full(h_hi), full(h_lo), m_x)

            dve.wait(*m_x)
            for i in range(DT):
                m_pad = dve.do(lambda e, i=i: e.memset(a_pad[i][:, 0:CONV_G - 1], 0.0))
            m_a, m_acc = {}, {}
            sig = {}

            def conv_taps(queue, tiles):
                def tap_of(i, k):
                    w = p[:, W_DW + 8 * k + i:W_DW + 8 * k + i + 1]
                    src, acc = a_pad[i][:, k:k + T], conv_acc[i][:, :]
                    if k == 0:
                        queue.wait(m_a[i], m_pad, m_spill, h[-1][2], *m_parl)
                        m_acc[i] = queue.do(lambda e: e.tensor_scalar(acc, src, w, p[:, B_DW + i:B_DW + i + 1],
                                                                      ALU.mult, ALU.add))
                    else:
                        queue.wait(m_acc[i])
                        m_acc[i] = queue.do(lambda e: e.scalar_tensor_tensor(acc, src, w, acc, ALU.mult, ALU.add))
                return [lambda i=i, k=k: tap_of(i, k) for k in range(CONV_G) for i in tiles]

            def glu_b_evac(n, ps, done):
                act.wait(done, m_a.get(n - 4))
                sig[n] = act.do(lambda e: e.activation(sig_b[n % 4][:, :], ps[:, :], ACT.Sigmoid))
                return [sig[n]]

            def glu_a_evac(n, ps, done):
                dve.wait(done, sig[n], m_pad)
                m_a[n] = dve.do(lambda e: e.tensor_tensor(a_pad[n][:, CONV_G - 1:], ps[:, :], sig_b[n % 4][:, :],
                                                          ALU.mult))
                return [m_a[n]]

            for half in range(2):
                gemm(f"glu_b{l}{half}", 0, DT, h, lambda n, ps, done: glu_b_evac(4 * half + n, ps, done))
                gemm(f"glu_a{l}{half}", 0, DT, h, lambda n, ps, done: glu_a_evac(4 * half + n, ps, done))
                for i in (4 * half, 4 * half + 2):
                    fill.extend(conv_taps(dve, (i, i + 1)))

            m_xm, m_xc, m_qkv = [None] * 4, [None] * 4, {}
            xf_free, xc_done = [None] * 3, {}
            dve.wait(h[-1][2])

            def x_m_evac(n, ps, done, war):
                j, r = n % 4, n % 3
                hi, lo, xf, acc = xm[j][0][:, :], xm[j][1][:, :], x_f[r][:, :], acc4[j][:, :]
                act.wait(done, xf_free[r], *war)
                m_hi = act.do(lambda e: e.activation(hi, ps[:, :], ACT.Copy))
                m_f = act.do(lambda e: e.activation(xf, ps[:, :], ACT.Copy))
                dve.wait(m_f, xc_done.get(n - 4))
                for k in range(CONV_M - 1, -1, -1):
                    w = p[:, W_CONV_M + 8 * k + n:W_CONV_M + 8 * k + n + 1]
                    back = CONV_M - 1 - k
                    if back == 0:
                        m = dve.do(lambda e: e.tensor_scalar(acc, xf, w, None, ALU.mult))
                        dve.wait(m_hi, *war)
                        m_xm[j] = dve.do(lambda e: e.tensor_tensor(lo, xf, hi.bitcast(F32), ALU.subtract))
                    else:
                        dve.wait(m)
                        m = dve.do(lambda e: e.scalar_tensor_tensor(acc[:, back:], xf[:, 0:T - back], w,
                                                                    acc[:, back:], ALU.mult, ALU.add))
                xf_free[r] = m

                def activate():
                    act.wait(m)
                    m2 = act.do(lambda e: e.activation(acc, acc, ACT.Silu, bias=p[:, B_CONV_M + n:B_CONV_M + n + 1]))
                    m_xc[j] = xc_done[n] = split(acc, xc[j][0][:, :], xc[j][1][:, :], [m2], war)

                later.append(activate)
                return [m_f]

            m_z = {}

            def z_evac(n, ps, done):
                act.wait(done, m_a[7], xc_done[n] if n >= 4 else None)
                m_z[n] = act.do(lambda e: e.activation(sig_z[n][:, :], ps[:, :], ACT.Sigmoid))
                return [m_z[n]]

            war = []
            for half in range(2):
                gemm(f"x_m{l}{half}", 0, DT, h, lambda n, ps, done: x_m_evac(4 * half + n, ps, done, war))
                gemm(f"z{l}{half}", 0, DT, h, lambda n, ps, done: z_evac(4 * half + n, ps, done))
                for head in (2 * half, 2 * half + 1):
                    while (f"qkv{l}", head, 0) not in ready:
                        prepare(nxt_prep[0] + 1)
                    t, m_w = ready.pop((f"qkv{l}", head, 0))
                    while nxt_prep[0] < len(plan) and not ready:
                        prepare(nxt_prep[0] + 1)
                    pe.wait(m_w)
                    for s in range(3):
                        src, marks = (xm, m_xm) if s == 2 else (xc, m_xc)
                        for m in range(2):
                            b, ps = take_bank()
                            for k in range(2):
                                j = 2 * (head % 2) + k
                                pe.wait(marks[j])
                                c0 = 512 * s + 256 * k + P * m
                                done = products(ps[:, :], w_hi[t][:, c0:c0 + P], w_lo[t][:, c0:c0 + P],
                                                src[j][0][:, :], src[j][1][:, :], k == 0, k == 1, k == 1)
                            dst = qkv[s, head, m][:, :]
                            if m:
                                act.wait(done)
                                mk = act.do(lambda e, dst=dst, ps=ps: e.activation(dst, ps[:, :], ACT.Copy))
                            else:
                                dve.wait(done)
                                mk = dve.do(lambda e, dst=dst, ps=ps: e.tensor_copy(dst, ps[:, :]))
                            bank_free[b] = [mk]
                            m_qkv[s, head, m] = mk
                    hl_free[t] = done
                    pump(6)
                war = [done]

            b, ps = take_bank()
            first = True
            for s in range(3):
                for m in range(2):
                    for head in range(HEADS):
                        pe.wait(m_qkv[s, head, m], m_wg)
                        step = lambda e, s=s, m=m, head=head, st=first: e.matmul(
                            ps[0:8, :], wg[:, 2 * s + m, 8 * head:8 * head + 8], qkv[s, head, m][:, :],
                            start=st, stop=(s, m, head) == (2, 1, HEADS - 1))
                        first = False
                        if (s, m, head) == (2, 1, HEADS - 1):
                            done = pe.do(step)
                        else:
                            pe.quiet(step)
            act.wait(done, m_par)
            m_g8 = act.do(lambda e: e.activation(g8[:, :], ps[0:8, :], ACT.Identity, bias=gate_bias[l]))
            bank_free[b] = [m_g8]
            flush_gemv()
            act.quiet(lambda e: e.preload_act_table_set("natural_log_exp_and_others"))
            b, ps_f = take_bank()
            pe.wait(m_g8)
            m_f = pe.do(lambda e: e.matmul(ps_f[0:4, :], ident[0:8, 4:8], g8[:, :], start=True, stop=True))
            act.wait(m_f, *[(q.sem, q.count) for q in (dve,)])
            m = act.do(lambda e: e.activation(row_t[:, :], ps_f[0:4, :], ACT.Abs))
            act.wait(m)
            m = act.do(lambda e: e.activation(row_t[:, :], row_t[:, :], ACT.Exp, scale=-1.0))
            act.wait(m)
            m = act.do(lambda e: e.activation(row_t[:, :], row_t[:, :], ACT.Ln, bias=one_col[0:4, :]))
            dve.wait(m_f, m, part_free[0], *gemv_free.values())
            m_o = dve.do(lambda e: e.memset(row_ones[:, :], 1.0))
            m2 = dve.do(lambda e: e.tensor_scalar(row_lf[:, :], ps_f[0:4, :], 0.0, None, ALU.min))
            bank_free[b] = [m2, m]
            dve.wait(m2)
            m = dve.do(lambda e: e.tensor_tensor(row_lf[:, :], row_lf[:, :], row_t[:, :], ALU.subtract))
            dve.wait(m, m_o)
            m = dve.do(lambda e: e.tensor_tensor_scan(row_b[:, :], row_ones[:, :], row_lf[:, :], 0.0, ALU.mult, ALU.add))
            dve.wait(m)
            m_c = dve.do(lambda e: e.tensor_tensor(row_c[:, :], g8[0:4, :], row_b[:, :], ALU.subtract))
            dve.wait(m_c)
            m = dve.do(lambda e: e.tensor_tensor_scan(row_t[:, :], row_ones[:, :], row_c[:, :], 0.0, ALU.mult, ALU.max))
            dve.wait(m)
            m_nm = dve.do(lambda e: e.tensor_scalar(row_negm[:, :], row_t[:, :], -1.0, None, ALU.mult))
            m = dve.do(lambda e: e.tensor_tensor(row_em[:, :], row_b[:, :], row_t[:, :], ALU.add))
            act.wait(m)
            m_em = act.do(lambda e: e.activation(row_em[:, :], row_em[:, :], ACT.Exp, scale=-1.0))
            b, ps = take_bank()
            pe.wait(m_c)
            for j in range(N_CH):
                m = pe.do(lambda e, j=j: e.transpose(ps[:, 4 * j:4 * j + 4], row_c[:, j * P:(j + 1) * P],
                                                     ident[0:4, 0:4]))
            dve.wait(m)
            m_cc = dve.do(lambda e: e.tensor_copy(c_col, ps[:, 0:4 * N_CH]))
            bank_free[b] = [m_cc]

            m_hm, head_end = {}, {}
            rows_done = [m_nm, m_em, m_cc, done]
            bc_free = [None]

            def run_head(head):
                r = head % 2
                war = rows_done + head_end.get(head - 2, [])
                v_t, pt, den, hm_sq, hm_rstd = v_t2[r], pt2[r], den2[r], hm_sq2[r], hm_rstd2[r]
                sel = ident[0:4, head:head + 1].to_broadcast([4, P])
                for jj in range(2):
                    b, ps = take_bank()
                    for j in (2 * jj, 2 * jj + 1):
                        for m in range(2):
                            pe.wait(m_qkv[2, head, m], m_ident)
                            mt = pe.do(lambda e: e.transpose(
                                ps[:, (2 * (j - 2 * jj) + m) * P:(2 * (j - 2 * jj) + m + 1) * P],
                                qkv[2, head, m][:, j * P:(j + 1) * P], ident[:, :]))
                    act.wait(mt, *war)
                    m_vt = act.do(lambda e: e.activation(
                        v_t[:, 2 * jj:2 * jj + 2, :], ps[:, :].rearrange("p (j n) -> p j n", j=2), ACT.Copy))
                    bank_free[b] = [m_vt]
                b, ps = take_bank()
                pe.wait(m_nm)
                m = pe.do(lambda e: e.matmul(ps[:, :], sel, row_negm[:, :], start=True, stop=True))
                act.wait(m, bc_free[0], *war)
                m_bc = act.do(lambda e: e.activation(negm_bc[:, :], ps[:, :], ACT.Copy))
                bank_free[b] = [m_bc]
                pool.wait(m_bc, *war)
                m_dg = pool.do(lambda e: e.affine_select(
                    out=diag[:, :].rearrange("p (j t) -> p j t", j=N_CH),
                    in_=negm_bc[:, :].rearrange("p (j t) -> p j t", j=N_CH), compare_op=ALU.is_ge, fill=NEG, base=0,
                    pattern=[[0, N_CH], [1, P]], channel_multiplier=-1))
                m_e = []
                act.wait(m_bc)
                for j in range(N_CH):
                    cj = c_col[:, 4 * j + head:4 * j + head + 1]
                    if j < N_CH - 1:
                        act.do(lambda e: e.activation(pt[j][:, P:], negm_bc[:, (j + 1) * P:], ACT.Exp, bias=cj))
                act.wait(m_dg)
                for j in range(N_CH):
                    cj = c_col[:, 4 * j + head:4 * j + head + 1]
                    m_e.append(act.do(lambda e: e.activation(pt[j][:, 0:P], diag[:, j * P:(j + 1) * P],
                                                             ACT.Exp, bias=cj)))
                bc_free[0] = m_e[-1]
                m_p = []
                for j in range(N_CH):
                    b, ps = take_bank()
                    n_t = T - j * P
                    for m in range(2):
                        pe.wait(m_qkv[0, head, m], m_qkv[1, head, m])
                        ms = pe.do(lambda e: e.matmul(
                            ps[:, 0:n_t], qkv[1, head, m][:, j * P:(j + 1) * P], qkv[0, head, m][:, j * P:],
                            start=m == 0, stop=m == 1))
                    dve.wait(ms, m_e[j])
                    m = dve.do(lambda e: e.scalar_tensor_tensor(
                        pt[j][:, :], ps[:, 0:n_t], float(HEAD_D) ** -0.5, pt[j][:, :], ALU.mult, ALU.mult))
                    bank_free[b] = [m]
                    m_p.append(m)
                    if j == 1:
                        yield
                yield
                b_den, ps_den = take_bank()
                for j in range(N_CH):
                    pe.wait(m_p[j])
                    m_den = pe.do(lambda e: e.matmul(ps_den[:, j * P:], ones[:, :], pt[j][:, :],
                                                     start=j == 0, stop=j == N_CH - 1))
                b_em, ps_em = take_bank()
                pe.wait(m_em)
                m_emb = pe.do(lambda e: e.matmul(ps_em[:, :], sel, row_em[:, :], start=True, stop=True))
                act.wait(m_den, *war)
                m = act.do(lambda e: e.activation(den[:, :], ps_den[:, :], ACT.Abs))
                bank_free[b_den] = [m]
                dve.wait(m, m_emb)
                m = dve.do(lambda e: e.tensor_tensor(den[:, :], den[:, :], ps_em[:, :], ALU.max))
                bank_free[b_em] = [m]
                dve.wait(m)
                m_rec = dve.do(lambda e: e.reciprocal(den[:, :], den[:, :]))
                hm = [qkv[0, head, m][:, :] for m in range(2)]
                m_h = []
                pe.wait(m_vt)
                for m in range(2):
                    b, ps = take_bank()
                    for j in range(N_CH):
                        mv = pe.do(lambda e: e.matmul(ps[:, j * P:], v_t[:, j, m * P:(m + 1) * P], pt[j][:, :],
                                                      start=j == 0, stop=j == N_CH - 1))
                    dve.wait(mv, m_rec)
                    mk = dve.do(lambda e: e.tensor_tensor(hm[m], ps[:, :], den[:, :], ALU.mult))
                    bank_free[b] = [mk]
                    m_h.append(mk)
                yield
                b, ps = take_bank()
                for m in range(2):
                    pe.wait(m_h[m])
                    mm = pe.do(lambda e: e.matmul(ps[:, :], ones[:, :], hm[m], start=m == 0, stop=m == 1))
                m_sq = []
                for m in range(2):
                    dve.wait(mm, m_h[m])
                    m_h[m] = dve.do(lambda e: e.scalar_tensor_tensor(hm[m], ps[:, :], -1.0 / HEAD_D, hm[m],
                                                                     ALU.mult, ALU.add))
                    act.wait(m_h[m], *war)
                    m_sq.append(act.do(lambda e: e.activation(hm_sq[m][:, :], hm[m], ACT.Square)))
                bank_free[b] = [m_h[1]]
                yield
                b, ps = take_bank()
                for m in range(2):
                    pe.wait(m_sq[m])
                    m_v = pe.do(lambda e: e.matmul(ps[:, :], ones[:, :], hm_sq[m][:, :], start=m == 0, stop=m == 1))
                act.wait(m_v)
                mk = act.do(lambda e: e.activation(hm_rstd[:, :], ps[:, :], ACT.Ln, bias=eps_col, scale=1.0 / HEAD_D))
                bank_free[b] = [mk]
                act.wait(mk)
                m_rs = act.do(lambda e: e.activation(hm_rstd[:, :], hm_rstd[:, :], ACT.Exp, scale=-0.5))
                for m in range(2):
                    n = 2 * head + m
                    dve.wait(m_rs, m_h[m])
                    mk = dve.do(lambda e: e.scalar_tensor_tensor(
                        hm[m], hm[m], p[:, G_MH + n:G_MH + n + 1], hm_rstd[:, :], ALU.mult, ALU.mult))
                    dve.wait(mk, m_z[n])
                    mk = dve.do(lambda e: e.tensor_tensor(hm[m], hm[m], sig_z[n][:, :], ALU.mult))
                    m_hm[n] = split(hm[m], hm_hi[n][:, :], hm_lo[n][:, :], [mk])
                head_end[head] = [mk, m_rs, m_v, mv]

            normed, ring_free = {}, list(rows_done[3:]) * 2
            weave([(2, deque((lambda: True, run_head(head)) for head in range(HEADS))),
                   (2, deque((lambda i=i: len(fill) <= 2 * CONV_G * ((DT - 1 - i) // 2),
                              finish_conv(p, i, m_acc, ring_free, normed)) for i in range(DT)))])
            m_aa = {}
            for i in range(DT):
                acc = conv_acc[i][:, :]
                act.wait(normed[i])
                m = act.do(lambda e: e.activation(acc, acc, ACT.Silu, bias=p[:, B_CN + i:B_CN + i + 1]))
                m_aa[i] = split(acc, a_hi[i][:, :], a_lo[i][:, :], [m])
            act.wait(*m_hm.values(), *ring_free, m_spill)
            m_back = land_back.load(act, x_old[:, :, :], x_spill)

            mix = [(hm_hi[n][:, :], hm_lo[n][:, :], m_hm[n]) for n in range(DT)] + \
                  [(a_hi[n][:, :], a_lo[n][:, :], m_aa[n]) for n in range(DT)]
            m_y = [None] * DT

            def y_evac(n, ps, done):
                act.wait(done, *m_hm.values())
                m_y[n] = act.do(lambda e: e.activation(y[n][:, :], ps[:, :], ACT.Copy))
                m_sum[0] = add_square(n, y[n][:, :], m_y[n], [*m_hm.values()])
                return [m_y[n]]

            m_sum = [None]
            for g in range(2):
                gemm(f"w_out{l}", g, 2 * DT, mix, y_evac)
            flush_gemv()
            m_g = gate_columns(g_mixo[l], p[:, G_POST_MIX:G_POST_MIX + 8], mod[l][:, 16:24], m_mod[f"ada{l}", 0])
            m_s = scale_columns(s_mlp[l], p[:, G_PRE_MLP:G_PRE_MLP + 8], mod[l][:, 32:40], m_mod[f"ada{l}", 0])
            m_r = finish_square(m_sum[0], 1.0 / D)
            m_x = residual(y_ap, m_y, g_mixo[l], m_g, rstd, m_r, [x_old[:, n, :] for n in range(DT)], [m_back] * DT)
            m_r = mean_square(x_ap, m_x, sq_ring, sq_free, T, 1.0 / D, rstd, m_x[-1])
            h = modulate(x_ap, m_x, rstd, m_r, s_mlp[l], mod[l][:, 24:32], m_s, mod_tmp, tmp_free,
                         full(h_hi), full(h_lo), m_x)

            hidden = [[None] * QUARTER for _ in range(2)]
            t_free = [None] * 2
            m_yq = [None] * DT

            def up_evac(b, n, ps, done):
                r = n % 2
                t1, t2 = tmpf[3 + r][:, :], tmpf[5 + r][:, :]
                hi, lo = (t[:, :] for t in f1[b][n])
                act.wait(done, t_free[r])
                m1 = act.do(lambda e: e.activation(t1, ps[:, :], ACT.Relu))
                dve.wait(m1, t_free[r])
                m2 = dve.do(lambda e: e.tensor_tensor(t2, t1, t1, ALU.mult))
                act.wait(m1)
                m3 = act.do(lambda e: e.activation(hi, t1, ACT.Square))
                dve.wait(m2, m3)
                t_free[r] = dve.do(lambda e: e.tensor_tensor(lo, t2, hi.bitcast(F32), ALU.subtract))
                hidden[b][n] = (hi, lo, t_free[r])
                return [m1]

            def down_evac(q, n, ps, done):
                if q == 0:
                    act.wait(done, *m_x)
                    m_yq[n] = act.do(lambda e: e.activation(y[n][:, :], ps[:, :], ACT.Copy))
                else:
                    dve.wait(done, m_yq[n])
                    m_yq[n] = dve.do(lambda e: e.tensor_tensor(y[n][:, :], y[n][:, :], ps[:, :], ALU.add))
                if q == 3:
                    m_sum[0] = add_square(n, y[n][:, :], m_yq[n], [h[-1][2]])
                return [m_yq[n]]

            for step in ("up0", "up1", "down0", "up2", "down1", "up3", "down2", "down3"):
                q = int(step[-1])
                for g in range(2):
                    if step[:2] == "up":
                        gemm(f"{step}_{l}", g, DT, h, lambda n, ps, done: up_evac(q % 2, n, ps, done))
                    else:
                        gemm(f"{step}_{l}", g, DT, hidden[q % 2], lambda n, ps, done: down_evac(q, n, ps, done))
            m_g = gate_columns(g_mlpo[l], p[:, G_POST_MLP:G_POST_MLP + 8], mod[l][:, 40:48], m_mod[f"ada{l}", 0])
            m_r = finish_square(m_sum[0], 1.0 / D)
            return residual(y_ap, m_yq, g_mlpo[l], m_g, rstd, m_r, x, m_x)

        def second(m_x):
            flush_gemv()
            hc_hi = [at(f"hc_hi{i}", 51, [P, CTX], F32R, part=CTX * i) for i in range(DT)]
            hc_lo = [at(f"hc_lo{i}", 55, [P, CTX], F32R, part=CTX * i) for i in range(DT)]
            q2 = [at(f"q2_{i}", 59 + i, [P, T]) for i in range(DT)]
            k2 = [at(f"k2_{i}", 67 + i, [P, T]) for i in range(DT)]
            vw = at("v_windows", 75, [P, 2 * N_CH, D])
            kc = at("k_ctx", 91, [P, DT, CTX])
            vc = at("v_ctx", 95, [P, 2, D])
            sgb = [at(f"sig_gb{i}", 24 + i, [P, T]) for i in range(DT)]
            c_tok = at("ctx_tok", 59, [P, CTX // P, D])
            c_f = [at(f"ctx_f{i}", 63, [P, CTX], part=CTX * i) for i in range(DT)]
            csq = [at(f"ctx_sq{i}", 67, [P, CTX], part=CTX * i)[:, :] for i in range(2)]
            c_rstd = at("ctx_rstd", 68, [P, CTX])
            c_tmp = [at(f"ctx_tmp{i}", 69, [P, CTX], part=CTX * i)[:, :] for i in range(4)]
            rope = at("rope", 75, [P, 2, T])
            raw_t = [at(f"rope_in{i}", 77 + i, [P, T]) for i in range(3)]
            rot_t = [at(f"rope_rot{i}", 80 + i, [P, T]) for i in range(3)]
            v_f = at("v_f", 99, [P, N_CH, ROWS, K_COLS])
            vc_f = [at(f"v_ctx_f{i}", 101 + i, [P, 2 * CTX]) for i in range(2)]
            rot = at("rotation", 103, [P, P], part=320)
            mask = at("mask", 51, [P, 3, ROWS * K_COLS])
            bias = [at(f"bias{i}", 52, [P, 3, ROWS * K_COLS], part=256 + 768 * i) for i in range(2)]
            toep = [at(f"toeplitz{i}", 55, [P, ROWS, TOEP], part=256 + ROWS * TOEP * i) for i in range(2)]
            pr = [at(f"prob{i}", s, [P, T]) for i, s in enumerate((57, 58, 99))]
            prt = [at(f"prob_t{i}", 100 + i, [P, T]) for i in range(3)]

            land_c = Landing(sem("second_landed"))
            act.wait(*m_x)
            m_ctx = land_c.load(act, c_tok[:, :, :], A["ctx_2"][0].rearrange("(j p) n -> p j n", p=P))
            land_rope = Landing(sem("rope_landed"))
            m_rope = land_rope.load(act, rope[:, :, :], A["rope"].rearrange("f p t -> p f t"))

            m = pool.do(lambda e: e.memset(rot[:, :], 0.0))
            pool.wait(m)
            view = rot[:, :].rearrange("p (b h c) -> p b h c", h=2, c=16)
            m = pool.do(lambda e: e.affine_select(out=view[:, :, 1, :], in_=view[:, :, 1, :],
                                                  compare_op=ALU.not_equal, fill=1.0, base=0,
                                                  pattern=[[32, 4], [1, 16]], channel_multiplier=-1))
            pool.wait(m)
            m_rot = pool.do(lambda e: e.affine_select(out=view[:, :, 0, :], in_=view[:, :, 0, :],
                                                      compare_op=ALU.not_equal, fill=-1.0, base=16,
                                                      pattern=[[32, 4], [1, 16]], channel_multiplier=-1))

            m_s = scale_columns(s_2, par2[:, 24:32], mod2[:, 8:16], m_mod["mod2", 0])
            m_sc = scale_columns(s_2c, par2[:, 24:32], mod2c[:, 8:16], m_mod["mod2", 1])
            m_r = mean_square(x, m_x, sq_ring, sq_free, T, 1.0 / D, rstd, m_x[-1])
            h = modulate(x, m_x, rstd, m_r, s_2, mod2[:, 0:8], m_s, mod_tmp, [None] * 4,
                         full(h_hi), full(h_lo), m_x)
            m_c = transpose_in(lambda f, j: c_tok[:, j, f * P:(f + 1) * P], lambda f: c_f[f][:, :], DT, CTX // P,
                               [m_ctx, m_ident])
            m_r = mean_square([t[:, :] for t in c_f], m_c, csq, [None, None], CTX, 1.0 / D, c_rstd[:, :], None)
            hc = modulate([t[:, :] for t in c_f], m_c, c_rstd[:, :], m_r, s_2c, mod2c[:, 0:8], m_sc, c_tmp,
                          [None] * 4, full(hc_hi), full(hc_lo), m_x)

            act.wait(h[-1][2])
            m_spill = land_spill.load(act, x_spill, x_all[:, :, :])

            rope_free = [None] * 3
            m_q, m_k = {}, {}

            def rope_evac(dst, got, scale, n, ps, done):
                r = n % 3
                t, ro = raw_t[r][:, :], rot_t[r][:, :]
                act.wait(done, rope_free[r], *m_x)
                m1 = act.do(lambda e: e.activation(t, ps[:, :], ACT.Copy, scale=scale))
                b, ps2 = take_bank()
                pe.wait(m1, m_rot)
                m2 = pe.do(lambda e: e.matmul(ps2[:, :], rot[:, :], t, start=True, stop=True))
                dve.wait(m2, m_rope, rope_free[r])
                m3 = dve.do(lambda e: e.tensor_tensor(ro, ps2[:, :], rope[:, 1, :], ALU.mult))
                bank_free[b] = [m3]
                pool.wait(m2, m_rope, hc[-1][2])
                m4 = pool.do(lambda e: e.tensor_tensor(t, t, rope[:, 0, :], ALU.mult))
                dve.wait(m4, m3)
                if dst is q2:
                    kept = dst[n][:, :].rearrange("p (i r a) -> p r i a", i=N_CH, r=ROWS)
                    t, ro = (v.rearrange("p (r i a) -> p r i a", i=N_CH, r=ROWS) for v in (t, ro))
                else:
                    kept = dst[n][:, :]
                got[n] = rope_free[r] = dve.do(lambda e: e.tensor_tensor(kept, t, ro, ALU.add))
                return [m1]

            m_kc = {}

            def kc_evac(n, ps, done):
                act.wait(done, hc[-1][2], *m_x)
                m_kc[n] = act.do(lambda e: e.activation(kc[:, 2 * n:2 * n + 2, :],
                                                        ps[:, :].rearrange("p (a t) -> p a t", a=2), ACT.Copy))
                return [m_kc[n]]

            for g in range(2):
                gemm("q2", g, DT, h, lambda n, ps, done: rope_evac(q2, m_q, float(A_DIM) ** -0.5, n, ps, done))
            for g in range(2):
                gemm("k2", g, DT, h, lambda n, ps, done: rope_evac(k2, m_k, 1.0, n, ps, done), hc, kc_evac)

            vf_free, vcf_free = None, [None, None]
            m_v, m_vc = {}, {}

            def v_evac(n, ps, done):
                nonlocal vf_free
                act.wait(done, vf_free, *m_q.values())
                grid = ps[:, :].rearrange("p (r c) -> p r c", r=ROWS)
                for i in range(N_CH):
                    m1 = act.do(lambda e: e.activation(v_f[:, i, :, :], grid[:, :, K_START[i]:K_START[i] + K_COLS],
                                                       ACT.Copy))
                for half in range(2):
                    b, ps2 = take_bank()
                    pe.wait(m1)
                    for w in range(4):
                        i, rows_half = (4 * half + w) // 2, (4 * half + w) % 2
                        src = v_f[:, i, 4 * rows_half:4 * rows_half + 4, :].rearrange("p r c -> p (r c)")
                        m2 = pe.do(lambda e: e.transpose(ps2[:, w * P:(w + 1) * P], src, ident[:, :]))
                    dve.wait(m2, m_k[DT - 1])
                    m_v[n] = dve.do(lambda e: e.tensor_copy(vw[:, 4 * half:4 * half + 4, n * P:(n + 1) * P],
                                                            ps2[:, :].rearrange("p (w n) -> p w n", w=4)))
                    bank_free[b] = [m_v[n]]
                vf_free = m2
                return [m1]

            def vc_evac(n, ps, done):
                r = n % 2
                act.wait(done, vcf_free[r])
                m1 = act.do(lambda e: e.activation(vc_f[r][:, :], ps[:, :], ACT.Copy))
                b, ps2 = take_bank()
                pe.wait(m1)
                for j in range(2):
                    for u in range(2):
                        m2 = pe.do(lambda e: e.transpose(ps2[:, (2 * j + u) * P:(2 * j + u + 1) * P],
                                                         vc_f[r][:, u * CTX + j * P:u * CTX + (j + 1) * P], ident[:, :]))
                vcf_free[r] = m2
                dve.wait(m2, *m_x)
                m_vc[n] = dve.do(lambda e: e.tensor_copy(vc[:, :, 2 * n * P:2 * n * P + 2 * P],
                                                         ps2[:, :].rearrange("p (j n) -> p j n", j=2)))
                bank_free[b] = [m_vc[n]]
                return [m1]

            for g in range(2):
                gemm("v2", g, DT, h, v_evac, hc, vc_evac)

            after_v = [(pe.sem, pe.count), m_v[DT - 1], m_vc[3]]
            sp.wait(*after_v)
            land_mask = Landing(sem("mask_landed"))
            m_mask = land_mask.load(sp, mask[:, :, :], A["mask"].rearrange("v p k -> p v k"))
            land_t = [Landing(sem(f"toeplitz_landed{i}")) for i in range(2)]
            toep_free, bias_free = [None, None], [[], []]
            m_toep, m_bias = {}, {}

            def load_toeplitz(hd):
                r = hd % 2
                sp.wait(toep_free[r])
                t = A["rpb_padded"]
                for qr in range(ROWS):
                    src = bass.AP(t.tensor, (hd * (2 * ROWS - 1) + qr) * RPB_W, [[1, CH_COLS], [RPB_W, ROWS], [1, TOEP]])
                    m_toep[hd] = land_t[r].load(sp, toep[r][CH_COLS * qr:CH_COLS * (qr + 1), :, :], src)

            def make_bias(hd):
                r = hd % 2
                for v, off in enumerate((16, 8, 0)):
                    last = TOEP - 1 - off
                    src = toep[r][:, ::-1, last - K_COLS + 1:last + 1][:, :, ::-1]
                    pool.wait(m_toep[hd], m_mask, *bias_free[r], *after_v)
                    m_bias[hd] = pool.do(lambda e: e.tensor_tensor(
                        bias[r][:, v, :].rearrange("p (k b) -> p k b", k=ROWS), src,
                        mask[:, v, :].rearrange("p (k b) -> p k b", k=ROWS), ALU.add))
                toep_free[r] = m_bias[hd]
                bias_free[r] = []

            NB = ROWS * K_COLS
            work = [(hd, i) for hd in range(A_HEADS) for i in range(N_CH)]
            st = {}
            pr_free, prt_free = [None] * 3, [None] * 3
            small_free = [None] * 8
            o_bank, m_o = {}, {}

            def scores(n):
                hd, i = work[n]
                e2, pb, c3, c8 = hd // 2, A_DIM * (hd % 2), n % 3, n % 8
                part = slice(pb, pb + A_DIM)
                b, ps = take_bank()
                qv = q2[e2][part, i * P:(i + 1) * P]
                kv = k2[e2][part, :].rearrange("p (r c) -> p r c", r=ROWS)[:, :, K_START[i]:K_START[i] + K_COLS]
                pe.wait(m_q[e2], m_k[e2], m_kc[e2 // 2])
                pe.quiet(lambda e: e.matmul(ps[:, 0:NB], qv, kv, start=True, stop=True))
                ms = pe.do(lambda e: e.matmul(ps[:, NB:], qv, kc[part, e2, :], start=True, stop=True))
                top, neg = rowmax[:, c8:c8 + 1], rowsum[:, c8:c8 + 1]
                s1, s2 = rowsum[:, 8 + c8:9 + c8], rowsum[:, 16 + c8:17 + c8]
                v = (0, 1, 1, 2)[i]
                dve.wait(ms, small_free[c8])
                m1 = dve.do(lambda e: e.reduce_max(top, ps[:, NB:], AX.X))
                dve.wait(m1, m_bias[hd], pr_free[c3])
                m2 = dve.do(lambda e: e.tensor_tensor_reduce(pr[c3][:, 0:NB], ps[:, 0:NB], bias[hd % 2][:, v, :],
                                                             1.0, top, ALU.add, ALU.max, neg))
                bias_free[hd % 2].append(m2)
                dve.wait(m2)
                m3 = dve.do(lambda e: e.tensor_scalar(neg, neg, -1.0, None, ALU.mult))
                act.wait(m3)
                m4 = act.do(lambda e: e.activation(pr[c3][:, 0:NB], pr[c3][:, 0:NB], ACT.Exp, bias=neg, accum_out=s1))
                m5 = act.do(lambda e: e.activation(pr[c3][:, NB:], ps[:, NB:], ACT.Exp, bias=neg, accum_out=s2))
                bank_free[b] = [m5]
                st[n] = m5

            def normalise(n):
                c3, c8 = n % 3, n % 8
                s1, s2 = rowsum[:, 8 + c8:9 + c8], rowsum[:, 16 + c8:17 + c8]
                dve.wait(st[n])
                m = dve.do(lambda e: e.tensor_tensor(s1, s1, s2, ALU.add))
                dve.wait(m)
                m = dve.do(lambda e: e.reciprocal(s1, s1))
                pool.wait(m)
                st[n] = small_free[c8] = pool.do(lambda e: e.tensor_scalar(pr[c3][:, :], pr[c3][:, :], s1, None, ALU.mult))

            def turn(n):
                c3 = n % 3
                b, ps = take_bank()
                pe.wait(st[n])
                for k in range(4):
                    m = pe.do(lambda e: e.transpose(ps[:, k * P:(k + 1) * P], pr[c3][:, k * P:(k + 1) * P], ident[:, :]))
                pr_free[c3] = m
                act.wait(m, prt_free[c3])
                st[n] = act.do(lambda e: e.activation(prt[c3][:, :], ps[:, :], ACT.Copy))
                bank_free[b] = [st[n]]

            def values(n):
                hd, i = work[n]
                e2, pb, c3 = hd // 2, A_DIM * (hd % 2), n % 3
                part = slice(pb, pb + A_DIM)
                if i == 0:
                    o_bank[hd] = take_bank()
                b, ps = o_bank[hd]
                pe.wait(st[n])
                col = slice(A_DIM * hd, A_DIM * hd + A_DIM)
                for k in range(4):
                    vk = vw[:, 2 * i + k, col] if k < 2 else vc[:, k - 2, col]
                    m = pe.do(lambda e: e.matmul(ps[part, i * P:(i + 1) * P], vk, prt[c3][:, k * P:(k + 1) * P],
                                                 start=k == 0, stop=k == 3))
                prt_free[c3] = m
                if i == N_CH - 1:
                    dve.wait(m)
                    m_o[hd] = dve.do(lambda e: e.tensor_copy(
                        q2[e2][part, :].rearrange("p (r i a) -> p i r a", r=ROWS, i=N_CH),
                        ps[part, :].rearrange("p (i r a) -> p i r a", i=N_CH, r=ROWS)))
                    bank_free[b] = [m_o[hd]]

            m_sgb = {}

            def gb_evac(n, ps, done):
                act.wait(done, m_spill)
                m_sgb[n] = act.do(lambda e: e.activation(sgb[n][:, :], ps[:, :], ACT.Copy))
                return [m_sgb[n]]

            def g_b():
                for g in range(2):
                    yield from gemm_steps("g_b", g, DT, h, gb_evac)

            filler = g_b()
            load_toeplitz(0)
            load_toeplitz(1)
            make_bias(0)
            for n in range(len(work) + 3):
                if n < len(work):
                    hd, i = work[n]
                    if i == 1 and hd + 1 < A_HEADS:
                        make_bias(hd + 1)
                        if hd + 2 < A_HEADS:
                            load_toeplitz(hd + 2)
                    scores(n)
                if 0 <= n - 1 < len(work):
                    normalise(n - 1)
                if 0 <= n - 2 < len(work):
                    turn(n - 2)
                if 0 <= n - 3 < len(work):
                    values(n - 3)
                next(filler, None)
            for _ in filler:
                pass

            m_att = [m_o[A_HEADS - 1], (pe.sem, pe.count)]
            zo = [(at(f"zo_hi{i}", 67 + i, [P, T], F32R), at(f"zo_lo{i}", 75 + i, [P, T], F32R)) for i in range(DT)]
            yb = [at(f"y_b{i}", 83 + i, [P, T]) for i in range(DT)]
            sg = [at(f"sig_g{i}", 51 + i, [P, T]) for i in range(4)]
            z_free, m_zo, m_yb = [None] * 4, {}, {}

            def zb_evac(n, ps, done):
                r = n % 4
                act.wait(done, z_free[r], *m_att)
                m = act.do(lambda e: e.activation(sg[r][:, :], ps[:, :], ACT.Silu))
                dve.wait(m, m_o[2 * n + 1])
                m1 = dve.do(lambda e: e.tensor_tensor(sg[r][:, :], sg[r][:, :], q2[n][:, :], ALU.mult))
                hi, lo = zo[n][0][:, :], zo[n][1][:, :]
                z_free[r] = split(sg[r][:, :], hi, lo, [m1], m_att)
                m_zo[n] = (hi, lo, z_free[r])
                return [m]

            for g in range(2):
                gemm("z_b", g, DT, h, zb_evac)

            def copy_evac(dst, got, n, ps, done):
                act.wait(done, *m_att)
                got[n] = act.do(lambda e: e.activation(dst[n][:, :], ps[:, :], ACT.Copy))
                return [got[n]]

            def yb_evac(n, ps, done):
                act.wait(m_sgb[n])
                m = act.do(lambda e: e.activation(sgb[n][:, :], sgb[n][:, :], ACT.Sigmoid))
                dve.wait(done, m, *m_att)
                m_yb[n] = dve.do(lambda e: e.tensor_tensor(yb[n][:, :], ps[:, :], sgb[n][:, :], ALU.mult))
                return [m_yb[n]]

            for g in range(2):
                gemm("w_out_attn", g, DT, m_zo, yb_evac)
            act.wait(m_yb[DT - 1], m_spill)
            m_back = land_back.load(act, x_all[:, :, :], x_spill)

            sz = [at(f"silu_za{i}", 91 + i, [P, T]) for i in range(4)]
            cg = [at(f"c_gate{i}", 95 + i, [P, T]) for i in range(4)]
            up = [at(f"u_pad{i}", 51, [P, T + 2], part=(T + 8) * i) for i in range(4)]
            ac = [at(f"conv3_{i}", 99 + i, [P, T]) for i in range(4)]
            cv = [(at(f"cv_hi{i}", 59 + i, [P, T], F32R), at(f"cv_lo{i}", 67 + i, [P, T], F32R)) for i in range(DT)]
            dve.wait(*z_free, *m_att)
            for i in range(4):
                dve.do(lambda e: e.memset(up[i][:, 0:1], 0.0))
                m_pad = dve.do(lambda e: e.memset(up[i][:, T + 1:T + 2], 0.0))
            sz_m, cg_m, m_cv, ac_free = {}, {}, {}, {}

            def za_evac(n, ps, done):
                act.wait(done, ac_free.get(n - 4), *m_att)
                sz_m[n] = act.do(lambda e: e.activation(sz[n % 4][:, :], ps[:, :], ACT.Silu))
                return [sz_m[n]]

            def bg_evac(n, ps, done):
                dve.wait(done, sz_m[n])
                sz_m[n] = dve.do(lambda e: e.tensor_tensor(sz[n % 4][:, :], sz[n % 4][:, :], ps[:, :], ALU.mult))
                return [sz_m[n]]

            def cg_evac(n, ps, done):
                act.wait(done, ac_free.get(n - 4))
                cg_m[n] = act.do(lambda e: e.activation(cg[n % 4][:, :], ps[:, :], ACT.Copy))
                return [cg_m[n]]

            def xi_evac(n, ps, done):
                r = n % 4
                dve.wait(done, cg_m[n], m_pad, ac_free.get(n - 4))
                m_u = m = dve.do(lambda e: e.tensor_tensor(up[r][:, 1:T + 1], ps[:, :], cg[r][:, :], ALU.mult))
                for k in range(3):
                    w = par2[:, 40 + 8 * k + n:41 + 8 * k + n]
                    dve.wait(m)
                    if k == 0:
                        m = dve.do(lambda e: e.tensor_scalar(ac[r][:, :], up[r][:, 0:T], w, par2[:, 64 + n:65 + n],
                                                             ALU.mult, ALU.add))
                    else:
                        m = dve.do(lambda e: e.scalar_tensor_tensor(ac[r][:, :], up[r][:, k:k + T], w, ac[r][:, :],
                                                                    ALU.mult, ALU.add))
                dve.wait(m, sz_m[n])
                m = dve.do(lambda e: e.tensor_tensor(ac[r][:, :], ac[r][:, :], sz[r][:, :], ALU.mult))
                hi, lo = cv[n][0][:, :], cv[n][1][:, :]
                ac_free[n] = split(ac[r][:, :], hi, lo, [m], [m_yb[DT - 1]])
                m_cv[n] = (hi, lo, ac_free[n])
                return [m_u]

            for half in range(2):
                for key, evac in (("z_a", za_evac), ("b_gate", bg_evac), ("c_gate", cg_evac), ("x_in", xi_evac)):
                    gemm(f"{key}{half}", 0, DT, h, lambda n, ps, done: evac(4 * half + n, ps, done))

            sga = [at(f"sig_ga{i}", 75 + i, [P, T]) for i in range(DT)]
            m_ga, m_mg = {}, {}

            def ga_evac(n, ps, done):
                act.wait(done, m_yb[DT - 1])
                m_ga[n] = act.do(lambda e: e.activation(sga[n][:, :], ps[:, :], ACT.Sigmoid))
                return [m_ga[n]]

            for g in range(2):
                gemm("g_a", g, DT, h, ga_evac)
            h_read = (pe.sem, pe.count)

            def merge_evac(n, ps, done):
                dve.wait(done, m_ga[n])
                m = dve.do(lambda e: e.tensor_tensor(sga[n][:, :], ps[:, :], sga[n][:, :], ALU.mult))
                dve.wait(m, m_yb[n])
                m2 = dve.do(lambda e: e.tensor_tensor(yb[n][:, :], yb[n][:, :], sga[n][:, :], ALU.add))
                hi, lo = h_hi[n][:, :], h_lo[n][:, :]
                m_mg[n] = (hi, lo, split(yb[n][:, :], hi, lo, [m2], [h_read]))
                return [m]

            for g in range(2):
                gemm("w_out_conv", g, DT, m_cv, merge_evac)
            y2 = [at(f"y_second{i}", 51 + i, [P, T]) for i in range(DT)]
            m_y2 = {}
            m_sum = [None]

            def y2_evac(n, ps, done):
                copy_evac(y2, m_y2, n, ps, done)
                m_sum[0] = add_square(n, y2[n][:, :], m_y2[n], [h_read])
                return [m_y2[n]]

            for g in range(2):
                gemm("w_o", g, DT, m_mg, y2_evac)
            m_g = gate_columns(g_2o, par2[:, 32:40], mod2[:, 16:24], m_mod["mod2", 0])
            m_r = finish_square(m_sum[0], 1.0 / D)
            return residual(full(y2), m_y2, g_2o, m_g, rstd, m_r, x, [m_back] * DT)

        if probe is None or probe >= 1:
            prepare(8)
        if probe is None or probe >= 1:
            m_x = layer(0, m_x)
        if probe is None or probe >= 2:
            m_x = layer(1, m_x)
        if probe is None or probe >= 3:
            m_x = second(m_x)
        m_barrier = m_x

        y_tok = at("y_tok", 35, [P, N_CH, D])
        land_out = Landing(sem("out_landed"))
        for j in range(N_CH):
            for half in range(2):
                i, ps = take_bank()
                for f in range(4):
                    n = 4 * half + f
                    pe.wait(m_x[n])
                    m = pe.do(lambda e, n=n, j=j, f=f, ps=ps: e.transpose(ps[:, f * P:(f + 1) * P],
                                                                          x[n][:, j * P:(j + 1) * P], ident[:, :]))
                q = (dve, act)[half]
                q.wait(m, *m_barrier)
                dst = y_tok[:, j, 512 * half:512 * half + 512]
                if half:
                    m = act.do(lambda e, dst=dst, ps=ps: e.activation(dst, ps[:, :], ACT.Copy))
                else:
                    m = dve.do(lambda e, dst=dst, ps=ps: e.tensor_copy(dst, ps[:, :]))
                bank_free[i] = [m]
                sp.wait(m)
            m_out = land_out.load(sp, out[0, j * P:(j + 1) * P, :], y_tok[:, j, :])
        sp.wait(m_out)
        if land_spill.count:
            sp.wait((land_spill.sem, land_spill.count))


_INS = ["x", "c", "w_ada", "b_ada", "g_pre_mix", "g_post_mix", "g_pre_mlp", "g_post_mlp", "w_in", "w_conv_m",
        "b_conv_m", "w_q", "w_k", "w_v", "w_gates", "b_gates", "g_mh", "w_dw", "b_dw", "g_cn", "b_cn", "w_out",
        "w_ff1", "w_ff2", "c_2", "ctx_2", "c_ctx_2", "w_mod_2", "b_mod_2", "pre_g_2", "post_g_2", "w_in_2",
        "conv_w_2", "conv_b_2", "w_out_conv_2", "w_out_attn_2", "w_o_2"]


def shape_constants():
    tok = np.arange(T)
    half = A_DIM // 2
    inv = np.float32(10000.0) ** (-np.arange(0, half, 2, dtype=np.float32) / np.float32(half))
    ang_r = (tok // GRID).astype(np.float32)[:, None] * inv
    ang_c = (tok % GRID).astype(np.float32)[:, None] * inv
    ang = np.concatenate([ang_r, ang_r, ang_c, ang_c], axis=-1)
    rope = np.stack([np.tile(f(ang).astype(np.float32).T, (P // A_DIM, 1)) for f in (np.cos, np.sin)])
    mask = np.zeros((3, ROWS, CH_COLS, ROWS, K_COLS), np.float32)
    for v, i in enumerate((0, 1, 3)):
        qc = CH_COLS * i + np.arange(CH_COLS)
        kc = K_START[i] + np.arange(K_COLS)
        start = np.clip(qc - WIN // 2, 0, GRID - WIN)[:, None]
        seen = (kc >= start) & (kc < start + WIN)
        mask[v] = np.where(seen, 0.0, NEG)[None, :, None, :]
    return {"rope": rope, "mask": mask.reshape(3, P, ROWS * K_COLS)}


def kernel(**inputs):
    import concourse.bacc as bacc
    from concourse.bass_utils import run_bass_kernel_spmd

    nc = bacc.Bacc("TRN2", target_bir_lowering=False, num_devices=1)
    arrays = {name: np.ascontiguousarray(inputs[name]) for name in _INS}
    rpb = inputs["rpb_2"]
    padded = np.zeros((A_HEADS, 2 * ROWS - 1, RPB_W), rpb.dtype)
    padded[:, :, WIN:WIN + 2 * WIN - 1] = rpb[0][:, ::-1, ::-1]
    arrays["rpb_padded"] = padded
    arrays.update(shape_constants())
    A = {name: nc.dram_tensor(f"in_{name}", a.shape, mybir.dt.from_np(a.dtype), kind="ExternalInput").ap()
         for name, a in arrays.items()}
    out = nc.dram_tensor("x_out", (1, T, D), F32, kind="ExternalOutput").ap()
    build(nc, A, out)
    r = run_bass_kernel_spmd(nc, [{f"in_{name}": a for name, a in arrays.items()}], core_ids=[0])
    return r.results[0]["x_out"]
```

```python
from collections import deque
from contextlib import ExitStack

import numpy as np

import concourse.bass as bass
from concourse import mybir

F32 = mybir.dt.float32
BF16 = mybir.dt.bfloat16
F32R = mybir.dt.float32r
ALU = mybir.AluOpType
ACT = mybir.ActivationFunctionType
AX = mybir.AxisListType

P = 128
D = 1024
T = 512
DT = D // P
DEPTH = 2
HEADS, HEAD_D = 4, 256
CONV_M, CONV_G = 4, 31
FF = 4 * D
QUARTER = FF // 4 // P
EPS = 1e-6
NEG = -1e30

GRID = 64
ROWS = T // GRID
CTX = 256
A_HEADS, A_DIM = 16, 64
WIN = 16
CH_COLS = P // ROWS
N_CH = T // P
K_COLS = 32
K_START = [0, 8, 24, 32]
TOEP = 48
RPB_W = 64
SLOT = 2048


class Queue:

    def __init__(self, engine, sem):
        self.engine, self.sem, self.count, self.seen = engine, sem, 0, {}

    def wait(self, *marks):
        for mark in marks:
            if mark is None:
                continue
            sem, value = mark
            if self.seen.get(sem.name, 0) < value:
                self.seen[sem.name] = value
                self.engine.wait_ge(sem, value)

    def do(self, step):
        self.count += 1
        step(self.engine).then_inc(self.sem, 1)
        return (self.sem, self.count)

    def quiet(self, step):
        step(self.engine)


class Landing:

    def __init__(self, sem):
        self.sem, self.count = sem, 0

    def load(self, queue, dst, src):
        self.count += 16
        queue.engine.dma_start(dst, src).then_inc(self.sem, 16)
        return (self.sem, self.count)


def build(nc, A, out):
    ctx = ExitStack()
    with ctx:
        sem = lambda name: ctx.enter_context(nc.semaphore(name))
        base = (nc.sbuf_base + 63) // 64 * 64
        n_arena = (nc.sbuf_usable_end - base) // 32 * 32
        ctx.enter_context(nc.sbuf_tensor("arena", [P, n_arena // 4 - 16], F32))

        def at(name, slot, shape, dtype=F32, part=0):
            return nc.alloc_sbuf_tensor_at(name, shape, dtype, offset=base + int(slot * SLOT) + 4 * part)

        pe, act, dve, pool = Queue(nc.tensor, sem("pe_done")), Queue(nc.scalar, sem("act_done")), \
            Queue(nc.vector, sem("dve_done")), Queue(nc.gpsimd, sem("pool_done"))
        sp = Queue(nc.sync, None)

        psum = [ctx.enter_context(nc.psum_tensor(f"bank{i}", [P, 512], F32)) for i in range(8)]
        bank_turn = [0]
        bank_free = [[] for _ in range(8)]

        def take_bank():
            assert any(marks is not None for marks in bank_free)
            while bank_free[bank_turn[0] % 8] is None:
                bank_turn[0] += 1
            i = bank_turn[0] % 8
            bank_turn[0] += 1
            pe.wait(*bank_free[i])
            bank_free[i] = None
            return i, psum[i]

        par = [at(f"params{l}", 32 + l, [P, 512]) for l in range(DEPTH)]
        par2 = at("params_second", 34, [P, 128])
        cols = at("columns", 34, [P, 384], part=128)
        ident = at("ident", 103, [P, P])
        ones = at("ones", 103, [P, P], part=128)
        misc = at("misc", 103, [P, 64], part=256)
        ones_bf = at("ones_bf", 103, [P, 2], BF16, part=448)
        eps_col, one_col = misc[:, 0:1], misc[:, 1:2]
        gate_bias = [par2[0:8, 96 + l:97 + l] for l in range(DEPTH)]
        rowmax, rowsum = misc[:, 8:16], misc[:, 16:48]

        c = [0]

        def column(n):
            c[0] += n
            return cols[:, c[0] - n:c[0]]

        mod = [column(48) for _ in range(DEPTH)]
        mod2, mod2c = column(24), column(16)
        s_mix, s_mlp, g_mixo, g_mlpo = ([column(8) for _ in range(DEPTH)] for _ in range(4))
        s_2, s_2c, g_2o = column(8), column(8), column(8)
        cact = column(24)

        m_ones = [pool.do(lambda e: e.memset(ones[:, :], 1.0)),
                  pool.do(lambda e: e.memset(ident[:, :], 0.0)),
                  pool.do(lambda e: e.memset(eps_col, EPS)),
                  pool.do(lambda e: e.memset(one_col, 1.0)),
                  pool.do(lambda e: e.memset(ones_bf[:, :], 1.0))]
        pool.wait(m_ones[1])
        m_ident = pool.do(lambda e: e.affine_select(out=ident[:, :], in_=ident[:, :], compare_op=ALU.not_equal,
                                                    fill=1.0, base=0, pattern=[[-1, P]], channel_multiplier=1))

        stage = at("param_rows", 90, [P, 9, P])
        land_par = Landing(sem("params_landed"))
        m_par = land_par.load(sp, stage[:, :, :], A["param_rows"].rearrange("(t r) c -> r t c", r=P))
        W_CONV_M, W_DW = ROW["w_conv_m"], ROW["w_dw"]
        B_ADA, G_PRE_MIX, G_POST_MIX, G_PRE_MLP, G_POST_MLP, B_CONV_M, G_MH, B_DW, G_CN, B_CN = \
            (ROW[n] for n in ("b_ada", "g_pre_mix", "g_post_mix", "g_pre_mlp", "g_post_mlp", "b_conv_m", "g_mh",
                              "b_dw", "g_cn", "b_cn"))

        x_all = at("x_all", 24, [P, DT, T])
        x = [x_all[:, i, :] for i in range(DT)]
        x_tok = at("x_tok", 80, [P, N_CH, D])
        land_x = Landing(sem("x_landed"))
        m_xt = land_x.load(sp, x_tok[:, :, :], A["x"][0].rearrange("(j p) n -> p j n", p=P))

        def to_columns(tiles, dst_of, marks):
            i, ps = take_bank()
            for n, t in enumerate(tiles):
                pe.wait(*marks)
                m = pe.do(lambda e, n=n, t=t: e.transpose(ps[:, n * P:(n + 1) * P], stage[:, t, :], ident[:, :]))
            dve.wait(m)
            m = dve.do(lambda e: e.tensor_copy(dst_of, ps[:, 0:len(tiles) * P]))
            bank_free[i] = [m]
            return m

        m_par2 = to_columns([8], par2[:, :], [m_par, m_ident])
        m_parl = [to_columns(range(4 * l, 4 * l + 4), par[l][:, :], [m_par, m_ident]) for l in range(DEPTH)]
        act.wait(m_par2)
        m_cact = act.do(lambda e: e.activation(cact, par2[:, 72:96], ACT.Silu))

        def transpose_in(src_of, dst_of, n_feat, n_chunk, marks, extra=()):
            done = []
            for f in range(n_feat):
                i, ps = take_bank()
                for j in range(n_chunk):
                    pe.wait(*marks)
                    m = pe.do(lambda e, f=f, j=j: e.transpose(ps[:, j * P:(j + 1) * P], src_of(f, j), ident[:, :]))
                q = (dve, act)[f % 2]
                q.wait(m, *extra)
                if f % 2:
                    m = act.do(lambda e, f=f, ps=ps: e.activation(dst_of(f), ps[:, 0:n_chunk * P], ACT.Copy))
                else:
                    m = dve.do(lambda e, f=f, ps=ps: e.tensor_copy(dst_of(f), ps[:, 0:n_chunk * P]))
                bank_free[i] = [m]
                done.append(m)
            return done

        m_x = transpose_in(lambda f, j: x_tok[:, j, f * P:(f + 1) * P], lambda f: x[f][:, :], DT, N_CH,
                           [m_xt, m_ident])

        RAW, HL, PIECE = 4, 2, 1024
        raw = [at(f"w_raw{i}", 2 * i, [P, PIECE]) for i in range(RAW)]
        w_hi = [at(f"w_hi{i}", 8 + 4 * i, [P, 2048], F32R) for i in range(HL)]
        w_lo = [at(f"w_lo{i}", 16 + 4 * i, [P, 2048], F32R) for i in range(HL)]
        land_w = [Landing(sem(f"w_landed{i}")) for i in range(RAW)]
        plan = []

        def block(key, src, is_split):
            src = src.rearrange("(k p) n -> p k n", p=P)
            plan_pieces = [[(0, PIECE, src[:, k:k + 2, :])] for k in (0, 2)]
            return (key, plan_pieces, is_split)

        def plan_gemm(key, w, row0, kt, col0, groups, interleave=(), first=0, skip=0):
            interleave = deque(interleave)
            for g in range(groups):
                per_block = 0 if g < skip else 1 if not skip else 2
                for kh in range(kt // 4):
                    row = row0 + 512 * ((kh + first) % (kt // 4))
                    src = w[row:row + 512, col0 + g * 512:col0 + g * 512 + 512]
                    plan.append(block((key, g, kh), src, True))
                    for _ in range(min(per_block, len(interleave))):
                        plan.append(interleave.popleft())
            plan.extend(interleave)
            plan[:] = [b for b in plan if b]

        def gemv_blocks(key, w, g0, g1):
            return [block((key, g, kh), w[kh * 512:kh * 512 + 512, g * 512:g * 512 + 512], False)
                    for g in range(g0, g1) for kh in range(2)]

        for pair in (0, 2):
            even, odd = (gemv_blocks("ada0", A["w_ada"][0], g, g + 1) for g in (pair, pair + 1))
            plan += [b for both in zip(even, odd) for b in both]
        GLU_B, GLU_A, X_M, Z = 3072, 2048, 0, 1024
        for l in range(DEPTH):
            rest = deque(gemv_blocks("ada0", A["w_ada"][0], 4, 12) if l == 0 else [])
            take = lambda n: [rest.popleft() for _ in range(min(n, len(rest)))]
            for half in range(2):
                plan_gemm(f"glu_b{l}{half}", A["w_in"][l], 0, DT, GLU_B + 512 * half, 1, take(2))
                plan_gemm(f"glu_a{l}{half}", A["w_in"][l], 0, DT, GLU_A + 512 * half, 1, take(2 - 2 * half))
            for half in range(2):
                plan_gemm(f"x_m{l}{half}", A["w_in"][l], 0, DT, X_M + 512 * half, 1)
                plan_gemm(f"z{l}{half}", A["w_in"][l], 0, DT, Z + 512 * half, 1)
                for h in (2 * half, 2 * half + 1):
                    wq, wk, wv = (A[w][l, h].rearrange("(k p) n -> p k n", p=P) for w in ("w_q", "w_k", "w_v"))
                    plan.append(((f"qkv{l}", h, 0), [[(0, 512, wq), (512, 512, wk)], [(0, 512, wv)]], True))
            plan_gemm(f"w_out{l}", A["w_out"][l], 0, 2 * DT, 0, 2, take(6), 2, 1)
            nxt = gemv_blocks("ada1", A["w_ada"][1], 0, 12) if l == 0 else [b for gemv in gemv_blocks("mod2", A["w_mod_2"][0], 0, 6) for b in (gemv, None)]
            nxt = deque(list(rest) + nxt)
            take = lambda n: [nxt.popleft() for _ in range(min(n, len(nxt)))]
            for step in ("up0", "up1", "down0", "up2", "down1", "up3", "down2", "down3"):
                q = int(step[-1])
                if step[:2] == "up":
                    plan_gemm(f"{step}_{l}", A["w_ff1"][l], 0, DT, q * 1024, 2, take(4))
                else:
                    plan_gemm(f"{step}_{l}", A["w_ff2"][l], q * 1024, DT, 0, 2, take(4))
        w2 = A["w_in_2"][0]
        for key, col in (("q2", 4096), ("k2", 5120), ("v2", 6144), ("g_b", 9216), ("z_b", 7168)):
            plan_gemm(key, w2, 0, DT, col, 2)
        plan_gemm("w_out_attn", A["w_out_attn_2"][0], 0, DT, 0, 2)
        for half in range(2):
            for key, col in (("z_a", 3072), ("b_gate", 0), ("c_gate", 1024), ("x_in", 2048)):
                plan_gemm(f"{key}{half}", w2, 0, DT, col + 512 * half, 1)
        plan_gemm("g_a", w2, 0, DT, 8192, 2)
        plan_gemm("w_out_conv", A["w_out_conv_2"][0], 0, DT, 0, 2)
        plan_gemm("w_o", A["w_o_2"][0], 0, DT, 0, 2)

        raw_free = [None] * RAW
        hl_free = [None] * HL
        ready = {}
        nxt_prep, split_count = [0], [0]
        all_pieces = [piece for _, pieces, _ in plan for piece in pieces]
        landed = []

        def issue_loads(limit):
            while len(landed) < min(limit, len(all_pieces)):
                s = len(landed) % RAW
                sp.wait(raw_free[s])
                for off, size, src in all_pieces[len(landed)]:
                    dst = raw[s][:, off:off + size].rearrange("p (k n) -> p k n", k=src.shape[1])
                    mark = land_w[s].load(sp, dst, src)
                landed.append(mark)

        taken = [0]

        def prepare(limit):
            while nxt_prep[0] < min(limit, len(plan)):
                key, pieces, is_split = plan[nxt_prep[0]]
                if is_split:
                    t = split_count[0] % HL
                    split_count[0] += 1
                for n, piece in enumerate(pieces):
                    issue_loads(taken[0] + RAW)
                    s, here = taken[0] % RAW, landed[taken[0]]
                    size = sum(p[1] for p in piece)
                    if is_split:
                        part = slice(PIECE * n, PIECE * n + size)
                        act.wait(here, hl_free[t])
                        m = act.do(lambda e: e.activation(w_hi[t][:, part], raw[s][:, 0:size], ACT.Copy))
                        pool.wait(here, m)
                        m = pool.do(lambda e: e.tensor_tensor(w_lo[t][:, part], raw[s][:, 0:size],
                                                              w_hi[t][:, part].bitcast(F32), ALU.subtract))
                        raw_free[s] = m
                        ready[key] = (t, m)
                    else:
                        raw_free[s] = consume_gemv(key, n, raw[s], here)
                    taken[0] += 1
                issue_loads(taken[0] + RAW)
                nxt_prep[0] += 1

        def prefetch():
            while nxt_prep[0] < len(plan) and sum(is_split for _, _, is_split in plan[nxt_prep[0]:nxt_prep[0] + 1]) \
                    and len(ready) < HL:
                prepare(nxt_prep[0] + 1)

        gemv_acc = [at("gemv_acc", 102, [P, 512]), at("gemv_acc_ctx", 83, [P, 512])]
        gemv_part = [at(f"gemv_part{i}", 100, [P, 512], BF16, part=256 * i) for i in range(3)]
        gemv_last = {0: None, 1: None}
        gemv_row = [at(f"gemv_row{i}", 98 + i, [1, T]) for i in range(2)]
        row_free, row_bank = [None, None], [None]
        gemv_free = {0: None, 1: None}
        part_free = [None]
        TARGETS = {"ada0": [(0, 0, mod[0], 48)], "ada1": [(0, 0, mod[1], 48)],
                   "mod2": [(0, 1, mod2, 24), (1, 2, mod2c, 16)]}
        m_mod = {}
        gemv_tail, gemv_cut = [], []

        def product_gemv(g, n, w, m_landed):
            if n == 0:
                row_bank[0] = take_bank()
            ps = row_bank[0][1]
            pe.wait(m_landed, m_cact)
            for k in (n, n + 1):
                m = pe.do(lambda e: e.matmul(ps[0:1, :], cact[:, k:k + 1], w[:, 512 * (k - n):512 * (k - n) + 512],
                                             start=k == 0, stop=k == DT - 1))
            if n == DT - 2:
                r = g // 2
                act.wait(m, row_free[r])
                mk = act.do(lambda e: e.activation(gemv_row[r][:, :], ps[0:1, :], ACT.Copy))
                bank_free[row_bank[0][0]] = [mk]
                row_columns(g, r, mk)
            return m

        def row_columns(g, r, m_row):
            b, ps = take_bank()
            pe.wait(m_row, *m_ones)
            for i in range(4):
                m = pe.do(lambda e: e.matmul(ps[:, i:i + 1], gemv_row[r][:, i * P:(i + 1) * P], ones[0:1, 0:1],
                                             start=True, stop=True))
            row_free[r] = m
            dve.wait(m, *m_parl)
            m = dve.do(lambda e: e.tensor_tensor(mod[0][:, 4 * g:4 * g + 4], ps[:, 0:4], par[0][:, 4 * g:4 * g + 4],
                                                 ALU.add))
            bank_free[b] = [m]
            m_mod["ada0", 0] = m

        def consume_gemv(key, piece, w, m_landed):
            name, g, kh = key
            if name == "ada0" and g in (1, 3):
                return product_gemv(g, 4 * kh + 2 * piece, w, m_landed)
            if kh == 0 and piece == 0:
                cut_gemv()
            targets = [t for t in TARGETS[name] if 4 * g < t[3]]
            for a, which, dst, _ in targets:
                acc = gemv_acc[a]
                for k in range(2):
                    n = 4 * kh + 2 * piece + k
                    ck, wk = cact[:, 8 * which + n:8 * which + n + 1], w[:, 512 * k:512 * k + 512]
                    if n == 0:
                        dve.wait(m_landed, m_cact, gemv_free[a])
                        gemv_last[a] = dve.do(lambda e: e.tensor_scalar(acc[:, :], wk, ck, None, ALU.mult))
                    else:
                        dve.wait(m_landed, gemv_last[a])
                        gemv_last[a] = dve.do(lambda e: e.scalar_tensor_tensor(acc[:, :], wk, ck, acc[:, :],
                                                                               ALU.mult, ALU.add))
            if kh == 1 and piece == 1:
                gemv_tail.extend((name, a, g, dst, gemv_last[a]) for a, _, dst, _ in targets)
                if len(targets) == 1:
                    cut_gemv()
            return (dve.sem, dve.count)

        def cut_gemv():
            while gemv_tail:
                sum_gemv()
                name, a, g, dst, m = gemv_tail.pop(0)
                acc = gemv_acc[a][:, :]
                dve.wait(m, part_free[0])
                for n in range(3):
                    m = dve.do(lambda e: e.tensor_copy(gemv_part[n][:, :], acc))
                    dve.wait(m)
                    if n < 2:
                        m = dve.do(lambda e: e.tensor_tensor(acc, acc, gemv_part[n][:, :], ALU.subtract))
                        dve.wait(m)
                gemv_free[a] = m
                gemv_cut.append((name, a, g, dst, m))

        def sum_gemv():
            while gemv_cut:
                name, a, g, dst, m_part = gemv_cut.pop(0)
                i, ps = take_bank()
                pe.wait(m_part, *m_ones)
                for n in range(4):
                    for k in range(3):
                        step = lambda e: e.matmul(ps[:, n:n + 1], gemv_part[k][:, n * P:(n + 1) * P],
                                                  ones_bf[:, 0:1], start=k == 0, stop=k == 2)
                        if n < 3 or k < 2:
                            pe.quiet(step)
                part_free[0] = m = pe.do(step)
                bias = par2[:, 4 * g:4 * g + 4] if name == "mod2" else par[int(name[-1])][:, 4 * g:4 * g + 4]
                dve.wait(m, m_par2, *m_parl)
                m = dve.do(lambda e: e.tensor_tensor(dst[:, 4 * g:4 * g + 4], ps[:, 0:4], bias, ALU.add))
                bank_free[i] = [m]
                m_mod[name, a] = m

        def flush_gemv():
            cut_gemv()
            sum_gemv()

        fill, pool_fill, later = deque(), deque(), deque()

        def pump(n, keep=0, pool_taps=1):
            for _ in range(min(n, len(fill))):
                fill.popleft()()
            for _ in range(min(pool_taps, len(pool_fill))):
                pool_fill.popleft()()
            while len(later) > keep:
                later.popleft()()

        def products(ps_ap, whi, wlo, xhi, xlo, first, last, mark, shared=False):
            seq = [(wlo, xhi), (whi, xlo), (whi, xhi)]
            for n, (a, b) in enumerate(seq):
                step = lambda e, a=a, b=b, n=n: e.matmul(ps_ap, a, b, start=first and n == 0,
                                                         stop=last and n == 2, skip_group_check=shared)
                if mark and n == 2:
                    return pe.do(step)
                pe.quiet(step)

        def gemm_steps(key, group, kt, rhs, evac, second=None, evac2=None, fills=(4, 4), keep=0):
            banks = [take_bank() for _ in range(4)]
            banks2 = [take_bank() for _ in range(2)] if second else []
            n_kh = kt // 4
            for kh in range(n_kh):
                while (key, group, kh) not in ready:
                    prepare(nxt_prep[0] + 1)
                t, m_w = ready.pop((key, group, kh))
                while nxt_prep[0] < len(plan) and not ready:
                    prepare(nxt_prep[0] + 1)
                pe.wait(m_w)
                for m in range(4):
                    for k in range(4):
                        while isinstance(rhs, dict) and 4 * kh + k not in rhs:
                            yield
                        hi, lo, mark = rhs[4 * kh + k]
                        pe.wait(mark)
                        c0 = 512 * k + P * m
                        last = kh == n_kh - 1 and k == 3
                        done = products(banks[m][1][:, 0:hi.shape[1]], w_hi[t][:, c0:c0 + P], w_lo[t][:, c0:c0 + P],
                                        hi, lo, kh == 0 and k == 0, last, k == 3)
                        if last:
                            banks[m] += (done,)
                        yield
                    if second:
                        ps2 = banks2[m // 2][1][:, (m % 2) * CTX:(m % 2 + 1) * CTX]
                        for k in range(4):
                            hi, lo, mark = second[4 * kh + k]
                            pe.wait(mark)
                            c0 = 512 * k + P * m
                            last = kh == n_kh - 1 and k == 3
                            done = products(ps2, w_hi[t][:, c0:c0 + P], w_lo[t][:, c0:c0 + P], hi, lo,
                                            kh == 0 and k == 0 and m % 2 == 0, last, k == 3, True)
                        if last:
                            banks2[m // 2] += (done,)
                    if m == 3:
                        sum_gemv()
                    if kh == n_kh - 1 and m:
                        i, ps, ready_mark = banks[m - 1]
                        bank_free[i] = evac(4 * group + m - 1, ps, ready_mark)
                    pump(fills[kh == n_kh - 1], keep, int(not keep))
                hl_free[t] = done
            i, ps, ready_mark = banks[3]
            bank_free[i] = evac(4 * group + 3, ps, ready_mark)
            for m, b in enumerate(banks2):
                bank_free[b[0]] = evac2(2 * group + m, b[1], b[3])

        def gemm(*args, **more):
            for _ in gemm_steps(*args, **more):
                pass

        y = [at(f"y{i}", 84 + i, [P, T]) for i in range(DT)]
        tmpf = [at(f"tmp{i}", 92 + i, [P, T]) for i in range(8)]
        sq_ring = [tmpf[0][:, :], tmpf[1][:, :]]
        sq_free = [None, None]
        rstd = tmpf[2][:, :]
        mod_tmp = [t[:, :] for t in tmpf[3:7]]
        ssum = tmpf[7][:, :]

        def mean_square(tiles, marks, sq_ring, sq_free, n_tok, scale, rstd, rstd_free, pooled=True):
            act.quiet(lambda e: e.preload_act_table_set("natural_log_exp_and_others"))
            i, ps = take_bank()
            last = len(tiles) - 1
            m_sum = None
            for n, tl in enumerate(tiles):
                r = n % 2
                act.wait(marks[n], sq_free[r])
                on_pool = pooled and r == 0
                sq = ssum if on_pool and n == 0 else sq_ring[r]
                m = act.do(lambda e: e.activation(sq, tl, ACT.Square))
                if on_pool:
                    if n:
                        pool.wait(m, m_sum)
                        m = sq_free[r] = pool.do(lambda e: e.tensor_tensor(ssum, ssum, sq, ALU.add))
                    m_sum = m
                    continue
                if pooled and n == last:
                    pe.wait(m_sum)
                    pe.do(lambda e: e.matmul(ps[:, 0:n_tok], ones[:, :], ssum, start=False, stop=False))
                pe.wait(m, m_ones[0])
                sq_free[r] = pe.do(lambda e: e.matmul(ps[:, 0:n_tok], ones[:, :], sq, start=n == int(pooled),
                                                      stop=n == last))
            if pooled:
                prefetch()
            act.wait(sq_free[r], rstd_free, *m_ones)
            m = act.do(lambda e: e.activation(rstd, ps[:, 0:n_tok], ACT.Ln, bias=eps_col, scale=scale))
            bank_free[i] = [m]
            act.wait(m)
            return act.do(lambda e: e.activation(rstd, rstd, ACT.Exp, scale=-0.5))


        def add_square(n, tile, mark, war):
            r = n % 2
            act.wait(mark, sq_free[r], *war)
            m = act.do(lambda e: e.activation(sq_ring[r], tile, ACT.Square))
            pool.wait(m, *war)
            if n == 0:
                sq_free[r] = pool.do(lambda e: e.tensor_copy(ssum, sq_ring[r]))
            else:
                pool.wait(sq_free[(n - 1) % 2])
                sq_free[r] = pool.do(lambda e: e.tensor_tensor(ssum, ssum, sq_ring[r], ALU.add))
            return sq_free[r]

        def finish_square(m_sum, scale):
            act.quiet(lambda e: e.preload_act_table_set("natural_log_exp_and_others"))
            i, ps = take_bank()
            pe.wait(m_sum)
            m = pe.do(lambda e: e.matmul(ps[:, :], ones[:, :], ssum, start=True, stop=True))
            act.wait(m, *m_ones)
            m = act.do(lambda e: e.activation(rstd, ps[:, :], ACT.Ln, bias=eps_col, scale=scale))
            bank_free[i] = [m]
            act.wait(m)
            return act.do(lambda e: e.activation(rstd, rstd, ACT.Exp, scale=-0.5))

        def modulate(tiles, marks, rstd, m_rstd, s, sh, m_s, tmp, tmp_free, hi, lo, war):
            got = []
            for n, tl in enumerate(tiles):
                r = n % len(tmp)
                dve.wait(marks[n], m_rstd, m_s, tmp_free[r])
                m1 = dve.do(lambda e, tl=tl, r=r, n=n: e.scalar_tensor_tensor(tmp[r], tl, s[:, n:n + 1], rstd,
                                                                              ALU.mult, ALU.mult))
                act.wait(m1, *war)
                m2 = act.do(lambda e, r=r, n=n: e.activation(hi[n], tmp[r], ACT.Identity, bias=sh[:, n:n + 1]))
                got.append((m2, r, n))
                if n >= 1:
                    got[n - 1] = lo_part(got[n - 1], tmp, sh, hi, lo, tmp_free, war)
            got[-1] = lo_part(got[-1], tmp, sh, hi, lo, tmp_free, war)
            return got

        def lo_part(g, tmp, sh, hi, lo, tmp_free, war):
            m2, r, n = g
            dve.wait(m2, *war)
            m3 = dve.do(lambda e: e.scalar_tensor_tensor(lo[n], tmp[r], sh[:, n:n + 1], hi[n].bitcast(F32),
                                                         ALU.add, ALU.subtract))
            tmp_free[r] = m3
            return (hi[n], lo[n], m3)

        def scale_columns(dst, g, sc, mark):
            dve.wait(mark)
            m = dve.do(lambda e: e.tensor_scalar(dst, sc, 1.0, None, ALU.add))
            dve.wait(m)
            return dve.do(lambda e: e.tensor_tensor(dst, dst, g, ALU.mult))

        def gate_columns(dst, g, gt, mark):
            dve.wait(mark)
            return dve.do(lambda e: e.tensor_tensor(dst, gt, g, ALU.mult))

        def split(src, hi, lo, marks, war=(), queue=None):
            act.wait(*marks, *war)
            m = act.do(lambda e: e.activation(hi, src, ACT.Copy))
            queue = queue or dve
            queue.wait(m, *marks, *war)
            return queue.do(lambda e: e.tensor_tensor(lo, src, hi.bitcast(F32), ALU.subtract))

        exp_table = [False]

        def ln_exp_table(wanted=True):
            if wanted and not exp_table[0]:
                act.quiet(lambda e: e.preload_act_table_set("natural_log_exp_and_others"))
            exp_table[0] = wanted

        x_spill = nc.dram_tensor("x_spill", (D, T), F32, kind="Internal").ap().rearrange("(n p) t -> p n t", p=P)
        land_spill, land_back = Landing(sem("x_spilled")), Landing(sem("x_back"))

        def residual(tiles, marks, g, m_g, rstd, m_rstd, x_old, x_marks):
            res, prod = [], []
            for n in range(DT):
                dve.wait(marks[n], m_rstd, m_g)
                prod.append(dve.do(lambda e, n=n: e.scalar_tensor_tensor(tiles[n], tiles[n], g[:, n:n + 1], rstd,
                                                                         ALU.mult, ALU.mult)))
                if n >= 1:
                    k = n - 1
                    dve.wait(prod[k], x_marks[k])
                    res.append(dve.do(lambda e, k=k: e.tensor_tensor(x[k], x_old[k], tiles[k], ALU.add)))
            dve.wait(prod[-1], x_marks[-1])
            res.append(dve.do(lambda e: e.tensor_tensor(x[DT - 1], x_old[DT - 1], tiles[DT - 1], ALU.add)))
            return res

        h_hi = [at(f"h_hi{i}", 35 + i, [P, T], F32R) for i in range(DT)]
        h_lo = [at(f"h_lo{i}", 43 + i, [P, T], F32R) for i in range(DT)]
        x_ap = [t[:, :] for t in x]
        y_ap = [t[:, :] for t in y]
        full = lambda tiles: [t[:, :] for t in tiles]

        a_pad = [at(f"a_pad{i}", 51, [P, CONV_G - 1 + T], part=(CONV_G + 1 + T) * i) for i in range(DT)]
        conv_acc = [at(f"conv_acc{i}", 24 + i, [P, T]) for i in range(DT)]
        tap_prod = at("tap_product", 99, [P, T])
        sig_b = [at(f"sig_b{i}", 88 + i, [P, T]) for i in range(4)]
        xm = [(at(f"xm_hi{i}", 60 + i, [P, T], F32R), at(f"xm_lo{i}", 64 + i, [P, T], F32R)) for i in range(4)]
        xc = [(at(f"xc_hi{i}", 68 + i, [P, T], F32R), at(f"xc_lo{i}", 72 + i, [P, T], F32R)) for i in range(4)]
        x_f = [at(f"x_m_f{i}", 96 + i, [P, T]) for i in range(3)]
        acc4 = [at(f"acc4_{i}", 92 + i, [P, T]) for i in range(4)]
        sig_z = [at(f"sig_z{i}", 88 + i, [P, T]) for i in range(DT)]
        q_slot = lambda h, m: (76 if h < 2 else 35) + 2 * (h % 2) + m
        qkv = {(s, h, m): at(f"{'qkv'[s]}{h}{m}", q_slot(h, m) + 4 * s, [P, T])
               for s in range(3) for h in range(HEADS) for m in range(2)}
        hm_hi = [at(f"hm_hi{n}", q_slot(n // 2, n % 2) + 4, [P, T], F32R) for n in range(DT)]
        hm_lo = [at(f"hm_lo{n}", q_slot(n // 2, n % 2), [P, T], F32R) for n in range(DT)]
        wg = at("w_gates_sb", 59, [P, 6, 32], part=256)
        a_hi = [at(f"a_hi{i}", 51, [P, T], F32R, part=(CONV_G + 1 + T) * i) for i in range(DT)]
        a_lo = [at(f"a_lo{i}", 24 + i, [P, T], F32R) for i in range(DT)]
        a_sq = [at(f"a_sq{i}", 60 + i, [P, T]) for i in range(2)]
        a_rstd = [at(f"a_rstd{i}", 62 + i, [P, T]) for i in range(2)]
        x_old = at("x_old", 60, [P, DT, T])
        g8 = at("gates", 75, [8, T])
        row_t, row_lf, row_ones = (at(n, s, [4, T]) for n, s in (("row_t", 96), ("row_lf", 97), ("row_ones", 98)))
        row_negm, row_em = at("row_negm", 100, [4, T]), at("row_em", 75, [4, T])
        row_b, row_c = at("row_b", 101, [4, T]), at("row_c", 102, [4, T])
        c_col = misc[:, 48:64]
        v_t2 = [at(f"v_t{i}", 47 + 2 * i, [P, N_CH, HEAD_D]) for i in range(2)]
        pt2 = [[at(f"p_t{i}{j}", (96, 66)[i], [P, T - P * j], part=sum(T - P * n for n in range(j)))
                for j in range(N_CH)] for i in range(2)]
        negm_bc, diag = at("negm_bc", 101, [P, T]), at("diag", 102, [P, T])
        den2 = [at(f"den{i}", 70 + i, [P, T]) for i in range(2)]
        hm_sq2 = [[at(f"hm_sq{i}{m}", (72, 64)[i] + m, [P, T]) for m in range(2)] for i in range(2)]
        hm_rstd2 = [at(f"hm_rstd{i}", (74, 69)[i], [P, T]) for i in range(2)]
        land_wg = Landing(sem("w_gates_landed"))

        f1 = [[(at(f"f1_hi{b}{i}", 51 + 16 * b + i, [P, T], F32R), at(f"f1_lo{b}{i}", 59 + 16 * b + i, [P, T], F32R))
               for i in range(QUARTER)] for b in range(2)]

        def finish_conv(p, i, m_acc, ring_free, normed, out):
            acc, r = conv_acc[i][:, :], i % 2
            yield
            b, ps = take_bank()
            pe.wait(m_acc[i], m_ones[0])
            m = pe.do(lambda e: e.matmul(ps[:, :], ones[:, :], acc, start=True, stop=True))
            dve.wait(m)
            m = dve.do(lambda e: e.scalar_tensor_tensor(acc, ps[:, :], -1.0 / P, acc, ALU.mult, ALU.add))
            bank_free[b] = [m]
            act.wait(m, ring_free[r])
            m = act.do(lambda e: e.activation(a_sq[r][:, :], acc, ACT.Square))
            yield
            b, ps2 = take_bank()
            pe.wait(m)
            m = pe.do(lambda e: e.matmul(ps2[:, :], ones[:, :], a_sq[r][:, :], start=True, stop=True))
            ln_exp_table()
            act.wait(m)
            m = act.do(lambda e: e.activation(a_rstd[r][:, :], ps2[:, :], ACT.Ln, bias=eps_col, scale=1.0 / P))
            bank_free[b] = [m]
            act.wait(m)
            m = act.do(lambda e: e.activation(a_rstd[r][:, :], a_rstd[r][:, :], ACT.Exp, scale=-0.5))
            dve.wait(m)
            m = dve.do(lambda e: e.scalar_tensor_tensor(acc, acc, p[:, G_CN + i:G_CN + i + 1], a_rstd[r][:, :],
                                                        ALU.mult, ALU.mult))
            ring_free[r] = m
            normed.add(i)
            yield
            act.wait(m)
            m = act.do(lambda e: e.activation(acc, acc, ACT.Silu, bias=p[:, B_CN + i:B_CN + i + 1]))
            ln_exp_table(False)
            m = split(acc, a_hi[i][:, :], a_lo[i][:, :], [m], (), pool)
            yield
            yield
            out[i] = (a_hi[i][:, :], a_lo[i][:, :], m)

        def weave(queues):
            running = [[] for _ in queues]
            while any(running) or any(waiting for _, _, waiting in queues):
                for n, (limit, steps, waiting) in enumerate(queues):
                    while waiting and len(running[n]) < limit and waiting[0][0]():
                        running[n].append(waiting.popleft()[1])
                    for g in list(running[n]):
                        for _ in range(steps):
                            if next(g, StopIteration) is StopIteration:
                                running[n].remove(g)
                                break
                    pump(1)

        def layer(l, m_x, m_rstd=None):
            p = par[l]
            flush_gemv()
            m_s = scale_columns(s_mix[l], p[:, G_PRE_MIX:G_PRE_MIX + 8], mod[l][:, 8:16], m_mod[f"ada{l}", 0])
            m_r = m_rstd or mean_square(x_ap, m_x, sq_ring, sq_free, T, 1.0 / D, rstd, None)
            tmp_free = [None] * 4
            h = modulate(x_ap, m_x, rstd, m_r, s_mix[l], mod[l][:, 0:8], m_s, mod_tmp, tmp_free,
                         full(h_hi), full(h_lo), m_x)

            act.wait(*m_x)
            m_spill = land_spill.load(act, x_spill, x_all[:, :, :])
            m_wg = land_wg.load(act, wg[:, :, :],
                                A["w_gates"][l].rearrange("(n p h) g -> p n (h g)", p=P, h=HEADS))

            dve.wait(*m_x)
            for i in range(DT):
                m_pad = dve.do(lambda e, i=i: e.memset(a_pad[i][:, 0:CONV_G - 1], 0.0))
            m_a, m_acc, prod_free = {}, {}, [None]
            sig = {}

            conv_whole = set()

            def vector_tap(i, k):
                w = p[:, W_DW + 8 * k + i:W_DW + 8 * k + i + 1]
                src, acc = a_pad[i][:, k:k + T], conv_acc[i][:, :]
                if k == 0:
                    dve.wait(m_a[i], m_pad, m_spill, h[-1][2], *m_parl)
                    m_acc[i] = dve.do(lambda e: e.tensor_scalar(acc, src, w, p[:, B_DW + i:B_DW + i + 1],
                                                                ALU.mult, ALU.add))
                else:
                    dve.wait(m_acc[i])
                    m_acc[i] = dve.do(lambda e: e.scalar_tensor_tensor(acc, src, w, acc, ALU.mult, ALU.add))
                if k == CONV_G - 1:
                    conv_whole.add(i)

            def pool_tap(i, k):
                w = p[:, W_DW + 8 * k + i:W_DW + 8 * k + i + 1]
                src, acc, prod = a_pad[i][:, k:k + T], conv_acc[i][:, :], tap_prod[:, :]
                if k == 0:
                    act.wait(m_a[i], m_pad, m_spill, h[-1][2], *m_parl)
                    m_acc[i] = act.do(lambda e: e.activation(acc, src, ACT.Identity, scale=w,
                                                             bias=p[:, B_DW + i:B_DW + i + 1]))
                else:
                    act.wait(prod_free[0])
                    m = act.do(lambda e: e.activation(prod, src, ACT.Copy, scale=w))
                    pool.wait(m, m_acc[i])
                    prod_free[0] = m_acc[i] = pool.do(lambda e: e.tensor_tensor(acc, acc, prod, ALU.add))
                if k == CONV_G - 1:
                    conv_whole.add(i)

            def taps(tap, tiles):
                return [lambda i=i, k=k: tap(i, k) for k in range(CONV_G) for i in tiles]

            def glu_b_evac(n, ps, done):
                act.wait(done, m_a.get(n - 4))
                sig[n] = act.do(lambda e: e.activation(sig_b[n % 4][:, :], ps[:, :], ACT.Sigmoid))
                return [sig[n]]

            def glu_a_evac(n, ps, done):
                dve.wait(done, sig[n], m_pad)
                m_a[n] = dve.do(lambda e: e.tensor_tensor(a_pad[n][:, CONV_G - 1:], ps[:, :], sig_b[n % 4][:, :],
                                                          ALU.mult))
                return [m_a[n]]

            for half in range(2):
                gemm(f"glu_b{l}{half}", 0, DT, h, lambda n, ps, done: glu_b_evac(4 * half + n, ps, done))
                gemm(f"glu_a{l}{half}", 0, DT, h, lambda n, ps, done: glu_a_evac(4 * half + n, ps, done))
                if half == 0:
                    fill.extend(taps(vector_tap, (0, 1)) + taps(vector_tap, (2, 3)))
                else:
                    fill.extend(taps(vector_tap, (4, 5, 6)))
                    pool_fill.extend(taps(pool_tap, (7,)))

            m_xm, m_xc, m_qkv = [None] * 4, [None] * 4, {}
            xf_free, xm_read, xc_done = [None] * 3, [None] * 3, {}
            dve.wait(h[-1][2])

            def x_m_evac(n, ps, done, war):
                j, r = n % 4, n % 3
                hi, lo, xf, acc = xm[j][0][:, :], xm[j][1][:, :], x_f[r][:, :], acc4[j][:, :]
                act.wait(done, xf_free[r], xm_read[r], *war)
                m_hi = act.do(lambda e: e.activation(hi, ps[:, :], ACT.Copy))
                m_f = act.do(lambda e: e.activation(xf, ps[:, :], ACT.Copy))
                dve.wait(m_f, xc_done.get(n - 4))
                for k in range(CONV_M - 1, -1, -1):
                    w = p[:, W_CONV_M + 8 * k + n:W_CONV_M + 8 * k + n + 1]
                    back = CONV_M - 1 - k
                    if back == 0:
                        m = dve.do(lambda e: e.tensor_scalar(acc, xf, w, None, ALU.mult))
                        pool.wait(m_hi, m_f, *war)
                        m_xm[j] = pool.do(lambda e: e.tensor_tensor(lo, xf, hi.bitcast(F32), ALU.subtract))
                    else:
                        dve.wait(m)
                        m = dve.do(lambda e: e.scalar_tensor_tensor(acc[:, back:], xf[:, 0:T - back], w,
                                                                    acc[:, back:], ALU.mult, ALU.add))
                xf_free[r], xm_read[r] = m, m_xm[j]

                def activate():
                    act.wait(m)
                    m2 = act.do(lambda e: e.activation(acc, acc, ACT.Silu, bias=p[:, B_CONV_M + n:B_CONV_M + n + 1]))
                    m_xc[j] = xc_done[n] = split(acc, xc[j][0][:, :], xc[j][1][:, :], [m2], war)

                later.append(activate)
                return [m_f]

            m_z = {}

            def z_evac(n, ps, done):
                act.wait(done, m_a[7], xc_done[n] if n >= 4 else None)
                m_z[n] = act.do(lambda e: e.activation(sig_z[n][:, :], ps[:, :], ACT.Sigmoid))
                return [m_z[n]]

            war = []
            for half in range(2):
                gemm(f"x_m{l}{half}", 0, DT, h, lambda n, ps, done: x_m_evac(4 * half + n, ps, done, war),
                     fills=(3, 1), keep=1)
                gemm(f"z{l}{half}", 0, DT, h, lambda n, ps, done: z_evac(4 * half + n, ps, done))
                for head in (2 * half, 2 * half + 1):
                    while (f"qkv{l}", head, 0) not in ready:
                        prepare(nxt_prep[0] + 1)
                    t, m_w = ready.pop((f"qkv{l}", head, 0))
                    while nxt_prep[0] < len(plan) and not ready:
                        prepare(nxt_prep[0] + 1)
                    pe.wait(m_w)
                    for s in (2, 0, 1):
                        src, marks = (xm, m_xm) if s == 2 else (xc, m_xc)
                        for m in range(2):
                            b, ps = take_bank()
                            for k in range(2):
                                j = 2 * (head % 2) + k
                                pe.wait(marks[j])
                                c0 = 512 * s + 256 * k + P * m
                                done = products(ps[:, :], w_hi[t][:, c0:c0 + P], w_lo[t][:, c0:c0 + P],
                                                src[j][0][:, :], src[j][1][:, :], k == 0, k == 1, k == 1)
                            dst = qkv[s, head, m][:, :]
                            if m:
                                act.wait(done)
                                mk = act.do(lambda e, dst=dst, ps=ps: e.activation(dst, ps[:, :], ACT.Copy))
                            else:
                                dve.wait(done)
                                mk = dve.do(lambda e, dst=dst, ps=ps: e.tensor_copy(dst, ps[:, :]))
                            bank_free[b] = [mk]
                            m_qkv[s, head, m] = mk
                    hl_free[t] = done
                    pump(6)
                    pump(0)
                war = [done]

            def run_head(head):
                r = head % 2
                war = gates_read + head_end.get(head - 2, [])
                v_t, pt, den, hm_sq, hm_rstd = v_t2[r], pt2[r], den2[r], hm_sq2[r], hm_rstd2[r]
                sel = ident[0:4, head:head + 1].to_broadcast([4, P])
                for jj in range(2):
                    b, ps = take_bank()
                    for j in (2 * jj, 2 * jj + 1):
                        for m in range(2):
                            pe.wait(m_qkv[2, head, m], m_ident)
                            mt = pe.do(lambda e: e.transpose(
                                ps[:, (2 * (j - 2 * jj) + m) * P:(2 * (j - 2 * jj) + m + 1) * P],
                                qkv[2, head, m][:, j * P:(j + 1) * P], ident[:, :]))
                    act.wait(mt, *war)
                    m_vt = act.do(lambda e: e.activation(
                        v_t[:, 2 * jj:2 * jj + 2, :], ps[:, :].rearrange("p (j n) -> p j n", j=2), ACT.Copy))
                    bank_free[b] = [m_vt]
                yield
                score_banks = [take_bank() for _ in range(3)]
                scores = [score_banks[b][1][:, c0:c0 + T - j * P] for j, (b, c0) in
                          enumerate(((0, 0), (1, 0), (2, 0), (1, T - P)))]
                m_s = []
                for j in range(N_CH):
                    for m in range(2):
                        pe.wait(m_qkv[0, head, m], m_qkv[1, head, m])
                        ms = pe.do(lambda e: e.matmul(
                            scores[j], qkv[1, head, m][:, j * P:(j + 1) * P], qkv[0, head, m][:, j * P:],
                            start=m == 0, stop=m == 1))
                    m_s.append(ms)
                if head == 0:
                    yield
                war = war + rows_done
                b, ps = take_bank()
                pe.wait(m_nm)
                m = pe.do(lambda e: e.matmul(ps[:, :], sel, row_negm[:, :], start=True, stop=True))
                act.wait(m, bc_free[0], *war)
                m_bc = act.do(lambda e: e.activation(negm_bc[:, :], ps[:, :], ACT.Copy))
                bank_free[b] = [m_bc]
                pool.wait(m_bc, *war)
                m_dg = pool.do(lambda e: e.affine_select(
                    out=diag[:, :].rearrange("p (j t) -> p j t", j=N_CH),
                    in_=negm_bc[:, :].rearrange("p (j t) -> p j t", j=N_CH), compare_op=ALU.is_ge, fill=NEG, base=0,
                    pattern=[[0, N_CH], [1, P]], channel_multiplier=-1))
                ln_exp_table()
                m_e = []
                act.wait(m_bc)
                for j in range(N_CH):
                    cj = c_col[:, 4 * j + head:4 * j + head + 1]
                    if j < N_CH - 1:
                        act.do(lambda e: e.activation(pt[j][:, P:], negm_bc[:, (j + 1) * P:], ACT.Exp, bias=cj))
                act.wait(m_dg)
                for j in range(N_CH):
                    cj = c_col[:, 4 * j + head:4 * j + head + 1]
                    m_e.append(act.do(lambda e: e.activation(pt[j][:, 0:P], diag[:, j * P:(j + 1) * P],
                                                             ACT.Exp, bias=cj)))
                bc_free[0] = m_e[-1]
                m_p = []
                for j in range(N_CH):
                    dve.wait(m_s[j], m_e[j])
                    m_p.append(dve.do(lambda e: e.scalar_tensor_tensor(
                        pt[j][:, :], scores[j], float(HEAD_D) ** -0.5, pt[j][:, :], ALU.mult, ALU.mult)))
                for b, _ in score_banks:
                    bank_free[b] = [m_p[-1]]
                yield
                b_den, ps_den = take_bank()
                for j in range(N_CH):
                    pe.wait(m_p[j])
                    m_den = pe.do(lambda e: e.matmul(ps_den[:, j * P:], ones[:, :], pt[j][:, :],
                                                     start=j == 0, stop=j == N_CH - 1))
                b_em, ps_em = take_bank()
                pe.wait(m_em)
                m_emb = pe.do(lambda e: e.matmul(ps_em[:, :], sel, row_em[:, :], start=True, stop=True))
                act.wait(m_den, *war)
                m = act.do(lambda e: e.activation(den[:, :], ps_den[:, :], ACT.Abs))
                bank_free[b_den] = [m]
                dve.wait(m, m_emb)
                m = dve.do(lambda e: e.tensor_tensor(den[:, :], den[:, :], ps_em[:, :], ALU.max))
                bank_free[b_em] = [m]
                dve.wait(m)
                m_rec = dve.do(lambda e: e.reciprocal(den[:, :], den[:, :]))
                hm = [qkv[0, head, m][:, :] for m in range(2)]
                m_h = []
                pe.wait(m_vt)
                for m in range(2):
                    b, ps = take_bank()
                    for j in range(N_CH):
                        mv = pe.do(lambda e: e.matmul(ps[:, j * P:], v_t[:, j, m * P:(m + 1) * P], pt[j][:, :],
                                                      start=j == 0, stop=j == N_CH - 1))
                    dve.wait(mv, m_rec)
                    mk = dve.do(lambda e: e.tensor_tensor(hm[m], ps[:, :], den[:, :], ALU.mult))
                    bank_free[b] = [mk]
                    m_h.append(mk)
                yield
                b, ps = take_bank()
                for m in range(2):
                    pe.wait(m_h[m])
                    mm = pe.do(lambda e: e.matmul(ps[:, :], ones[:, :], hm[m], start=m == 0, stop=m == 1))
                m_sq = []
                for m in range(2):
                    dve.wait(mm, m_h[m])
                    m_h[m] = dve.do(lambda e: e.scalar_tensor_tensor(hm[m], ps[:, :], -1.0 / HEAD_D, hm[m],
                                                                     ALU.mult, ALU.add))
                    act.wait(m_h[m], *war)
                    m_sq.append(act.do(lambda e: e.activation(hm_sq[m][:, :], hm[m], ACT.Square)))
                bank_free[b] = [m_h[1]]
                yield
                b, ps = take_bank()
                for m in range(2):
                    pe.wait(m_sq[m])
                    m_v = pe.do(lambda e: e.matmul(ps[:, :], ones[:, :], hm_sq[m][:, :], start=m == 0, stop=m == 1))
                ln_exp_table()
                act.wait(m_v)
                mk = act.do(lambda e: e.activation(hm_rstd[:, :], ps[:, :], ACT.Ln, bias=eps_col, scale=1.0 / HEAD_D))
                bank_free[b] = [mk]
                act.wait(mk)
                m_rs = act.do(lambda e: e.activation(hm_rstd[:, :], hm_rstd[:, :], ACT.Exp, scale=-0.5))
                for m in range(2):
                    n = 2 * head + m
                    dve.wait(m_rs, m_h[m])
                    mk = dve.do(lambda e: e.scalar_tensor_tensor(
                        hm[m], hm[m], p[:, G_MH + n:G_MH + n + 1], hm_rstd[:, :], ALU.mult, ALU.mult))
                    dve.wait(mk, m_z[n])
                    mk = dve.do(lambda e: e.tensor_tensor(hm[m], hm[m], sig_z[n][:, :], ALU.mult))
                    m_hm[n] = split(hm[m], hm_hi[n][:, :], hm_lo[n][:, :], [mk], (), pool)
                head_end[head] = [mk, m_rs, m_v, mv]
                yield
                for n in (2 * head, 2 * head + 1):
                    mix[DT + n] = (hm_hi[n][:, :], hm_lo[n][:, :], m_hm[n])

            pump(20)
            b, ps = take_bank()
            first = True
            for s in range(3):
                for m in range(2):
                    for head in range(HEADS):
                        pe.wait(m_qkv[s, head, m], m_wg)
                        step = lambda e, s=s, m=m, head=head, st=first: e.matmul(
                            ps[0:8, :], wg[:, 2 * s + m, 8 * head:8 * head + 8], qkv[s, head, m][:, :],
                            start=st, stop=(s, m, head) == (2, 1, HEADS - 1))
                        first = False
                        if (s, m, head) == (2, 1, HEADS - 1):
                            done = pe.do(step)
                        else:
                            pe.quiet(step)
            act.wait(done, m_par2)
            m_g8 = act.do(lambda e: e.activation(g8[:, :], ps[0:8, :], ACT.Identity, bias=gate_bias[l]))
            bank_free[b] = [m_g8]
            flush_gemv()
            exp_table[0] = False
            ln_exp_table()
            prefetch()
            gates_read = [done]
            m_hm, head_end, rows_done = {}, {}, []
            bc_free = [None]
            heads = [run_head(head) for head in range(HEADS)]
            next(heads[0])
            b, ps_f = take_bank()
            pe.wait(m_g8)
            m_f = pe.do(lambda e: e.matmul(ps_f[0:4, :], ident[0:8, 4:8], g8[:, :], start=True, stop=True))
            act.wait(m_f, (dve.sem, dve.count))
            m = act.do(lambda e: e.activation(row_t[:, :], ps_f[0:4, :], ACT.Abs))
            act.wait(m)
            m = act.do(lambda e: e.activation(row_t[:, :], row_t[:, :], ACT.Exp, scale=-1.0))
            act.wait(m)
            m = act.do(lambda e: e.activation(row_t[:, :], row_t[:, :], ACT.Ln, bias=one_col[0:4, :]))
            next(heads[0])
            next(heads[1])
            dve.wait(m_f, m, part_free[0], *gemv_free.values())
            m_o = dve.do(lambda e: e.memset(row_ones[:, :], 1.0))
            m2 = dve.do(lambda e: e.tensor_scalar(row_lf[:, :], ps_f[0:4, :], 0.0, None, ALU.min))
            bank_free[b] = [m2, m]
            dve.wait(m2)
            m = dve.do(lambda e: e.tensor_tensor(row_lf[:, :], row_lf[:, :], row_t[:, :], ALU.subtract))
            dve.wait(m, m_o)
            m = dve.do(lambda e: e.tensor_tensor_scan(row_b[:, :], row_ones[:, :], row_lf[:, :], 0.0, ALU.mult, ALU.add))
            dve.wait(m)
            m_c = dve.do(lambda e: e.tensor_tensor(row_c[:, :], g8[0:4, :], row_b[:, :], ALU.subtract))
            dve.wait(m_c)
            m = dve.do(lambda e: e.tensor_tensor_scan(row_t[:, :], row_ones[:, :], row_c[:, :], 0.0, ALU.mult, ALU.max))
            dve.wait(m)
            m_nm = dve.do(lambda e: e.tensor_scalar(row_negm[:, :], row_t[:, :], -1.0, None, ALU.mult))
            m = dve.do(lambda e: e.tensor_tensor(row_em[:, :], row_b[:, :], row_t[:, :], ALU.add))
            act.wait(m)
            m_em = act.do(lambda e: e.activation(row_em[:, :], row_em[:, :], ACT.Exp, scale=-1.0))
            b, ps = take_bank()
            pe.wait(m_c)
            for j in range(N_CH):
                m = pe.do(lambda e, j=j: e.transpose(ps[:, 4 * j:4 * j + 4], row_c[:, j * P:(j + 1) * P],
                                                     ident[0:4, 0:4]))
            dve.wait(m)
            m_cc = dve.do(lambda e: e.tensor_copy(c_col, ps[:, 0:4 * N_CH]))
            bank_free[b] = [m_cc]

            rows_done += [m_nm, m_em, m_cc]
            ring_free, normed = list(gates_read) * 2, set()
            mix = {}

            def y_evac(n, ps, done):
                act.wait(done, *m_hm.values())
                m_y[n] = act.do(lambda e: e.activation(y[n][:, :], ps[:, :], ACT.Copy))
                m_sum[0] = add_square(n, y[n][:, :], m_y[n], [*m_hm.values()])
                return [m_y[n]]

            m_sum, m_y = [None], [None] * DT
            weave([(2, 1, deque((lambda: True, head) for head in heads)),
                   (4, 1, deque((lambda i=i: i in conv_whole and (i < 2 or i - 2 in normed),
                                 finish_conv(p, i, m_acc, ring_free, normed, mix))
                                for i in range(DT))),
                   (1, 3, deque([(lambda: 3 in mix, gemm_steps(f"w_out{l}", 0, 2 * DT, mix, y_evac))]))])
            act.wait(*m_hm.values(), *ring_free, *[mix[i][2] for i in range(DT)], m_spill)
            m_back = land_back.load(act, x_old[:, :, :], x_spill)
            gemm(f"w_out{l}", 1, 2 * DT, mix, y_evac)
            flush_gemv()
            m_g = gate_columns(g_mixo[l], p[:, G_POST_MIX:G_POST_MIX + 8], mod[l][:, 16:24], m_mod[f"ada{l}", 0])
            m_s = scale_columns(s_mlp[l], p[:, G_PRE_MLP:G_PRE_MLP + 8], mod[l][:, 32:40], m_mod[f"ada{l}", 0])
            m_r = finish_square(m_sum[0], 1.0 / D)
            m_x = residual(y_ap, m_y, g_mixo[l], m_g, rstd, m_r, [x_old[:, n, :] for n in range(DT)], [m_back] * DT)
            m_r = mean_square(x_ap, m_x, sq_ring, sq_free, T, 1.0 / D, rstd, m_x[-1])
            h = modulate(x_ap, m_x, rstd, m_r, s_mlp[l], mod[l][:, 24:32], m_s, mod_tmp, tmp_free,
                         full(h_hi), full(h_lo), m_x)

            hidden = [[None] * QUARTER for _ in range(2)]
            t_free = [None] * 2
            m_yq = [None] * DT

            def up_evac(b, n, ps, done):
                r = n % 2
                t1, t2 = tmpf[3 + r][:, :], tmpf[5 + r][:, :]
                hi, lo = (t[:, :] for t in f1[b][n])
                act.wait(done, t_free[r])
                m1 = act.do(lambda e: e.activation(t1, ps[:, :], ACT.Relu))
                dve.wait(m1, t_free[r])
                m2 = dve.do(lambda e: e.tensor_tensor(t2, t1, t1, ALU.mult))
                act.wait(m1)
                m3 = act.do(lambda e: e.activation(hi, t1, ACT.Square))
                dve.wait(m2, m3)
                t_free[r] = dve.do(lambda e: e.tensor_tensor(lo, t2, hi.bitcast(F32), ALU.subtract))
                hidden[b][n] = (hi, lo, t_free[r])
                return [m1]

            def down_evac(q, n, ps, done):
                if q == 0:
                    act.wait(done, *m_x)
                    m_yq[n] = act.do(lambda e: e.activation(y[n][:, :], ps[:, :], ACT.Copy))
                else:
                    dve.wait(done, m_yq[n])
                    m_yq[n] = dve.do(lambda e: e.tensor_tensor(y[n][:, :], y[n][:, :], ps[:, :], ALU.add))
                if q == 3:
                    m_sum[0] = add_square(n, y[n][:, :], m_yq[n], [h[-1][2]])
                return [m_yq[n]]

            for step in ("up0", "up1", "down0", "up2", "down1", "up3", "down2", "down3"):
                q = int(step[-1])
                for g in range(2):
                    if step[:2] == "up":
                        gemm(f"{step}_{l}", g, DT, h, lambda n, ps, done: up_evac(q % 2, n, ps, done))
                    else:
                        gemm(f"{step}_{l}", g, DT, hidden[q % 2], lambda n, ps, done: down_evac(q, n, ps, done))
            m_g = gate_columns(g_mlpo[l], p[:, G_POST_MLP:G_POST_MLP + 8], mod[l][:, 40:48], m_mod[f"ada{l}", 0])
            m_r = finish_square(m_sum[0], 1.0 / D)
            return residual(y_ap, m_yq, g_mlpo[l], m_g, rstd, m_r, x, m_x)

        def second(m_x):
            flush_gemv()
            hc_hi = [at(f"hc_hi{i}", 51, [P, CTX], F32R, part=CTX * i) for i in range(DT)]
            hc_lo = [at(f"hc_lo{i}", 55, [P, CTX], F32R, part=CTX * i) for i in range(DT)]
            q2 = [at(f"q2_{i}", 59 + i, [P, T]) for i in range(DT)]
            k2 = [at(f"k2_{i}", 67 + i, [P, T]) for i in range(DT)]
            vw = at("v_windows", 75, [P, 2 * N_CH, D])
            kc = at("k_ctx", 91, [P, DT, CTX])
            vc = at("v_ctx", 95, [P, 2, D])
            sgb = [at(f"sig_gb{i}", 24 + i, [P, T]) for i in range(DT)]
            c_tok = at("ctx_tok", 67, [P, CTX // P, D])
            c_f = [at(f"ctx_f{i}", 71, [P, CTX], part=CTX * i) for i in range(DT)]
            csq = [at(f"ctx_sq{i}", 84, [P, CTX], part=CTX * i)[:, :] for i in range(2)]
            c_rstd = at("ctx_rstd", 85, [P, CTX])
            c_tmp = [at(f"ctx_tmp{i}", 86, [P, CTX], part=CTX * i)[:, :] for i in range(4)]
            rope = at("rope", 75, [P, 2, T])
            raw_t = [at(f"rope_in{i}", 77 + i, [P, T]) for i in range(3)]
            rot_t = [at(f"rope_rot{i}", 80 + i, [P, T]) for i in range(3)]
            v_f = at("v_f", 99, [P, N_CH, ROWS, K_COLS])
            vc_f = [at(f"v_ctx_f{i}", 101 + i, [P, 2 * CTX]) for i in range(2)]
            rot = at("rotation", 103, [P, P], part=320)
            mask = at("mask", 51, [P, 3, ROWS * K_COLS])
            bias = [at(f"bias{i}", 52, [P, 3, ROWS * K_COLS], part=256 + 768 * i) for i in range(2)]
            toep = [at(f"toeplitz{i}", 55, [P, ROWS, TOEP], part=256 + ROWS * TOEP * i) for i in range(2)]
            pr = [at(f"prob{i}", s, [P, T]) for i, s in enumerate((57, 58, 99))]
            prt = [at(f"prob_t{i}", 100 + i, [P, T]) for i in range(3)]

            land_c = Landing(sem("second_landed"))
            land_rope = Landing(sem("rope_landed"))

            m = pool.do(lambda e: e.memset(rot[:, :], 0.0))
            pool.wait(m)
            view = rot[:, :].rearrange("p (b h c) -> p b h c", h=2, c=16)
            m = pool.do(lambda e: e.affine_select(out=view[:, :, 1, :], in_=view[:, :, 1, :],
                                                  compare_op=ALU.not_equal, fill=1.0, base=0,
                                                  pattern=[[32, 4], [1, 16]], channel_multiplier=-1))
            pool.wait(m)
            m_rot = pool.do(lambda e: e.affine_select(out=view[:, :, 0, :], in_=view[:, :, 0, :],
                                                      compare_op=ALU.not_equal, fill=-1.0, base=16,
                                                      pattern=[[32, 4], [1, 16]], channel_multiplier=-1))

            m_s = scale_columns(s_2, par2[:, 24:32], mod2[:, 8:16], m_mod["mod2", 0])
            m_sc = scale_columns(s_2c, par2[:, 24:32], mod2c[:, 8:16], m_mod["mod2", 1])
            m_r = mean_square(x, m_x, sq_ring, sq_free, T, 1.0 / D, rstd, m_x[-1])
            h = modulate(x, m_x, rstd, m_r, s_2, mod2[:, 0:8], m_s, mod_tmp, [None] * 4,
                         full(h_hi), full(h_lo), m_x)
            act.wait(*m_x)
            m_ctx = land_c.load(act, c_tok[:, :, :], A["ctx_2"][0].rearrange("(j p) n -> p j n", p=P))
            m_rope = land_rope.load(act, rope[:, :, :], A["rope"].rearrange("f p t -> p f t"))

            act.wait(h[-1][2])
            m_spill = land_spill.load(act, x_spill, x_all[:, :, :])

            rope_free = [None] * 3
            m_q, m_k = {}, {}

            def rope_evac(dst, got, scale, n, ps, done):
                r = n % 3
                t, ro = raw_t[r][:, :], rot_t[r][:, :]
                act.wait(done, rope_free[r], *m_x)
                m1 = act.do(lambda e: e.activation(t, ps[:, :], ACT.Copy, scale=scale))
                b, ps2 = take_bank()
                pe.wait(m1, m_rot)
                m2 = pe.do(lambda e: e.matmul(ps2[:, :], rot[:, :], t, start=True, stop=True))
                dve.wait(m2, m_rope, rope_free[r])
                m3 = dve.do(lambda e: e.tensor_tensor(ro, ps2[:, :], rope[:, 1, :], ALU.mult))
                bank_free[b] = [m3]
                pool.wait(m2, m_rope)
                m4 = pool.do(lambda e: e.tensor_tensor(t, t, rope[:, 0, :], ALU.mult))
                dve.wait(m4, m3)
                if dst is q2:
                    kept = dst[n][:, :].rearrange("p (i r a) -> p r i a", i=N_CH, r=ROWS)
                    t, ro = (v.rearrange("p (r i a) -> p r i a", i=N_CH, r=ROWS) for v in (t, ro))
                else:
                    kept = dst[n][:, :]
                got[n] = rope_free[r] = dve.do(lambda e: e.tensor_tensor(kept, t, ro, ALU.add))
                return [m1]

            m_kc = {}

            def kc_evac(n, ps, done):
                act.wait(done, hc[-1][2], *m_x)
                m_kc[n] = act.do(lambda e: e.activation(kc[:, 2 * n:2 * n + 2, :],
                                                        ps[:, :].rearrange("p (a t) -> p a t", a=2), ACT.Copy))
                return [m_kc[n]]

            q_evac = lambda n, ps, done: rope_evac(q2, m_q, float(A_DIM) ** -0.5, n, ps, done)
            gemm("q2", 0, DT, h, q_evac)
            m_c = transpose_in(lambda f, j: c_tok[:, j, f * P:(f + 1) * P], lambda f: c_f[f][:, :], DT, CTX // P,
                               [m_ctx, m_ident])
            m_r = mean_square([t[:, :] for t in c_f], m_c, csq, [None, None], CTX, 1.0 / D, c_rstd[:, :], None,
                              False)
            hc = modulate([t[:, :] for t in c_f], m_c, c_rstd[:, :], m_r, s_2c, mod2c[:, 0:8], m_sc, c_tmp,
                          [None] * 4, full(hc_hi), full(hc_lo), m_x)
            gemm("q2", 1, DT, h, q_evac)
            for g in range(2):
                gemm("k2", g, DT, h, lambda n, ps, done: rope_evac(k2, m_k, 1.0, n, ps, done), hc, kc_evac)

            vf_free, vcf_free = None, [None, None]
            m_v, m_vc = {}, {}

            def v_evac(n, ps, done):
                nonlocal vf_free
                act.wait(done, vf_free, *m_q.values())
                grid = ps[:, :].rearrange("p (r c) -> p r c", r=ROWS)
                for i in range(N_CH):
                    m1 = act.do(lambda e: e.activation(v_f[:, i, :, :], grid[:, :, K_START[i]:K_START[i] + K_COLS],
                                                       ACT.Copy))
                for half in range(2):
                    b, ps2 = take_bank()
                    pe.wait(m1)
                    for w in range(4):
                        i, rows_half = (4 * half + w) // 2, (4 * half + w) % 2
                        src = v_f[:, i, 4 * rows_half:4 * rows_half + 4, :].rearrange("p r c -> p (r c)")
                        m2 = pe.do(lambda e: e.transpose(ps2[:, w * P:(w + 1) * P], src, ident[:, :]))
                    dve.wait(m2, m_k[DT - 1])
                    m_v[n] = dve.do(lambda e: e.tensor_copy(vw[:, 4 * half:4 * half + 4, n * P:(n + 1) * P],
                                                            ps2[:, :].rearrange("p (w n) -> p w n", w=4)))
                    bank_free[b] = [m_v[n]]
                vf_free = m2
                return [m1]

            def vc_evac(n, ps, done):
                r = n % 2
                act.wait(done, vcf_free[r])
                m1 = act.do(lambda e: e.activation(vc_f[r][:, :], ps[:, :], ACT.Copy))
                b, ps2 = take_bank()
                pe.wait(m1)
                for j in range(2):
                    for u in range(2):
                        m2 = pe.do(lambda e: e.transpose(ps2[:, (2 * j + u) * P:(2 * j + u + 1) * P],
                                                         vc_f[r][:, u * CTX + j * P:u * CTX + (j + 1) * P], ident[:, :]))
                vcf_free[r] = m2
                dve.wait(m2, *m_x)
                m_vc[n] = dve.do(lambda e: e.tensor_copy(vc[:, :, 2 * n * P:2 * n * P + 2 * P],
                                                         ps2[:, :].rearrange("p (j n) -> p j n", j=2)))
                bank_free[b] = [m_vc[n]]
                return [m1]

            for g in range(2):
                gemm("v2", g, DT, h, v_evac, hc, vc_evac)

            after_v = [(pe.sem, pe.count), m_v[DT - 1], m_vc[3]]
            sp.wait(*after_v)
            land_mask = Landing(sem("mask_landed"))
            m_mask = land_mask.load(sp, mask[:, :, :], A["mask"].rearrange("v p k -> p v k"))
            land_t = [Landing(sem(f"toeplitz_landed{i}")) for i in range(2)]
            toep_free, bias_free = [None, None], [[], []]
            m_toep, m_bias = {}, {}

            def load_toeplitz(hd):
                r = hd % 2
                sp.wait(toep_free[r])
                t = A["rpb_padded"]
                for qr in range(ROWS):
                    src = bass.AP(t.tensor, (hd * (2 * ROWS - 1) + qr) * RPB_W, [[1, CH_COLS], [RPB_W, ROWS], [1, TOEP]])
                    m_toep[hd] = land_t[r].load(sp, toep[r][CH_COLS * qr:CH_COLS * (qr + 1), :, :], src)

            def make_bias(hd):
                r = hd % 2
                for v, off in enumerate((16, 8, 0)):
                    last = TOEP - 1 - off
                    src = toep[r][:, ::-1, last - K_COLS + 1:last + 1][:, :, ::-1]
                    pool.wait(m_toep[hd], m_mask, *bias_free[r], *after_v)
                    m_bias[hd] = pool.do(lambda e: e.tensor_tensor(
                        bias[r][:, v, :].rearrange("p (k b) -> p k b", k=ROWS), src,
                        mask[:, v, :].rearrange("p (k b) -> p k b", k=ROWS), ALU.add))
                toep_free[r] = m_bias[hd]
                bias_free[r] = []

            NB = ROWS * K_COLS
            work = [(hd, i) for hd in range(A_HEADS) for i in range(N_CH)]
            st = {}
            pr_free, prt_free = [None] * 3, [None] * 3
            small_free = [None] * 8
            o_bank, m_o = {}, {}

            def scores(n):
                hd, i = work[n]
                e2, pb, c3, c8 = hd // 2, A_DIM * (hd % 2), n % 3, n % 8
                part = slice(pb, pb + A_DIM)
                b, ps = take_bank()
                qv = q2[e2][part, i * P:(i + 1) * P]
                kv = k2[e2][part, :].rearrange("p (r c) -> p r c", r=ROWS)[:, :, K_START[i]:K_START[i] + K_COLS]
                pe.wait(m_q[e2], m_k[e2], m_kc[e2 // 2])
                pe.quiet(lambda e: e.matmul(ps[:, 0:NB], qv, kv, start=True, stop=True))
                ms = pe.do(lambda e: e.matmul(ps[:, NB:], qv, kc[part, e2, :], start=True, stop=True))
                top, neg = rowmax[:, c8:c8 + 1], rowsum[:, c8:c8 + 1]
                s1, s2 = rowsum[:, 8 + c8:9 + c8], rowsum[:, 16 + c8:17 + c8]
                v = (0, 1, 1, 2)[i]
                dve.wait(ms, small_free[c8])
                m1 = dve.do(lambda e: e.reduce_max(top, ps[:, NB:], AX.X))
                dve.wait(m1, m_bias[hd], pr_free[c3])
                m2 = dve.do(lambda e: e.tensor_tensor_reduce(pr[c3][:, 0:NB], ps[:, 0:NB], bias[hd % 2][:, v, :],
                                                             1.0, top, ALU.add, ALU.max, neg))
                bias_free[hd % 2].append(m2)
                dve.wait(m2)
                m3 = dve.do(lambda e: e.tensor_scalar(neg, neg, -1.0, None, ALU.mult))
                act.wait(m3)
                m4 = act.do(lambda e: e.activation(pr[c3][:, 0:NB], pr[c3][:, 0:NB], ACT.Exp, bias=neg, accum_out=s1))
                m5 = act.do(lambda e: e.activation(pr[c3][:, NB:], ps[:, NB:], ACT.Exp, bias=neg, accum_out=s2))
                bank_free[b] = [m5]
                st[n] = m5

            def normalise(n):
                c3, c8 = n % 3, n % 8
                s1, s2 = rowsum[:, 8 + c8:9 + c8], rowsum[:, 16 + c8:17 + c8]
                dve.wait(st[n])
                m = dve.do(lambda e: e.tensor_tensor(s1, s1, s2, ALU.add))
                dve.wait(m)
                m = dve.do(lambda e: e.reciprocal(s1, s1))
                dve.wait(m)
                st[n] = small_free[c8] = dve.do(lambda e: e.tensor_scalar(pr[c3][:, :], pr[c3][:, :], s1, None, ALU.mult))

            def turn(n):
                c3 = n % 3
                b, ps = take_bank()
                pe.wait(st[n])
                for k in range(4):
                    m = pe.do(lambda e: e.transpose(ps[:, k * P:(k + 1) * P], pr[c3][:, k * P:(k + 1) * P], ident[:, :]))
                pr_free[c3] = m
                act.wait(m, prt_free[c3])
                st[n] = act.do(lambda e: e.activation(prt[c3][:, :], ps[:, :], ACT.Copy))
                bank_free[b] = [st[n]]

            def values(n):
                hd, i = work[n]
                e2, pb, c3 = hd // 2, A_DIM * (hd % 2), n % 3
                part = slice(pb, pb + A_DIM)
                if i == 0:
                    o_bank[hd] = take_bank()
                b, ps = o_bank[hd]
                pe.wait(st[n])
                col = slice(A_DIM * hd, A_DIM * hd + A_DIM)
                for k in range(4):
                    vk = vw[:, 2 * i + k, col] if k < 2 else vc[:, k - 2, col]
                    m = pe.do(lambda e: e.matmul(ps[part, i * P:(i + 1) * P], vk, prt[c3][:, k * P:(k + 1) * P],
                                                 start=k == 0, stop=k == 3))
                prt_free[c3] = m
                if i == N_CH - 1:
                    dve.wait(m)
                    m_o[hd] = dve.do(lambda e: e.tensor_copy(
                        q2[e2][part, :].rearrange("p (r i a) -> p i r a", r=ROWS, i=N_CH),
                        ps[part, :].rearrange("p (i r a) -> p i r a", i=N_CH, r=ROWS)))
                    bank_free[b] = [m_o[hd]]

            m_sgb = {}

            def gb_evac(n, ps, done):
                act.wait(done, m_spill)
                m_sgb[n] = act.do(lambda e: e.activation(sgb[n][:, :], ps[:, :], ACT.Copy))
                return [m_sgb[n]]

            def g_b():
                for g in range(2):
                    yield from gemm_steps("g_b", g, DT, h, gb_evac)

            filler = g_b()
            load_toeplitz(0)
            load_toeplitz(1)
            make_bias(0)
            for _ in range(24):
                next(filler)
            for n in range(len(work) + 3):
                if n < len(work):
                    hd, i = work[n]
                    if i == 1 and hd + 1 < A_HEADS:
                        make_bias(hd + 1)
                        if hd + 2 < A_HEADS:
                            load_toeplitz(hd + 2)
                    scores(n)
                if 0 <= n - 1 < len(work):
                    normalise(n - 1)
                if 0 <= n - 2 < len(work):
                    turn(n - 2)
                if 0 <= n - 3 < len(work):
                    values(n - 3)
                next(filler, None)
            for _ in filler:
                pass

            m_att = [m_o[A_HEADS - 1], (pe.sem, pe.count)]
            zo = [(at(f"zo_hi{i}", 67 + i, [P, T], F32R), at(f"zo_lo{i}", 75 + i, [P, T], F32R)) for i in range(DT)]
            yb = [at(f"y_b{i}", 83 + i, [P, T]) for i in range(DT)]
            sg = [at(f"sig_g{i}", 51 + i, [P, T]) for i in range(4)]
            z_free, m_zo, m_yb = [None] * 4, {}, {}

            def zb_evac(n, ps, done):
                r = n % 4
                act.wait(done, z_free[r], *m_att)
                m = act.do(lambda e: e.activation(sg[r][:, :], ps[:, :], ACT.Silu))
                dve.wait(m, m_o[2 * n + 1])
                m1 = dve.do(lambda e: e.tensor_tensor(sg[r][:, :], sg[r][:, :], q2[n][:, :], ALU.mult))
                hi, lo = zo[n][0][:, :], zo[n][1][:, :]
                z_free[r] = split(sg[r][:, :], hi, lo, [m1], m_att)
                m_zo[n] = (hi, lo, z_free[r])
                return [m]

            for g in range(2):
                gemm("z_b", g, DT, h, zb_evac)

            def copy_evac(dst, got, n, ps, done):
                act.wait(done, *m_att)
                got[n] = act.do(lambda e: e.activation(dst[n][:, :], ps[:, :], ACT.Copy))
                return [got[n]]

            def yb_evac(n, ps, done):
                act.wait(m_sgb[n])
                m = act.do(lambda e: e.activation(sgb[n][:, :], sgb[n][:, :], ACT.Sigmoid))
                dve.wait(done, m, *m_att)
                m_yb[n] = dve.do(lambda e: e.tensor_tensor(yb[n][:, :], ps[:, :], sgb[n][:, :], ALU.mult))
                return [m_yb[n]]

            for g in range(2):
                gemm("w_out_attn", g, DT, m_zo, yb_evac)
            act.wait(m_yb[DT - 1], m_spill)
            m_back = land_back.load(act, x_all[:, :, :], x_spill)

            sz = [at(f"silu_za{i}", 91 + i, [P, T]) for i in range(4)]
            cg = [at(f"c_gate{i}", 95 + i, [P, T]) for i in range(4)]
            up = [at(f"u_pad{i}", 51, [P, T + 2], part=(T + 8) * i) for i in range(4)]
            ac = [at(f"conv3_{i}", 99 + i, [P, T]) for i in range(4)]
            cv = [(at(f"cv_hi{i}", 59 + i, [P, T], F32R), at(f"cv_lo{i}", 67 + i, [P, T], F32R)) for i in range(DT)]
            dve.wait(*z_free, *m_att)
            for i in range(4):
                dve.do(lambda e: e.memset(up[i][:, 0:1], 0.0))
                m_pad = dve.do(lambda e: e.memset(up[i][:, T + 1:T + 2], 0.0))
            sz_m, cg_m, m_cv, ac_free = {}, {}, {}, {}

            def za_evac(n, ps, done):
                act.wait(done, ac_free.get(n - 4), *m_att)
                sz_m[n] = act.do(lambda e: e.activation(sz[n % 4][:, :], ps[:, :], ACT.Silu))
                return [sz_m[n]]

            def bg_evac(n, ps, done):
                dve.wait(done, sz_m[n])
                sz_m[n] = dve.do(lambda e: e.tensor_tensor(sz[n % 4][:, :], sz[n % 4][:, :], ps[:, :], ALU.mult))
                return [sz_m[n]]

            def cg_evac(n, ps, done):
                act.wait(done, ac_free.get(n - 4))
                cg_m[n] = act.do(lambda e: e.activation(cg[n % 4][:, :], ps[:, :], ACT.Copy))
                return [cg_m[n]]

            def xi_evac(n, ps, done):
                r = n % 4
                dve.wait(done, cg_m[n], m_pad, ac_free.get(n - 4))
                m_u = m = dve.do(lambda e: e.tensor_tensor(up[r][:, 1:T + 1], ps[:, :], cg[r][:, :], ALU.mult))
                for k in range(3):
                    w = par2[:, 40 + 8 * k + n:41 + 8 * k + n]
                    dve.wait(m)
                    if k == 0:
                        m = dve.do(lambda e: e.tensor_scalar(ac[r][:, :], up[r][:, 0:T], w, par2[:, 64 + n:65 + n],
                                                             ALU.mult, ALU.add))
                    else:
                        m = dve.do(lambda e: e.scalar_tensor_tensor(ac[r][:, :], up[r][:, k:k + T], w, ac[r][:, :],
                                                                    ALU.mult, ALU.add))
                dve.wait(m, sz_m[n])
                m = dve.do(lambda e: e.tensor_tensor(ac[r][:, :], ac[r][:, :], sz[r][:, :], ALU.mult))
                hi, lo = cv[n][0][:, :], cv[n][1][:, :]

                def finish():
                    ac_free[n] = split(ac[r][:, :], hi, lo, [m], [m_yb[DT - 1]])
                    m_cv[n] = (hi, lo, ac_free[n])

                later.append(finish)
                return [m_u]

            for half in range(2):
                for key, evac in (("z_a", za_evac), ("b_gate", bg_evac), ("c_gate", cg_evac), ("x_in", xi_evac)):
                    gemm(f"{key}{half}", 0, DT, h, lambda n, ps, done: evac(4 * half + n, ps, done),
                         keep=int(key == "x_in"))

            sga = [at(f"sig_ga{i}", 75 + i, [P, T]) for i in range(DT)]
            m_ga, m_mg = {}, {}

            def ga_evac(n, ps, done):
                act.wait(done, m_yb[DT - 1])
                m_ga[n] = act.do(lambda e: e.activation(sga[n][:, :], ps[:, :], ACT.Sigmoid))
                return [m_ga[n]]

            for g in range(2):
                gemm("g_a", g, DT, h, ga_evac)
            h_read = (pe.sem, pe.count)

            def merge_evac(n, ps, done):
                dve.wait(done, m_ga[n])
                m = dve.do(lambda e: e.tensor_tensor(sga[n][:, :], ps[:, :], sga[n][:, :], ALU.mult))
                dve.wait(m, m_yb[n])
                m2 = dve.do(lambda e: e.tensor_tensor(yb[n][:, :], yb[n][:, :], sga[n][:, :], ALU.add))
                hi, lo = h_hi[n][:, :], h_lo[n][:, :]
                m_mg[n] = (hi, lo, split(yb[n][:, :], hi, lo, [m2], [h_read]))
                return [m]

            for g in range(2):
                gemm("w_out_conv", g, DT, m_cv, merge_evac)
            y2 = [at(f"y_second{i}", 51 + i, [P, T]) for i in range(DT)]
            m_y2 = {}
            m_sum = [None]

            def y2_evac(n, ps, done):
                copy_evac(y2, m_y2, n, ps, done)
                m_sum[0] = add_square(n, y2[n][:, :], m_y2[n], [h_read])
                return [m_y2[n]]

            for g in range(2):
                gemm("w_o", g, DT, m_mg, y2_evac)
            m_g = gate_columns(g_2o, par2[:, 32:40], mod2[:, 16:24], m_mod["mod2", 0])
            m_r = finish_square(m_sum[0], 1.0 / D)
            return residual(full(y2), m_y2, g_2o, m_g, rstd, m_r, x, [m_back] * DT)

        m_rstd = mean_square(x_ap, m_x, sq_ring, sq_free, T, 1.0 / D, rstd, None)
        prepare(8)
        prefetch()
        m_x = layer(0, m_x, m_rstd)
        m_x = layer(1, m_x)
        m_x = second(m_x)
        m_barrier = m_x

        y_tok = at("y_tok", 35, [P, N_CH, D])
        land_out = Landing(sem("out_landed"))
        for j in range(N_CH):
            for half in range(2):
                i, ps = take_bank()
                for f in range(4):
                    n = 4 * half + f
                    pe.wait(m_x[n])
                    m = pe.do(lambda e, n=n, j=j, f=f, ps=ps: e.transpose(ps[:, f * P:(f + 1) * P],
                                                                          x[n][:, j * P:(j + 1) * P], ident[:, :]))
                q = (dve, act)[half]
                q.wait(m, *m_barrier)
                dst = y_tok[:, j, 512 * half:512 * half + 512]
                if half:
                    m = act.do(lambda e, dst=dst, ps=ps: e.activation(dst, ps[:, :], ACT.Copy))
                else:
                    m = dve.do(lambda e, dst=dst, ps=ps: e.tensor_copy(dst, ps[:, :]))
                bank_free[i] = [m]
                sp.wait(m)
            m_out = land_out.load(sp, out[0, j * P:(j + 1) * P, :], y_tok[:, j, :])
        sp.wait(m_out)
        sp.wait((land_spill.sem, land_spill.count))


_INS = ["x", "w_ada", "w_in", "w_q", "w_k", "w_v", "w_gates", "w_out", "w_ff1", "w_ff2", "ctx_2", "w_mod_2",
        "w_in_2", "w_out_conv_2", "w_out_attn_2", "w_o_2"]


LAYER_ROWS = [("b_ada", 48), ("g_pre_mix", 8), ("g_post_mix", 8), ("g_pre_mlp", 8), ("g_post_mlp", 8), ("b_conv_m", 8),
              ("g_mh", 8), ("b_dw", 8), ("g_cn", 8), ("b_cn", 8), (None, 8), ("w_conv_m", 32), ("w_dw", 248)]
ROW, _row = {}, 0
for _name, _n in LAYER_ROWS:
    ROW[_name] = _row
    _row += _n


def param_rows(v):
    rows = np.zeros((9 * P, P), np.float32)
    for l in range(DEPTH):
        for name, n in LAYER_ROWS:
            if name:
                rows[4 * P * l + ROW[name]:4 * P * l + ROW[name] + n] = v[name][l].reshape(n, P)
    second = np.concatenate([v["b_mod_2"][0], v["pre_g_2"][0], v["post_g_2"][0], v["conv_w_2"][0].reshape(-1),
                             v["conv_b_2"][0], v["c"][0], v["c_2"][0], v["c_ctx_2"]]).reshape(-1, P)
    rows[8 * P:8 * P + len(second)] = second
    for l in range(DEPTH):
        rows[8 * P + len(second) + l, 0:2 * HEADS] = v["b_gates"][l]
    return rows


def shape_constants():
    tok = np.arange(T)
    half = A_DIM // 2
    inv = np.float32(10000.0) ** (-np.arange(0, half, 2, dtype=np.float32) / np.float32(half))
    ang_r = (tok // GRID).astype(np.float32)[:, None] * inv
    ang_c = (tok % GRID).astype(np.float32)[:, None] * inv
    ang = np.concatenate([ang_r, ang_r, ang_c, ang_c], axis=-1)
    rope = np.stack([np.tile(f(ang).astype(np.float32).T, (P // A_DIM, 1)) for f in (np.cos, np.sin)])
    mask = np.zeros((3, ROWS, CH_COLS, ROWS, K_COLS), np.float32)
    for v, i in enumerate((0, 1, 3)):
        qc = CH_COLS * i + np.arange(CH_COLS)
        kc = K_START[i] + np.arange(K_COLS)
        start = np.clip(qc - WIN // 2, 0, GRID - WIN)[:, None]
        seen = (kc >= start) & (kc < start + WIN)
        mask[v] = np.where(seen, 0.0, NEG)[None, :, None, :]
    return {"rope": rope, "mask": mask.reshape(3, P, ROWS * K_COLS)}


def kernel(**inputs):
    import concourse.bacc as bacc
    from concourse.bass_utils import run_bass_kernel_spmd

    nc = bacc.Bacc("TRN2", target_bir_lowering=False, num_devices=1)
    arrays = {name: np.ascontiguousarray(inputs[name]) for name in _INS}
    rpb = inputs["rpb_2"]
    padded = np.zeros((A_HEADS, 2 * ROWS - 1, RPB_W), rpb.dtype)
    padded[:, :, WIN:WIN + 2 * WIN - 1] = rpb[0][:, ::-1, ::-1]
    arrays["rpb_padded"] = padded
    arrays.update(shape_constants())
    arrays["param_rows"] = param_rows(inputs)
    A = {name: nc.dram_tensor(f"in_{name}", a.shape, mybir.dt.from_np(a.dtype), kind="ExternalInput").ap()
         for name, a in arrays.items()}
    out = nc.dram_tensor("x_out", (1, T, D), F32, kind="ExternalOutput").ap()
    build(nc, A, out)
    r = run_bass_kernel_spmd(nc, [{f"in_{name}": a for name, a in arrays.items()}], core_ids=[0])
    return r.results[0]["x_out"]
```
